# Optimizing a Trainium2 kernel written in Bass

```python
import math
import jax, jax.numpy as jnp
from jax import lax
import numpy as np

D_MODEL = 1024
BATCH = 1
SEQ = 1024
DEPTH = 2

SSD_HEADS = 8
SSD_HEAD_DIM = 64
SSD_GROUPS = 2
SSD_STATE = 128
SSD_CONV = 5
SSD_CHUNK = 128
SSD_INNER = SSD_HEADS * SSD_HEAD_DIM
SSD_XBC = SSD_INNER + 2 * SSD_GROUPS * SSD_STATE
GMLP_GROUPS = 4
GMLP_GROUP_DIM = 64
GMLP_WIDTH = GMLP_GROUPS * GMLP_GROUP_DIM
GMLP_CHUNK = 128
ATTN_HEADS = 4
ATTN_HEAD_DIM = 64
ATTN_WIDTH = ATTN_HEADS * ATTN_HEAD_DIM
ATTN_WINDOWS = (128, 512, 2048)
ATTN_DILATIONS = (1, 4, 16)
REL_BUCKETS = 32
REL_MAX_DISTANCE = 1024
MIX_WIDTH = SSD_INNER + GMLP_WIDTH + ATTN_WIDTH
IN_WIDTHS = (SSD_XBC, SSD_INNER, 2 * SSD_HEADS, GMLP_WIDTH, GMLP_WIDTH, ATTN_WIDTH, ATTN_WIDTH, ATTN_WIDTH)
IN_WIDTH = SSD_XBC + SSD_INNER + 2 * SSD_HEADS + 2 * GMLP_WIDTH + 3 * ATTN_WIDTH
FFN_DIM = 2816
FFN_CONV = 3
NORM_EPS = 1e-6
NEG_INF = -1e30

kernel_name = 'hybrid_ssd_gmlp_dilated_attn_encoder'

def rmsnorm(x, g):
    xf = x.astype(jnp.float32)
    y = xf * lax.rsqrt(jnp.mean(xf * xf, axis=-1, keepdims=True) + NORM_EPS)
    return (y * g.astype(jnp.float32)).astype(x.dtype)

def dwconv_centred(x, w, b):
    k, c = w.shape
    y = lax.conv_general_dilated(x, w[:, None, :].astype(x.dtype), window_strides=(1,),
                                 padding=[(k // 2, k // 2)],
                                 dimension_numbers=('NWC', 'WIO', 'NWC'),
                                 feature_group_count=c)
    return y + b

def ssd_chunked(x, dt, a_neg, bm, cm):
    b, s, g, hg, p = x.shape
    n = bm.shape[-1]
    q = SSD_CHUNK
    nc = s // q
    xdt = (x.astype(jnp.float32) * dt[..., None]).reshape(b, nc, q, g, hg, p)
    acs = jnp.cumsum((dt * a_neg).reshape(b, nc, q, g, hg), axis=2)
    bc = bm.astype(jnp.float32).reshape(b, nc, q, g, n)
    cc = cm.astype(jnp.float32).reshape(b, nc, q, g, n)
    tri = jnp.tril(jnp.ones((q, q), dtype=bool))
    seg = acs[:, :, :, None] - acs[:, :, None, :]
    decay_in = jnp.exp(jnp.where(tri[:, :, None, None], seg, NEG_INF))
    cb = jnp.einsum('bctgn,bcsgn->bctsg', cc, bc)
    y_diag = jnp.einsum('bctsg,bctsgh,bcsghp->bctghp', cb, decay_in, xdt)
    decay_out = jnp.exp(acs[:, :, -1:] - acs)
    states = jnp.einsum('bcsgn,bcsgh,bcsghp->bcghpn', bc, decay_out, xdt)
    chunk_decay = jnp.exp(acs[:, :, -1])

    def step(h, inp):
        st, dec = inp
        return h * dec[..., None, None] + st, h

    h0 = jnp.zeros((b, g, hg, p, n), jnp.float32)
    _, prev = lax.scan(step, h0, (jnp.moveaxis(states, 1, 0), jnp.moveaxis(chunk_decay, 1, 0)))
    prev = jnp.moveaxis(prev, 0, 1)
    y_off = jnp.einsum('bctgn,bcghpn,bctgh->bctghp', cc, prev, jnp.exp(acs))
    return (y_diag + y_off).reshape(b, s, g, hg, p)

def ssd_mixer(xbc, z, dt_raw, conv_w, conv_b, dt_bias, a_log, d_skip, out_gain):
    b, s, _ = xbc.shape
    hg = SSD_HEADS // SSD_GROUPS
    xbc_c = jax.nn.silu(dwconv_centred(xbc, conv_w, conv_b))
    xs, bm, cm = jnp.split(xbc_c, [SSD_INNER, SSD_INNER + SSD_GROUPS * SSD_STATE], axis=-1)
    xs = xs.reshape(b, s, SSD_GROUPS, hg, SSD_HEAD_DIM)
    bm = bm.reshape(b, s, SSD_GROUPS, SSD_STATE)
    cm = cm.reshape(b, s, SSD_GROUPS, SSD_STATE)
    dt = jax.nn.softplus(dt_raw.astype(jnp.float32).reshape(b, s, 2, SSD_HEADS)
                         + dt_bias.astype(jnp.float32)).reshape(b, s, 2, SSD_GROUPS, hg)
    a_neg = -jnp.exp(a_log.astype(jnp.float32)).reshape(2, SSD_GROUPS, hg)
    flip = lambda t: jnp.flip(t, axis=1)
    y_fwd = ssd_chunked(xs, dt[:, :, 0], a_neg[0], bm, cm)
    y_bwd = flip(ssd_chunked(flip(xs), flip(dt[:, :, 1]), a_neg[1], flip(bm), flip(cm)))
    y = y_fwd + y_bwd + d_skip.astype(jnp.float32).reshape(SSD_GROUPS, hg)[..., None] * xs
    y = y.reshape(b, s, SSD_INNER) * jax.nn.silu(z.astype(jnp.float32))
    y = rmsnorm(y.reshape(b, s, SSD_GROUPS, SSD_INNER // SSD_GROUPS),
                out_gain.reshape(SSD_GROUPS, SSD_INNER // SSD_GROUPS))
    return y.reshape(b, s, SSD_INNER).astype(xbc.dtype)

def gmlp_mixer(u, v, v_gain, w_s, b_s):
    b, s, _ = u.shape
    nc = s // GMLP_CHUNK
    u = jax.nn.gelu(u)
    v = rmsnorm(jax.nn.gelu(v), v_gain)
    vc = v.reshape(b, nc, GMLP_CHUNK, GMLP_GROUPS, GMLP_GROUP_DIM)
    mixed = jnp.einsum('gts,bcsge->bctge', w_s, vc) + jnp.swapaxes(b_s, 0, 1)[:, :, None]
    return u * mixed.reshape(b, s, GMLP_WIDTH)

def rel_bucket(rel):
    nb = REL_BUCKETS // 2
    max_exact = nb // 2
    n = jnp.abs(rel)
    large = max_exact + (jnp.log(jnp.maximum(n, 1).astype(jnp.float32) / max_exact)
                         / math.log(REL_MAX_DISTANCE / max_exact) * (nb - max_exact)).astype(jnp.int32)
    large = jnp.minimum(large, nb - 1)
    return jnp.where(rel > 0, nb, 0) + jnp.where(n < max_exact, n, large)

def dilated_branch(q, k, v, window, dil, rel_table):
    b, s, h, e = q.shape
    half = window // (2 * dil)
    length = s // dil
    nb = -(-length // half)
    lp = nb * half

    def residues(t):
        return t.reshape(b, length, dil, h, e).transpose(0, 2, 1, 3, 4)

    def key_blocks(t):
        tp = jnp.pad(residues(t), ((0, 0), (0, 0), (half, lp - length + half), (0, 0), (0, 0)))
        tp = tp.reshape(b, dil, nb + 2, half, h, e)
        return jnp.concatenate([tp[:, :, i:i + nb] for i in range(3)], axis=3)

    qb = jnp.pad(residues(q), ((0, 0), (0, 0), (0, lp - length), (0, 0), (0, 0))).reshape(b, dil, nb, half, h, e)
    kb = key_blocks(k)
    vb = key_blocks(v)
    rel = jnp.arange(3 * half)[None, :] - half - jnp.arange(half)[:, None]
    bias = jnp.transpose(rel_table[rel_bucket(rel * dil)], (2, 0, 1)).astype(jnp.float32)
    key_pos = jnp.arange(nb)[:, None] * half - half + jnp.arange(3 * half)[None, :]
    mask = (jnp.abs(rel) <= half)[None] & ((key_pos >= 0) & (key_pos < length))[:, None, :]
    logits = jnp.einsum('brcthe,brcshe->brchts', qb, kb).astype(jnp.float32) * (e ** -0.5) + bias
    logits = jnp.where(mask[:, None], logits, NEG_INF)
    lse = jax.nn.logsumexp(logits, axis=-1)
    probs = jnp.exp(logits - lse[..., None]).astype(v.dtype)
    out = jnp.einsum('brchts,brcshe->brcthe', probs, vb).reshape(b, dil, lp, h, e)[:, :, :length]
    out = out.transpose(0, 2, 1, 3, 4).reshape(b, s, h, e)
    lse = lse.transpose(0, 1, 2, 4, 3).reshape(b, dil, lp, h)[:, :, :length]
    lse = lse.transpose(0, 2, 1, 3).reshape(b, s, h)
    return out, lse

def attn_mixer(q, k, v, q_gain, k_gain, rel_table):
    b, s, _ = q.shape
    q = rmsnorm(q.reshape(b, s, ATTN_HEADS, ATTN_HEAD_DIM), q_gain)
    k = rmsnorm(k.reshape(b, s, ATTN_HEADS, ATTN_HEAD_DIM), k_gain)
    v = v.reshape(b, s, ATTN_HEADS, ATTN_HEAD_DIM)
    outs, lses = [], []
    for window, dil in zip(ATTN_WINDOWS, ATTN_DILATIONS):
        o, l = dilated_branch(q, k, v, window, dil, rel_table)
        outs.append(o)
        lses.append(l)
    weights = jax.nn.softmax(jnp.stack(lses), axis=0)
    out = jnp.sum(weights[..., None] * jnp.stack(outs).astype(jnp.float32), axis=0)
    return out.reshape(b, s, ATTN_WIDTH).astype(v.dtype)

def conv_ffn(x, w_up, conv_w, conv_b, w_down):
    hid = dwconv_centred(x @ w_up, conv_w, conv_b)
    gate, val = jnp.split(hid, 2, axis=-1)
    return (jax.nn.silu(gate) * val) @ w_down

def setup_inputs(seed: int = 0) -> dict:
    key = jax.random.key(seed)
    ks = jax.random.split(key, 24)
    nrm = lambda k, shape, scale: jax.random.normal(k, shape, jnp.float32) * scale
    dt0 = jnp.exp(jax.random.uniform(ks[5], (DEPTH, 2, SSD_HEADS), jnp.float32,
                                     math.log(1e-3), math.log(1e-1)))
    return {
        'x': nrm(ks[0], (BATCH, SEQ, D_MODEL), 1.0),
        'mix_norm_gain': 1.0 + nrm(ks[1], (DEPTH, D_MODEL), 0.02),
        'w_in': nrm(ks[2], (DEPTH, D_MODEL, IN_WIDTH), D_MODEL ** -0.5),
        'ssd_conv_w': nrm(ks[3], (DEPTH, SSD_CONV, SSD_XBC), SSD_CONV ** -0.5),
        'ssd_conv_b': nrm(ks[4], (DEPTH, SSD_XBC), 0.02),
        'ssd_dt_bias': dt0 + jnp.log(-jnp.expm1(-dt0)),
        'ssd_a_log': jnp.log(jax.random.uniform(ks[6], (DEPTH, 2, SSD_HEADS), jnp.float32, 1.0, 16.0)),
        'ssd_d': 1.0 + nrm(ks[7], (DEPTH, SSD_HEADS), 0.02),
        'ssd_out_gain': 1.0 + nrm(ks[8], (DEPTH, SSD_INNER), 0.02),
        'gmlp_v_gain': 1.0 + nrm(ks[9], (DEPTH, GMLP_WIDTH), 0.02),
        'gmlp_w_s': nrm(ks[10], (DEPTH, GMLP_GROUPS, GMLP_CHUNK, GMLP_CHUNK), GMLP_CHUNK ** -0.5),
        'gmlp_b_s': 1.0 + nrm(ks[11], (DEPTH, GMLP_GROUPS, GMLP_CHUNK), 0.02),
        'attn_q_gain': 1.0 + nrm(ks[12], (DEPTH, ATTN_HEAD_DIM), 0.02),
        'attn_k_gain': 1.0 + nrm(ks[13], (DEPTH, ATTN_HEAD_DIM), 0.02),
        'rel_bias_table': nrm(ks[14], (REL_BUCKETS, ATTN_HEADS), 0.2),
        'w_out': nrm(ks[15], (DEPTH, MIX_WIDTH, D_MODEL), MIX_WIDTH ** -0.5),
        'ffn_norm_gain': 1.0 + nrm(ks[16], (DEPTH, D_MODEL), 0.02),
        'ffn_w_up': nrm(ks[17], (DEPTH, D_MODEL, 2 * FFN_DIM), D_MODEL ** -0.5),
        'ffn_conv_w': nrm(ks[18], (DEPTH, FFN_CONV, 2 * FFN_DIM), FFN_CONV ** -0.5),
        'ffn_conv_b': nrm(ks[19], (DEPTH, 2 * FFN_DIM), 0.02),
        'ffn_w_down': nrm(ks[20], (DEPTH, FFN_DIM, D_MODEL), FFN_DIM ** -0.5),
    }

def reference(x, mix_norm_gain, w_in, ssd_conv_w, ssd_conv_b, ssd_dt_bias, ssd_a_log, ssd_d,
              ssd_out_gain, gmlp_v_gain, gmlp_w_s, gmlp_b_s, attn_q_gain, attn_k_gain,
              rel_bias_table, w_out, ffn_norm_gain, ffn_w_up, ffn_conv_w, ffn_conv_b, ffn_w_down):
    split_points = np.cumsum(IN_WIDTHS)[:-1].tolist()
    for l in range(DEPTH):
        h = rmsnorm(x, mix_norm_gain[l])
        proj = h @ w_in[l]
        xbc, z, dt_raw, gu, gv, q, k, v = jnp.split(proj, split_points, axis=-1)
        y_ssd = ssd_mixer(xbc, z, dt_raw, ssd_conv_w[l], ssd_conv_b[l], ssd_dt_bias[l],
                          ssd_a_log[l], ssd_d[l], ssd_out_gain[l])
        y_gmlp = gmlp_mixer(gu, gv, gmlp_v_gain[l], gmlp_w_s[l], gmlp_b_s[l])
        y_attn = attn_mixer(q, k, v, attn_q_gain[l], attn_k_gain[l], rel_bias_table)
        y = jnp.concatenate([y_ssd, y_gmlp.astype(x.dtype), y_attn], axis=-1)
        x = x + y @ w_out[l]
        x = x + conv_ffn(rmsnorm(x, ffn_norm_gain[l]), ffn_w_up[l], ffn_conv_w[l],
                         ffn_conv_b[l], ffn_w_down[l])
    return x


_drawn_inputs = setup_inputs


def setup_inputs(seed=0):
    import zlib

    import numpy as np

    out = dict(_drawn_inputs(seed))
    spreads = {}
    factors = {'ssd_d': 7.777,
     'ssd_out_gain': 3.649,
     'gmlp_v_gain': 7.428,
     'gmlp_b_s': 7.479,
     'attn_q_gain': 8.0,
     'attn_k_gain': 8.0,
     'rel_bias_table': 4.821,
     'ffn_norm_gain': 3.344,
     'ffn_conv_b': 3.377}
    for name, (base, spread) in spreads.items():
        noise = np.random.default_rng([zlib.crc32(name.encode()), seed]).standard_normal(out[name].shape)
        drawn = base * np.exp(spread * noise) if base else spread * noise
        out[name] = __import__('jax').numpy.asarray(drawn.astype(out[name].dtype))
    for name, factor in factors.items():
        out[name] = (out[name] * factor).astype(out[name].dtype)
    return out
```

```python
import concourse.bass as bass
from concourse import mybir
from contextlib import ExitStack
import numpy as np

F32 = mybir.dt.float32
F32R = mybir.dt.float32r
ALU = mybir.AluOpType
ACT = mybir.ActivationFunctionType
AX = mybir.AxisListType

P = 128
DEPTH, SEQ, DM = 2, 1024, 1024
KT = DM // P
NT = SEQ // P
HALF = 512
HEADS, HD, GROUPS, STATE = 8, 64, 2, 128
INNER = HEADS * HD
XBC_T = (INNER + 2 * GROUPS * STATE) // P
CONV = 5
GG, GW = 4, 256
AH_, AD, AW = 4, 64, 256
FFN = 2816
FT = FFN // P
UC = 256
NG = FFN // UC
XBC_U = XBC_T * P // UC
TOK_U = 7
IN_U = XBC_U + TOK_U
OUT_U = DM // UC
UNITS = IN_U + OUT_U + 3 * NG
SLOTS = 3
AHEAD = IN_U + SLOTS
EPS = 1e-6
NBUCK = 32
A_FILLS = 2 * XBC_T + TOK_U * NT + 8 * NG
B_FILLS = 4 * OUT_U + 16 * NG
A_UP = 2 * XBC_T + TOK_U * NT

_PARTS = [("mix_gain", KT), ("ffn_gain", KT), ("conv_w", XBC_T * CONV), ("conv_b", XBC_T),
          ("dt_bias", 16), ("a_log", 16), ("d_skip", HEADS), ("out_gain", INNER), ("v_gain", GW),
          ("b_s", GG), ("q_gain", 1), ("k_gain", 1), ("w_s", GG * P), ("w_dt", KT * 16),
          ("ffn_conv", 2 * FT * 4)]
PAR = {}
_at = 0
for _n, _w in _PARTS:
    PAR[_n] = (_at, _w)
    _at += _w
NPAR = _at


class Steps:

    def __init__(self, eng, sem, per_pass):
        self.eng, self.sem, self.per = eng, sem, per_pass

    def begin(self, n):
        self.base, self.k = n * self.per, 0

    def then(self, ins):
        ins.then_inc(self.sem, 1)
        self.k += 1
        self.eng.wait_ge(self.sem, self.base + self.k)

    def end(self):
        assert self.k == self.per, f"{self.sem}: {self.k} steps, not {self.per}"


def trunk(nc, xT, wst, params, consts, onehot, lnrow, table, outT):
    xspill = nc.dram_tensor("xspill", (P, KT, SEQ), F32, kind="Internal").ap()
    xbc_d = nc.dram_tensor("xbc_d", (NT, P, XBC_T, P), F32, kind="Internal").ap()
    tok_d = nc.dram_tensor("tok_d", (TOK_U, P, NT, UC), F32, kind="Internal").ap()
    row_d = nc.dram_tensor("row_d", (AH_, 2 * SEQ), F32, kind="Internal").ap()
    toe_d = nc.dram_tensor("toe_d", (AH_, P * (2 * SEQ + 1)), F32, kind="Internal").ap()
    toe_rows = toe_d.rearrange("h (p n) -> p h n", p=P)[:, :, 0:2 * SEQ]
    toe_cols = toe_d[:, 0:P * 2 * SEQ].rearrange("h (p n) -> p h n", p=P)

    with ExitStack() as ctx:
        top = [-(-nc.sbuf_base // 32) * 32]

        def place(name, shape, at=None, dt=F32):
            size = 4 * int(np.prod(shape[1:]))
            if at is None:
                at = top[0]
                top[0] += -(-size // 32) * 32
            return nc.alloc_sbuf_tensor_at(name, shape, dt, offset=at)

        RAW = place("RAW", [P, 2, 1024])
        WH = place("WH", [P, SLOTS, 2048], dt=F32R)
        WL = place("WL", [P, SLOTS, 2048], dt=F32R)
        PARM = place("PARM", [P, NPAR])
        CST = place("CST", [P, 4 * P])
        WDH = place("WDH", [P, KT * 16], dt=F32R)
        WDL = place("WDL", [P, KT * 16], dt=F32R)
        U = place("U", [P, NT, 16])
        SPL = place("SPL", [P, NT, 16])
        DT = place("DT", [P, NT, 16])
        DTA = place("DTA", [P, NT, 16])
        ACS = place("ACS", [P, NT, 16])
        DEC = place("DEC", [P, NT, 16])
        EACS = place("EACS", [P, NT, 16])
        CDEC = place("CDEC", [P, NT, 16])
        WST = place("WST", [P, NT, 16])
        EA = place("EA", [P, 16])
        MS = place("MS", [P, NT])
        RS = place("RS", [P, NT])
        VSS = place("VSS", [P, NT])
        VR = place("VR", [P, NT])
        YSS = place("YSS", [P, NT, 2])
        YR = place("YR", [P, NT, 2])
        QGN = place("QGN", [P, 1])
        ident, tri_f, tri_b, ones = (CST[:, i * P:(i + 1) * P] for i in range(4))

        def par_(name, a=0, b=None):
            at, w = PAR[name]
            return PARM[:, at + a:at + (w if b is None else b)]

        h_at = top[0]
        top[0] += 2 * KT * SEQ * 4
        HH = place("HH", [P, KT, SEQ], h_at, F32R)
        HL = place("HL", [P, KT, SEQ], h_at + KT * SEQ * 4, F32R)
        x_at = top[0]
        top[0] += KT * SEQ * 4
        X = place("X", [P, KT, SEQ], x_at)
        YT = place("YT", [P, NT, DM], x_at)
        u_at = top[0]
        SQ = place("SQ", [P, 2, SEQ], u_at)
        HF = place("HF", [P, 2, SEQ], u_at + 8192)
        PAD = place("PAD", [P, 2, SEQ + 4], u_at)
        CV = place("CV", [P, 2, SEQ], u_at + 8224)
        SC = place("SC", [P, 2, SEQ], u_at + 16416)
        JUNK8 = place("JUNK8", [P, NT, UC], u_at)
        ST = place("ST", [P, 2, NT, UC], u_at + 24608)
        u_end = u_at + 24608 + 16384
        AHI = place("AHI", [P, 2, SEQ], u_at, F32R)
        ALO = place("ALO", [P, 2, SEQ], u_at + 8192, F32R)
        FPAD = place("FPAD", [P, 2, SEQ + 2], u_at + 16384)
        CVG = place("CVG", [P, 2, SEQ], u_at + 24608)
        CVV = place("CVV", [P, 2, SEQ], u_at + 32800)
        YN = place("YN", [P, 2, DM], u_at)
        ZG = place("ZG", [P, 2, 4, UC], u_at + 8192)
        XBS = place("XBS", [P, 2, XBC_T, P], u_at + 16384)
        QS = place("QS", [P, 2, 2, P], u_at + 24576)
        AST = place("AST", [P, 16], u_at + 26624)
        MN = place("MN", [P, AH_], u_at + 26688)
        RSUM = place("RSUM", [P, AH_], u_at + 26720)
        RC = place("RC", [P, AH_], u_at + 26752)
        QSS = place("QSS", [P, 2, NT * AH_], u_at + 26784)
        m_at = [h_at]

        def work(name, shape):
            t = place(name, shape, m_at[0])
            m_at[0] += 4 * int(np.prod(shape[1:]))
            assert m_at[0] <= x_at
            return t

        BW = work("BW", [P, NT + 1, INNER])
        CURF = work("CURF", [P, INNER])
        XS = work("XS", [P, INNER])
        BST = work("BST", [P, GROUPS * STATE])
        XD = work("XD", [P, 2, INNER])
        XW = work("XW", [P, INNER])
        SEG = work("SEG", [P, 4, 4, P])
        CBM = work("CBM", [P, 2, GROUPS, P])
        Y1 = work("Y1", [P, INNER])
        Y2 = work("Y2", [P, INNER])
        VN = work("VN", [P, GW])
        GT = work("GT", [P, GW])
        JUNK = work("JUNK", [P, GROUPS, 256])
        m_at[0] = h_at
        KTT = work("KTT", [P, 2, SEQ])
        QTT = work("QTT", [P, 2, SEQ])
        V = work("V", [P, NT, AW])
        TOE = work("TOE", [P, 2, 2, SEQ])
        lg_at = m_at[0]
        LG = work("LG", [P, 2, SEQ])
        PR = work("PR", [P, 2, SEQ])
        PT = work("PT", [P, 2, NT, P])
        QK = place("QK", [P, 2, NT, AW], lg_at)
        QSQ = place("QSQ", [P, NT, AW], lg_at + 16384)
        OH = place("OH", [NBUCK, 2 * SEQ], u_at)
        LNR = place("LNR", [AH_, 2 * SEQ], u_at + 8192)
        ROW = place("ROW", [AH_, 2 * SEQ], u_at + 16384)
        TAB = place("TAB", [NBUCK, AH_], u_at + 24576)
        assert u_end <= nc.sbuf_top, (u_end, nc.sbuf_top)

        PS = ctx.enter_context(nc.psum_tensor("PS", [P, 8, HALF], F32))

        def sem(name):
            return ctx.enter_context(nc.semaphore(name))

        raw_full = [sem("raw_full0"), sem("raw_full1")]
        hi_done, w_ready, w_used = sem("hi_done"), sem("w_ready"), sem("w_used")
        cst_in, x_in, par_in, oh_in = sem("cst_in"), sem("x_in"), sem("par_in"), sem("oh_in")
        row_ps, row_sb, row_out, toe_out = sem("row_ps"), sem("row_sb"), sem("row_out"), sem("toe_out")
        a_full, a_free, b_full, b_free = sem("a_full"), sem("a_free"), sem("b_full"), sem("b_free")
        sq_ready, sq_used, ss_ready = sem("sq_ready"), sem("sq_used"), sem("ss_ready")
        inv_ready, rs_ready, nb_ready = sem("inv_ready"), sem("rs_ready"), sem("nb_ready")
        hf_ready, hh_ready, h_ready = sem("hf_ready"), sem("hh_ready"), sem("h_ready")
        norm_step, settled = sem("norm_step"), sem("settled")
        x_spilled, x_back, y_out = sem("x_spilled"), sem("x_back"), sem("y_out")
        wdt_ready, pad_zero = sem("wdt_ready"), sem("pad_zero")
        tap_done, conv_done, silu_done = sem("tap_done"), sem("conv_done"), sem("silu_done")
        conv_step = sem("conv_step")
        xbc_out = [sem("xbc_out0"), sem("xbc_out1")]
        tok_out = [sem("tok_out0"), sem("tok_out1")]
        gv_done, vinv_ready, vr_ready, v_step = sem("gv_done"), sem("vinv_ready"), sem("vr_ready"), sem("v_step")
        dt_full, u_ready, sp_ready, dta_ready = sem("dt_full"), sem("u_ready"), sem("sp_ready"), sem("dta_ready")
        acs_full, acs_ready, dec_ready, wst_ready = sem("acs_full"), sem("acs_ready"), sem("dec_ready"), sem("wst_ready")
        sp_step, dt_step = sem("sp_step"), sem("dt_step")
        xbs_full = [sem("xbs_full0"), sem("xbs_full1")]
        zg_full = [sem("zg_full0"), sem("zg_full1")]
        xbs_used, zg_used = sem("xbs_used"), sem("zg_used")
        ra_t_full, ra_bst, ra_xw, ra_s_full, ra_done, ra_step = (
            sem("ra_t_full"), sem("ra_bst"), sem("ra_xw"), sem("ra_s_full"), sem("ra_done"), sem("ra_step"))
        ast_ready, t_full, bst_ready, xs_ready = sem("ast_ready"), sem("t_full"), sem("bst_ready"), sem("xs_ready")
        cb_full, cbm_ready, ab_full, seg_ready = sem("cb_full"), sem("cbm_ready"), sem("ab_full"), sem("seg_ready")
        exp_ready, w_masked, yo_full, sf_full = sem("exp_ready"), sem("w_masked"), sem("yo_full"), sem("sf_full")
        xd_ready, yd_full, yz_ready, yss_ready = sem("xd_ready"), sem("yd_full"), sem("yz_ready"), sem("yss_ready")
        vn_ready, mx_full, chunk_done, chunk_step = sem("vn_ready"), sem("mx_full"), sem("chunk_done"), sem("chunk_step")
        yinv_ready, yr_ready, yr_step = sem("yinv_ready"), sem("yr_ready"), sem("yr_step")
        qk_in, v_in, qsq_ready, qinv_ready = sem("qk_in"), sem("v_in"), sem("qsq_ready"), sem("qinv_ready")
        qr_ready, qn_ready, qt_full, qt_ready, q_step = (
            sem("qr_ready"), sem("qn_ready"), sem("qt_full"), sem("qt_ready"), sem("q_step"))
        toe_full = [sem("toe_full0"), sem("toe_full1")]
        toe_used = sem("toe_used")
        qs_ready, s_full, lg_ready, pr_ready = sem("qs_ready"), sem("s_full"), sem("lg_ready"), sem("pr_ready")
        pt_full, pta_ready, ptd_ready, av_done = sem("pt_full"), sem("pta_ready"), sem("ptd_ready"), sem("av_done")
        att_done, att_step = sem("att_done"), sem("att_step")
        yn_ready, yc_ready, yt_full, yh_ready, yl_ready = (
            sem("yn_ready"), sem("yc_ready"), sem("yt_full"), sem("yh_ready"), sem("yl_ready"))
        f_tap, f_conv, f_silu, f_hi, act_ready, f_step, down_done = (
            sem("f_tap"), sem("f_conv"), sem("f_silu"), sem("f_hi"), sem("act_ready"), sem("f_step"), sem("down_done"))

        block = ctx.enter_context(nc.Block())

        def settle(eng):
            eng.sem_inc(settled, 1)

        def bank(b, n=1):
            return PS[:, b, :] if n == 1 else PS[:, b:b + n, :].rearrange("p a b -> p (a b)")

        def per_head(t, w=HD):
            return t.unsqueeze(2).to_broadcast((P, t.shape[1], w))

        @block.sync
        def _(sp):
            def weights(l, first, last):
                settle(sp)
                with sp.Fori(first, last) as u:
                    for hf in range(2):
                        sp.wait_ge(w_ready, (l * UNITS + u) * 2 + hf + 1)
                        sp.dma_start(RAW[:, hf, :], wst[l * UNITS + u, hf]).then_inc(raw_full[hf], 16)

            sp.dma_start(CST[:], consts[:, :]).then_inc(cst_in, 16)
            sp.dma_start(X[:], xT[:, :, :]).then_inc(x_in, 16)
            with sp.Fori(0, DEPTH) as l:
                weights(l, 0, AHEAD)
                for par in range(2):
                    sp.wait_ge(xbc_out[par], (l + 1) * 16 * (XBC_T // 2))
                settle(sp)
                with sp.Fori(0, NT // 2) as i2:
                    for par in range(2):
                        sp.wait_ge(xbs_used, l * 2 * NT + i2 * 2 + par + 1)
                        sp.dma_start(XBS[:, par], xbc_d[i2 * -2 + (NT - 1 - par)]).then_inc(xbs_full[par], 16)
                sp.wait_ge(tok_out[0], (l + 1) * 16 * 4)
                settle(sp)
                sp.wait_ge(tok_out[1], (l + 1) * 16 * 3)
                settle(sp)
                with sp.Fori(0, NT // 2) as i2:
                    for par in range(2):
                        sp.wait_ge(xbs_used, l * 2 * NT + NT + i2 * 2 + par + 1)
                        sp.dma_start(XBS[:, par], xbc_d[2 * i2 + par]).then_inc(xbs_full[par], 16)
                        sp.wait_ge(zg_used, l * NT + i2 * 2 + par + 1)
                        sp.dma_start(ZG[:, par], tok_d[0:4, :, 2 * i2 + par, :].rearrange("u p n -> p u n")
                                     ).then_inc(zg_full[par], 16)
                sp.wait_ge(chunk_done, 1 + (l + 1) * NT)
                sp.wait_ge(yss_ready, 1 + (l + 1) * NT)
                sp.dma_start(QK[:], tok_d[4:6].rearrange("u p t n -> p u t n")).then_inc(qk_in, 16)
                sp.dma_start(V[:], tok_d[6]).then_inc(v_in, 16)
                sp.wait_ge(toe_out, 16 * AH_)
                settle(sp)
                with sp.Fori(0, NT) as i:
                    for hp in range(2):
                        sp.wait_ge(toe_used, (l * NT + i) * 2 + hp + 1)
                        settle(sp)
                        sp.dma_start(TOE[:, hp], toe_cols[:, 2 * hp:2 * hp + 2, bass.ds(SEQ - P * i, SEQ)]
                                     ).then_inc(toe_full[hp], 16)
                sp.wait_ge(yn_ready, (l + 1) * NT)
                sp.wait_ge(yc_ready, (l + 1) * NT)
                sp.dma_start(X[:], xspill[:, :, :]).then_inc(x_back, 16)
                weights(l, AHEAD, UNITS)
            sp.wait_ge(b_free, 4 + DEPTH * B_FILLS)
            sp.dma_start(outT[:, :, :], X[:]).then_inc(y_out, 16)
            sp.wait_ge(y_out, 16)

        @block.gpsimd
        def _(pool):
            pool.sem_inc(w_ready, 2)
            with pool.Fori(0, DEPTH * UNITS // SLOTS) as r:
                for s in range(SLOTS):
                    for hf in range(2):
                        n = (r * SLOTS + s) * 2 + hf
                        pool.wait_ge(raw_full[hf], 16 * (r * SLOTS + s + 1))
                        if hf == 0:
                            pool.wait_ge(w_used, r * SLOTS + s + 1)
                        hi = WH[:, s, hf * 1024:(hf + 1) * 1024]
                        settle(pool)
                        nc.gpsimd.tensor_copy(hi, RAW[:, hf, :]).then_inc(hi_done, 1)
                        pool.wait_ge(hi_done, n + 1)
                        nc.gpsimd.tensor_tensor(WL[:, s, hf * 1024:(hf + 1) * 1024], RAW[:, hf, :],
                                                hi.bitcast(F32), ALU.subtract).then_inc(w_ready, 1)

        @block.tensor
        def _(pe):
            def mm3(out, ws, xs, first, last, skip=False):
                (wh, wl), (xh, xl) = ws, xs
                kw = dict(skip_group_check=True) if skip else {}
                nc.tensor.matmul(out, wh, xh, start=first, stop=False, **kw)
                nc.tensor.matmul(out, wh, xl, start=False, stop=False, **kw)
                return nc.tensor.matmul(out, wl, xh, start=False, stop=last, **kw)

            def wtile(s, a):
                return WH[:, s, a:a + P], WL[:, s, a:a + P]

            def unit_ready(l, u):
                pe.wait_ge(w_ready, 2 + (l * UNITS + u) * 2 + 2)

            def norm_sums(n):
                for k in range(KT):
                    pe.wait_ge(sq_ready, n * KT + k + 1)
                    for t in range(NT):
                        last = nc.tensor.matmul(PS[:, 4, t:t + 1], SQ[:, k % 2, t * P:(t + 1) * P], ones[:, 0:1],
                                                start=(k == 0 and t == 0), stop=(k == KT - 1),
                                                skip_group_check=True)
                    last.then_inc(sq_used, 1)
                pe.wait_ge(rs_ready, n + 1)
                for t in range(NT):
                    last = nc.tensor.matmul(PS[:, 6 + t // 4, (t % 4) * P:(t % 4 + 1) * P],
                                            RS[:, t:t + 1].to_broadcast((P, P)), ident, start=True, stop=True)
                last.then_inc(nb_ready, 1)

            def columns_unit(l, u, s, n0, banks, full, free, h_waits=None):
                unit_ready(l, u)
                for f in range(4):
                    ct, th = divmod(f, 2)
                    b = banks + f
                    pe.wait_ge(free, n0 + f + 1)
                    for k in range(KT):
                        if h_waits is not None and f == 0:
                            pe.wait_ge(h_ready, h_waits + k + 1)
                        tok = slice(th * HALF, (th + 1) * HALF)
                        last = mm3(bank(b), wtile(s, k * UC + ct * P), (HH[:, k, tok], HL[:, k, tok]),
                                   k == 0, k == KT - 1)
                    last.then_inc(full, 1)

            pe.wait_ge(cst_in, 16)
            pe.sem_inc(w_used, SLOTS)
            for s in (chunk_done, yss_ready, ra_done, pta_ready, ptd_ready, att_done, yl_ready, yh_ready,
                      yt_full, act_ready, down_done, f_conv):
                pe.sem_inc(s, 1)
            pe.wait_ge(oh_in, 48)
            for q in range(4):
                last = nc.tensor.matmul(PS[0:AH_, q, :], TAB[:, :], OH[:, q * HALF:(q + 1) * HALF],
                                        start=True, stop=True)
            last.then_inc(row_ps, 1)
            pe.wait_ge(row_sb, 1)
            with pe.Fori(0, DEPTH) as l:
                a0, b0 = l * A_FILLS, l * B_FILLS
                norm_sums(2 * l)
                for u in range(XBC_U):
                    columns_unit(l, u, u % SLOTS, a0 + 4 * u, 0, a_full, a_free,
                                 2 * l * KT if u == 0 else None)
                    pe.wait_ge(a_full, a0 + 4 * u + 4)
                    pe.sem_inc(w_used, 1)
                settle(pe)
                with pe.Fori(0, TOK_U) as i:
                    unit_ready(l, XBC_U + i)
                    s = (i + XBC_U % SLOTS) % SLOTS
                    wh, wl = WH[:, bass.ds(s, 1), :], WL[:, bass.ds(s, 1), :]
                    for t in range(NT):
                        pe.wait_ge(a_free, a0 + 2 * XBC_T + i * NT + t + 1)
                        for k in range(KT):
                            tok = slice(t * P, (t + 1) * P)
                            cols = slice(k * UC, (k + 1) * UC)
                            xh, xl = HH[:, k, tok], HL[:, k, tok]
                            o = PS[:, t % 4, 0:UC]
                            nc.tensor.matmul(o, xh, wh[:, :, cols], start=(k == 0), stop=False)
                            nc.tensor.matmul(o, xh, wl[:, :, cols], start=False, stop=False)
                            last = nc.tensor.matmul(o, xl, wh[:, :, cols], start=False, stop=(k == KT - 1))
                        last.then_inc(a_full, 1)
                    pe.wait_ge(a_full, a0 + 2 * XBC_T + i * NT + NT)
                    pe.sem_inc(w_used, 1)
                pe.wait_ge(wdt_ready, l + 1)
                for t in range(NT):
                    for k in range(KT):
                        tok, cols = slice(t * P, (t + 1) * P), slice(k * 16, (k + 1) * 16)
                        last = mm3(PS[:, 4, t * 16:(t + 1) * 16], (HH[:, k, tok], HL[:, k, tok]),
                                   (WDH[:, cols], WDL[:, cols]), k == 0 and t == 0, k == KT - 1, skip=True)
                last.then_inc(dt_full, 1)
                pe.wait_ge(dta_ready, l + 1)
                for d, tri in enumerate((tri_f, tri_b)):
                    nc.tensor.matmul(PS[:, 5, d * 64:(d + 1) * 64], tri, DTA[:, :, d * 8:(d + 1) * 8],
                                     start=(d == 0), stop=True, skip_group_check=True)
                nc.tensor.matmul(PS[:, 5, 128:256], ones, DTA[:], start=False, stop=True,
                                 skip_group_check=True).then_inc(acs_full, 1)
                pe.wait_ge(a_free, 4 + a0 + A_UP)
                settle(pe)
                with pe.Fori(0, NT // 2) as i2:
                    for par in range(2):
                        n = l * NT + i2 * 2 + par
                        pe.wait_ge(xbs_full[par], 16 * (l * NT + i2 + 1))
                        pe.wait_ge(ra_done, 1 + n)
                        for j in range(6):
                            last = nc.tensor.transpose(PS[:, j // 4, (j % 4) * P:(j % 4 + 1) * P],
                                                       XBS[:, par, j, :], ident)
                        last.then_inc(ra_t_full, 1)
                        pe.wait_ge(ra_t_full, n + 1)
                        pe.sem_inc(xbs_used, 1)
                        pe.wait_ge(ra_bst, n + 1)
                        pe.wait_ge(ra_xw, n + 1)
                        for g in range(GROUPS):
                            last = nc.tensor.matmul(PS[:, 2, g * 256:(g + 1) * 256], BST[:, g * P:(g + 1) * P],
                                                    XW[:, g * 256:(g + 1) * 256], start=True, stop=True)
                        last.then_inc(ra_s_full, 1)
                pe.wait_ge(ra_done, 1 + (l + 1) * NT)
                settle(pe)
                with pe.Fori(0, NT // 2) as i2:
                    for par in range(2):
                        c = i2 * 2 + par
                        n = l * NT + c
                        pe.wait_ge(xbs_full[par], 16 * (l * NT + NT // 2 + i2 + 1))
                        pe.wait_ge(chunk_done, 1 + n)
                        pe.wait_ge(yss_ready, 1 + n)
                        for j in range(6):
                            last = nc.tensor.transpose(PS[:, j // 4, (j % 4) * P:(j % 4 + 1) * P],
                                                       XBS[:, par, j, :], ident)
                        last.then_inc(t_full, 1)
                        for g in range(GROUPS):
                            last = nc.tensor.matmul(PS[:, 2, g * P:(g + 1) * P], XBS[:, par, 4 + g, :],
                                                    XBS[:, par, 6 + g, :], start=True, stop=True)
                        last.then_inc(cb_full, 1)
                        pe.wait_ge(ast_ready, n + 1)
                        for j in range(4):
                            d, g = divmod(j, 2)
                            if j >= 2:
                                pe.wait_ge(seg_ready, n * 4 + j - 1)
                            for h in range(4):
                                e = d * 8 + g * 4 + h
                                last = nc.tensor.matmul(PS[:, 3 + j % 2, h * P:(h + 1) * P],
                                                        AST[:, e:e + 1].to_broadcast((P, P)),
                                                        tri_f if d == 0 else tri_b, start=True, stop=True)
                            last.then_inc(ab_full, 1)
                        for d in range(2):
                            for g in range(GROUPS):
                                cols = slice(g * 256, (g + 1) * 256)
                                st = CURF[:, cols] if d == 0 else BW[:, bass.ds(c + 1, 1), cols]
                                last = nc.tensor.matmul(PS[:, 6 + d, cols], XBS[:, par, 6 + g, :], st,
                                                        start=True, stop=True)
                        last.then_inc(yo_full, 1)
                        pe.wait_ge(yo_full, n + 1)
                        pe.sem_inc(xbs_used, 1)
                        pe.wait_ge(bst_ready, n + 1)
                        pe.wait_ge(xd_ready, n + 1)
                        for g in range(GROUPS):
                            last = nc.tensor.matmul(PS[:, 1, g * 256:(g + 1) * 256], BST[:, g * P:(g + 1) * P],
                                                    XW[:, g * 256:(g + 1) * 256], start=True, stop=True)
                        last.then_inc(sf_full, 1)
                        pe.wait_ge(vn_ready, n + 1)
                        pe.wait_ge(cbm_ready, n + 1)
                        for g in range(GG):
                            last = nc.tensor.matmul(PS[:, 2, g * HD:(g + 1) * HD], par_("w_s", g * P, (g + 1) * P),
                                                    VN[:, g * HD:(g + 1) * HD], start=True, stop=True)
                        last.then_inc(mx_full, 1)
                        pe.wait_ge(w_masked, n * 4 + 4)
                        for g in range(GROUPS):
                            for h in range(4):
                                e = g * 4 + h
                                for d in range(2):
                                    last = nc.tensor.matmul(PS[:, 5, e * HD:(e + 1) * HD],
                                                            SEG[:, d * 2 + g, h, :], XD[:, d, e * HD:(e + 1) * HD],
                                                            start=(d == 0), stop=(d == 1))
                        last.then_inc(yd_full, 1)
                pe.wait_ge(chunk_done, 1 + (l + 1) * NT)
                pe.wait_ge(yss_ready, 1 + (l + 1) * NT)
                for m in range(2):
                    pe.wait_ge(qn_ready, l * 2 + m + 1)
                    for hp in range(2):
                        f = (l * 2 + m) * 2 + hp
                        if m * 2 + hp >= 2:
                            pe.wait_ge(qt_ready, f - 1)
                        for t in range(NT):
                            last = nc.tensor.transpose(
                                PS[:, 2 * hp + t // 4, (t % 4) * P:(t % 4 + 1) * P],
                                QK[:, m, t, hp * P:(hp + 1) * P], ident)
                        last.then_inc(qt_full, 1)
                pe.wait_ge(qt_ready, (l + 1) * 4)
                pe.wait_ge(v_in, 16 * (l + 1))
                settle(pe)
                with pe.Fori(0, NT // 2) as i2:
                    for par in range(2):
                        i = l * NT + i2 * 2 + par

                        def scores(h):
                            if h >= 2:
                                pe.wait_ge(lg_ready, i * 4 + h - 1)
                            rows = slice(64 * (h % 2), 64 * (h % 2) + 64)
                            for th in range(2):
                                last = nc.tensor.matmul(bank(2 * (h % 2) + th), QS[rows, par, h // 2, :],
                                                        KTT[rows, h // 2, th * HALF:(th + 1) * HALF],
                                                        start=True, stop=True)
                            last.then_inc(s_full, 1)

                        def turn(h):
                            pe.wait_ge(pr_ready, i * 4 + h + 1)
                            pe.wait_ge(pta_ready, 1 + i * 4 + h)
                            pe.wait_ge(ptd_ready, 1 + i * 4 + h)
                            for t in range(NT):
                                last = nc.tensor.transpose(PS[:, 4 + t // 4, (t % 4) * P:(t % 4 + 1) * P],
                                                           PR[:, h % 2, t * P:(t + 1) * P], ident)
                            last.then_inc(pt_full, 1)

                        def values(h):
                            pe.wait_ge(pta_ready, 1 + i * 4 + h + 1)
                            pe.wait_ge(ptd_ready, 1 + i * 4 + h + 1)
                            for t in range(NT):
                                last = nc.tensor.matmul(PS[:, 6, h * AD:(h + 1) * AD], PT[:, h % 2, t, :],
                                                        V[:, t, h * AD:(h + 1) * AD],
                                                        start=(t == 0), stop=(t == NT - 1))
                            last.then_inc(av_done, 1)

                        pe.wait_ge(qs_ready, i + 1)
                        scores(0)
                        scores(1)
                        turn(0)
                        scores(2)
                        pe.wait_ge(att_done, 1 + i)
                        values(0)
                        turn(1)
                        scores(3)
                        values(1)
                        turn(2)
                        values(2)
                        turn(3)
                        values(3)
                pe.wait_ge(att_done, 1 + (l + 1) * NT)
                settle(pe)
                with pe.Fori(0, NT // 2) as i2:
                    for par in range(2):
                        n = l * NT + i2 * 2 + par
                        pe.wait_ge(yn_ready, n + 1)
                        pe.wait_ge(yc_ready, n + 1)
                        pe.wait_ge(yl_ready, 1 + n)
                        for k in range(KT):
                            last = nc.tensor.transpose(PS[:, 2 * par + k // 4, (k % 4) * P:(k % 4 + 1) * P],
                                                       YN[:, par, k * P:(k + 1) * P], ident)
                        last.then_inc(yt_full, 1)
                pe.wait_ge(yl_ready, 1 + (l + 1) * NT)
                for u in range(OUT_U):
                    columns_unit(l, IN_U + u, (IN_U + u) % SLOTS, b0 + 4 * u, 4, b_full, b_free)
                    pe.wait_ge(b_full, b0 + 4 * u + 4)
                    pe.sem_inc(w_used, 1)
                norm_sums(2 * l + 1)
                s0 = (IN_U + OUT_U) % SLOTS

                def up(g, unit, s, part, h_waits=None):
                    n0 = a0 + A_UP + g * 8 + part * 4
                    columns_unit(l, unit, s, n0, 0, a_full, a_free, h_waits)
                    pe.wait_ge(a_full, n0 + 4)
                    pe.sem_inc(w_used, 1)

                def down(g, unit, s):
                    unit_ready(l, unit)
                    pe.wait_ge(act_ready, 1 + (l * NG + g) * 2 + 2)
                    n0 = b0 + 4 * OUT_U + g * 16
                    for f in range(16):
                        dt, th = divmod(f, 2)
                        tok = slice(th * HALF, (th + 1) * HALF)
                        pe.wait_ge(b_free, n0 + f + 1)
                        for k in range(2):
                            last = mm3(bank(4 + f % 4), wtile(s, k * 1024 + dt * P),
                                       (AHI[:, k, tok], ALO[:, k, tok]), k == 0, k == 1)
                        last.then_inc(b_full, 1)
                    pe.wait_ge(b_full, n0 + 16)
                    pe.sem_inc(w_used, 1)
                    pe.sem_inc(down_done, 1)

                f0 = IN_U + OUT_U
                up(0, f0, s0, 0, (2 * l + 1) * KT)
                up(0, f0 + 1, (s0 + 1) % SLOTS, 1)
                settle(pe)
                with pe.Fori(1, NG) as g:
                    up(g, f0 + g * 3 - 1, (s0 + 2) % SLOTS, 0)
                    down(g - 1, f0 + g * 3, s0)
                    up(g, f0 + g * 3 + 1, (s0 + 1) % SLOTS, 1)
                down(NG - 1, f0 + NG * 3 - 1, (s0 + 2) % SLOTS)

        @block.scalar
        def _(act):
            A = nc.scalar.activation

            def norm(n, x_value):
                act.wait_ge(b_free, x_value)
                for k in range(KT):
                    if k >= 2:
                        act.wait_ge(sq_used, n * KT + k - 1)
                    A(SQ[:, k % 2, :], X[:, k, :], ACT.Square).then_inc(sq_ready, 1)
                act.wait_ge(inv_ready, n + 1)
                A(RS[:], MS[:], ACT.Sqrt).then_inc(rs_ready, 1)
                for k in range(KT):
                    act.wait_ge(hf_ready, n * KT + k + 1)
                    A(HH[:, k, :], HF[:, k % 2, :], ACT.Copy).then_inc(hh_ready, 1)

            act.dma_start(OH[:], onehot[:, :]).then_inc(oh_in, 16)
            act.dma_start(TAB[:], table[:, :]).then_inc(oh_in, 16)
            act.dma_start(LNR[:], lnrow[:, :]).then_inc(oh_in, 16)
            act.sem_inc(a_free, 4)
            act.wait_ge(row_sb, 1)
            act.dma_start(row_d[:, :], ROW[:]).then_inc(row_out, 16)
            act.wait_ge(row_out, 16)
            for h in range(AH_):
                act.dma_start(toe_rows[:, h, :], row_d[h:h + 1, :].to_broadcast((P, 2 * SEQ))).then_inc(toe_out, 16)
            act.wait_ge(x_in, 16)
            with act.Fori(0, DEPTH) as l:
                a0, b0 = l * A_FILLS, l * B_FILLS
                act.wait_ge(b_free, 4 + b0)
                act.dma_start(PARM[:], params[l]).then_inc(par_in, 16)
                act.dma_start(xspill[:, :, :], X[:]).then_inc(x_spilled, 16)
                norm(2 * l, 4 + b0)

                def silu_out(ti):
                    act.wait_ge(conv_done, l * XBC_T + ti + 1)
                    if ti >= 2:
                        act.wait_ge(xbc_out[ti % 2], 16 * (l * (XBC_T // 2) + ti // 2))
                    A(SC[:, ti % 2, :], CV[:, ti % 2, :], ACT.Silu).then_inc(silu_done, 1)
                    act.wait_ge(silu_done, l * XBC_T + ti + 1)
                    act.dma_start(xbc_d[:, :, ti, :].rearrange("c p n -> p c n"),
                                  SC[:, ti % 2, :].rearrange("p (c n) -> p c n", c=NT)).then_inc(xbc_out[ti % 2], 16)

                act.wait_ge(par_in, 16 * (l + 1))
                for ti in range(XBC_T):
                    if ti >= 2:
                        act.wait_ge(conv_done, l * XBC_T + ti - 1)
                    for th in range(2):
                        act.wait_ge(a_full, a0 + 2 * ti + th + 1)
                        A(PAD[:, ti % 2, 2 + th * HALF:2 + (th + 1) * HALF], bank((2 * ti + th) % 4),
                          ACT.Copy).then_inc(a_free, 1)
                    act.wait_ge(a_free, 4 + a0 + 2 * ti + 2)
                    A(CV[:, ti % 2, :], PAD[:, ti % 2, 2:2 + SEQ], ACT.Identity,
                      scale=par_("conv_w", ti * CONV + 2, ti * CONV + 3),
                      bias=par_("conv_b", ti, ti + 1)).then_inc(tap_done, 1)
                    if ti >= 1:
                        silu_out(ti - 1)
                silu_out(XBC_T - 1)
                for i, func in enumerate((ACT.Silu, ACT.Silu, ACT.Gelu_apprx_tanh, ACT.Gelu_apprx_tanh,
                                          ACT.Copy, ACT.Copy, ACT.Copy)):
                    if i >= 2:
                        act.wait_ge(tok_out[i % 2], 16 * (l * (4 - i % 2) + i // 2))
                    for t in range(NT):
                        n = a0 + 2 * XBC_T + i * NT + t
                        act.wait_ge(a_full, n + 1)
                        A(ST[:, i % 2, t, :], PS[:, t % 4, 0:UC], func).then_inc(a_free, 1)
                    act.wait_ge(a_free, 4 + a0 + 2 * XBC_T + i * NT + NT)
                    if i == 3:
                        for t in range(NT):
                            last = A(JUNK8[:, t, :], ST[:, 1, t, :], ACT.Square,
                                     accum_out=VSS[:, t:t + 1])
                        last.then_inc(gv_done, 1)
                    act.dma_start(tok_d[i], ST[:, i % 2]).then_inc(tok_out[i % 2], 16)
                act.wait_ge(vinv_ready, l + 1)
                A(VR[:], VSS[:], ACT.Sqrt).then_inc(vr_ready, 1)
                step = Steps(act, sp_step, 3)
                step.begin(l)
                act.wait_ge(u_ready, l + 1)
                A(EA[:], par_("a_log"), ACT.Exp)
                step.then(A(SPL[:], U[:], ACT.Abs))
                step.then(A(SPL[:], SPL[:], ACT.Exp, scale=-1.0))
                A(SPL[:], SPL[:], ACT.Ln, bias=1.0).then_inc(sp_ready, 1)
                act.wait_ge(acs_ready, l + 1)
                A(EACS[:], ACS[:], ACT.Exp)
                A(CDEC[:], CDEC[:], ACT.Exp)
                step.then(A(DEC[:], DEC[:], ACT.Exp))
                step.end()
                act.sem_inc(dec_ready, 1)
                settle(act)
                with act.Fori(0, NT) as i:
                    n = l * NT + i
                    act.wait_ge(ra_t_full, n + 1)
                    A(BST[:], PS[:, 1, 0:GROUPS * STATE], ACT.Copy).then_inc(ra_bst, 1)
                act.wait_ge(tok_out[0], (l + 1) * 16 * 4)
                act.wait_ge(tok_out[1], (l + 1) * 16 * 3)
                settle(act)
                with act.Fori(0, NT) as c:
                    n = l * NT + c
                    act.wait_ge(chunk_done, 1 + n)
                    A(AST[:], DTA[:, bass.ds(c, 1), :], ACT.Copy).then_inc(ast_ready, 1)
                    act.wait_ge(t_full, n + 1)
                    A(BST[:], PS[:, 1, 0:GROUPS * STATE], ACT.Copy).then_inc(bst_ready, 1)
                    act.wait_ge(xd_ready, n + 1)
                    A(XS[:], bank(0), ACT.Copy).then_inc(xs_ready, 1)
                    for j in range(4):
                        act.wait_ge(seg_ready, n * 4 + j + 1)
                        A(SEG[:, j], SEG[:, j], ACT.Exp).then_inc(exp_ready, 1)
                    act.wait_ge(yz_ready, n + 1)
                    act.wait_ge(yss_ready, 1 + n)
                    for g in range(GROUPS):
                        last = A(JUNK[:, g], YT[:, bass.ds(c, 1), g * 256:(g + 1) * 256], ACT.Square,
                                 accum_out=YSS[:, bass.ds(c, 1), g:g + 1])
                    last.then_inc(yss_ready, 1)
                act.wait_ge(yinv_ready, l + 1)
                A(YR[:], YSS[:], ACT.Sqrt).then_inc(yr_ready, 1)
                act.wait_ge(qk_in, 16 * (l + 1))
                for m in range(2):
                    if m:
                        act.wait_ge(qinv_ready, l * 2 + 1)
                    A(QSQ[:], QK[:, m], ACT.Square).then_inc(qsq_ready, 1)
                for m in range(2):
                    act.wait_ge(qinv_ready, l * 2 + m + 1)
                    A(QSS[:, m], QSS[:, m], ACT.Sqrt).then_inc(qr_ready, 1)
                for m in range(2):
                    for hp in range(2):
                        act.wait_ge(qt_full, (l * 2 + m) * 2 + hp + 1)
                        A((QTT, KTT)[m][:, hp, :], bank(2 * hp, 2), ACT.Copy,
                          scale=QGN[:] if m == 0 else par_("k_gain")).then_inc(qt_ready, 1)
                settle(act)
                with act.Fori(0, NT) as i:
                    n = l * NT + i

                    def exps(h):
                        act.wait_ge(lg_ready, n * 4 + h + 1)
                        if h >= 2:
                            act.wait_ge(pt_full, n * 4 + h - 1)
                        A(PR[:, h % 2, :], LG[:, h % 2, :], ACT.Exp, scale=-1.0, bias=MN[:, h:h + 1],
                          accum_out=RSUM[:, h:h + 1]).then_inc(pr_ready, 1)

                    def evac(h):
                        act.wait_ge(pt_full, n * 4 + h + 1)
                        if h >= 2:
                            act.wait_ge(av_done, n * 4 + h - 1)
                        A(PT[:, h % 2, 0:4, :], bank(4), ACT.Copy).then_inc(pta_ready, 1)

                    exps(0)
                    exps(1)
                    evac(0)
                    exps(2)
                    evac(1)
                    exps(3)
                    evac(2)
                    evac(3)
                settle(act)
                with act.Fori(0, NT // 2) as i2:
                    for par in range(2):
                        n = l * NT + i2 * 2 + par
                        act.wait_ge(att_done, 1 + (l + 1) * NT)
                        act.wait_ge(yh_ready, 1 + n)
                        A(YN[:, par, INNER:DM], YT[:, bass.ds(i2 * 2 + par, 1), INNER:DM], ACT.Copy
                          ).then_inc(yc_ready, 1)
                        act.wait_ge(yt_full, 1 + n + 1)
                        cols = bass.ds((i2 * 2 + par) * P, P)
                        A(HH[:, :, cols], bank(2 * par, 2).rearrange("p (k n) -> p k n", k=KT), ACT.Copy
                          ).then_inc(yh_ready, 1)
                norm(2 * l + 1, 4 + b0 + 4 * OUT_U)
                settle(act)
                with act.Fori(0, NG) as g:
                    n = l * NG + g
                    af = a0 + A_UP + g * 8

                    def take(x):
                        part, ct = divmod(x, 2)
                        act.wait_ge(f_conv, 1 + n * 4 + max(x - 1, 0))
                        for th in range(2):
                            f = 2 * x + th
                            act.wait_ge(a_full, af + f + 1)
                            A(FPAD[:, x % 2, 1 + th * HALF:1 + (th + 1) * HALF], bank(f % 4), ACT.Copy
                              ).then_inc(a_free, 1)
                        act.wait_ge(a_free, 4 + af + 2 * x + 2)
                        if part:
                            act.wait_ge(act_ready, 1 + n * 2)
                        at = PAR["ffn_conv"][0] + (part * FT + ct) * 4
                        A((CVG, CVV)[part][:, ct, :], FPAD[:, x % 2, 1:1 + SEQ], ACT.Identity,
                          scale=PARM[:, bass.ds(g * 8 + at + 1, 1)], bias=PARM[:, bass.ds(g * 8 + at + 3, 1)]
                          ).then_inc(f_tap, 1)

                    def silu(ct):
                        act.wait_ge(f_conv, 1 + n * 4 + ct + 1)
                        A(CVG[:, ct, :], CVG[:, ct, :], ACT.Silu).then_inc(f_silu, 1)

                    def high(ct):
                        act.wait_ge(f_conv, 1 + n * 4 + 3 + ct)
                        if ct == 0:
                            act.wait_ge(down_done, 1 + n)
                        A(AHI[:, ct, :], CVV[:, ct, :], ACT.Copy).then_inc(f_hi, 1)

                    take(0)
                    take(1)
                    silu(0)
                    take(2)
                    silu(1)
                    take(3)
                    high(0)
                    high(1)

        @block.vector
        def _(dve):
            TT, STT, TS = nc.vector.tensor_tensor, nc.vector.scalar_tensor_tensor, nc.vector.tensor_scalar

            def norm(n, gain):
                step = Steps(dve, norm_step, 1)
                step.begin(n)
                dve.wait_ge(sq_used, (n + 1) * KT)
                step.then(TS(MS[:], PS[:, 4, 0:NT], 1.0 / DM, EPS, ALU.mult, ALU.add))
                step.end()
                nc.vector.reciprocal(MS[:], MS[:]).then_inc(inv_ready, 1)
                dve.wait_ge(nb_ready, n + 1)
                for k in range(KT + 1):
                    if k < KT:
                        if k >= 2:
                            dve.wait_ge(h_ready, n * KT + k - 1)
                        STT(HF[:, k % 2, :], X[:, k, :], gain[:, k:k + 1], bank(6, 2), ALU.mult, ALU.mult
                            ).then_inc(hf_ready, 1)
                    if k >= 1:
                        dve.wait_ge(hh_ready, n * KT + k)
                        TT(HL[:, k - 1, :], HF[:, (k - 1) % 2, :], HH[:, k - 1, :].bitcast(F32), ALU.subtract
                           ).then_inc(h_ready, 1)
                dve.wait_ge(h_ready, (n + 1) * KT)

            dve.sem_inc(b_free, 4)
            dve.sem_inc(xbs_used, 2)
            dve.sem_inc(zg_used, 2)
            dve.sem_inc(toe_used, 2)
            dve.wait_ge(row_ps, 1)
            dve.wait_ge(oh_in, 48)
            STT(ROW[:], PS[0:AH_, 0:4, :].rearrange("p a b -> p (a b)"), -1.0, LNR[:], ALU.mult, ALU.add
                ).then_inc(row_sb, 1)
            dve.wait_ge(row_out, 16)
            with dve.Fori(0, DEPTH) as l:
                a0, b0 = l * A_FILLS, l * B_FILLS
                dve.wait_ge(par_in, 16 * (l + 1))
                nc.vector.tensor_copy(WDH[:], par_("w_dt")).then_inc(pad_zero, 1)
                dve.wait_ge(pad_zero, 5 * l + 1)
                TT(WDL[:], par_("w_dt"), WDH[:].bitcast(F32), ALU.subtract).then_inc(wdt_ready, 1)
                TS(QGN[:], par_("q_gain"), -(AD ** -0.5), None, ALU.mult)
                norm(2 * l, par_("mix_gain"))
                for x in range(2):
                    nc.vector.memset(PAD[:, x, 0:2], 0.0)
                    last = nc.vector.memset(PAD[:, x, SEQ + 2:SEQ + 4], 0.0)
                last.then_inc(pad_zero, 1)
                dve.wait_ge(pad_zero, 5 * l + 2)
                step = Steps(dve, conv_step, 3 * XBC_T)
                step.begin(l)
                for ti in range(XBC_T):
                    dve.wait_ge(tap_done, l * XBC_T + ti + 1)
                    for n, j in enumerate((0, 1, 3, 4)):
                        ins = STT(CV[:, ti % 2, :], PAD[:, ti % 2, j:j + SEQ],
                                  par_("conv_w", ti * CONV + j, ti * CONV + j + 1), CV[:, ti % 2, :],
                                  ALU.mult, ALU.add)
                        if n < 3:
                            step.then(ins)
                    ins.then_inc(conv_done, 1)
                step.end()
                step = Steps(dve, v_step, 1)
                step.begin(l)
                dve.wait_ge(gv_done, l + 1)
                step.then(TS(VSS[:], VSS[:], 1.0 / GW, EPS, ALU.mult, ALU.add))
                step.end()
                nc.vector.reciprocal(VSS[:], VSS[:]).then_inc(vinv_ready, 1)
                dve.wait_ge(dt_full, l + 1)
                TT(U[:], PS[:, 4, 0:128].rearrange("p (t e) -> p t e", t=NT),
                   par_("dt_bias").unsqueeze(1).to_broadcast((P, NT, 16)), ALU.add).then_inc(u_ready, 1)
                dve.wait_ge(sp_ready, l + 1)
                step = Steps(dve, dt_step, 3)
                step.begin(l)
                step.then(STT(DT[:], U[:], 0.0, SPL[:], ALU.max, ALU.add))
                STT(DTA[:], DT[:], -1.0, EA[:].unsqueeze(1).to_broadcast((P, NT, 16)), ALU.mult, ALU.mult
                    ).then_inc(dta_ready, 1)
                dve.wait_ge(acs_full, l + 1)
                for d in range(2):
                    ins = nc.vector.tensor_copy(ACS[:, :, d * 8:(d + 1) * 8],
                                                PS[:, 5, d * 64:(d + 1) * 64].rearrange("p (t e) -> p t e", t=NT))
                step.then(ins)
                tot = PS[:, 5, 128:256].rearrange("p (t e) -> p t e", t=NT)
                nc.vector.tensor_copy(CDEC[:], tot)
                TT(DEC[:], tot, ACS[:], ALU.subtract).then_inc(acs_ready, 1)
                dve.wait_ge(dec_ready, l + 1)
                step.then(TT(WST[:], DT[:], DEC[:], ALU.mult))
                step.end()
                dve.wait_ge(a_free, 4 + a0 + A_UP)
                nc.vector.memset(BW[:, NT, :], 0.0).then_inc(pad_zero, 1)
                nc.vector.memset(CURF[:], 0.0).then_inc(pad_zero, 1)
                dve.wait_ge(pad_zero, 5 * l + 4)
                step = Steps(dve, ra_step, 1)
                settle(dve)
                with dve.Fori(0, NT) as i:
                    n = l * NT + i
                    c = i * -1 + (NT - 1)
                    step.begin(n)
                    dve.wait_ge(ra_t_full, n + 1)
                    TT(XW[:].rearrange("p (h e) -> p h e", h=HEADS), bank(0).rearrange("p (h e) -> p h e", h=HEADS),
                       WST[:, bass.ds(c, 1), 8:16].rearrange("p a h -> p (a h)").unsqueeze(2).to_broadcast(
                           (P, HEADS, HD)), ALU.mult).then_inc(ra_xw, 1)
                    new = BW[:, bass.ds(c, 1), :].rearrange("p a n -> p (a n)")
                    old = BW[:, bass.ds(c + 1, 1), :].rearrange("p a n -> p (a n)")
                    dve.wait_ge(ra_done, 1 + n)
                    step.then(TT(new.rearrange("p (h e) -> p h e", h=HEADS), old.rearrange("p (h e) -> p h e", h=HEADS),
                                 CDEC[:, bass.ds(c, 1), 8:16].rearrange("p a h -> p (a h)").unsqueeze(2).to_broadcast(
                                     (P, HEADS, HD)), ALU.mult))
                    step.end()
                    dve.wait_ge(ra_s_full, n + 1)
                    TT(new, new, bank(2), ALU.add).then_inc(ra_done, 1)
                dve.wait_ge(vr_ready, l + 1)
                dve.wait_ge(x_spilled, 16 * (l + 1))
                step = Steps(dve, chunk_step, 13)
                settle(dve)
                with dve.Fori(0, NT // 2) as i2:
                    for par in range(2):
                        c = i2 * 2 + par
                        n = l * NT + c
                        step.begin(n)

                        def heads(t, lo):
                            return t[:, bass.ds(c, 1), lo:lo + 8].rearrange("p a h -> p (a h)").unsqueeze(
                                2).to_broadcast((P, HEADS, HD))

                        def by_head(t):
                            return t.rearrange("p (h e) -> p h e", h=HEADS)

                        dve.wait_ge(t_full, n + 1)
                        TT(by_head(XD[:, 0, :]), by_head(bank(0)), heads(DT, 0), ALU.mult)
                        TT(by_head(XD[:, 1, :]), by_head(bank(0)), heads(DT, 8), ALU.mult)
                        TT(by_head(XW[:]), by_head(bank(0)), heads(WST, 0), ALU.mult).then_inc(xd_ready, 1)
                        dve.wait_ge(cb_full, n + 1)
                        for d, tri in enumerate((tri_f, tri_b)):
                            ins = TT(CBM[:, d], PS[:, 2, 0:256].rearrange("p (g t) -> p g t", g=GROUPS),
                                     tri.unsqueeze(1).to_broadcast((P, GROUPS, P)), ALU.mult)
                        ins.then_inc(cbm_ready, 1)
                        dve.wait_ge(zg_full[par], 16 * (l * (NT // 2) + i2 + 1))
                        STT(VN[:], ZG[:, par, 3, :], VR[:, bass.ds(c, 1)], par_("v_gain"), ALU.mult, ALU.mult
                            ).then_inc(vn_ready, 1)
                        for j in range(4):
                            d, g = divmod(j, 2)
                            dve.wait_ge(ab_full, n * 4 + j + 1)
                            at = d * 8 + g * 4
                            step.then(TT(SEG[:, j], bank(3 + j % 2).rearrange("p (h t) -> p h t", h=4),
                               ACS[:, bass.ds(c, 1), at:at + 4].rearrange("p a h -> p (a h)").unsqueeze(
                                   2).to_broadcast((P, 4, P)), ALU.subtract))
                            nc.vector.tensor_scalar_min(SEG[:, j], SEG[:, j], 0.0).then_inc(seg_ready, 1)
                        dve.wait_ge(cbm_ready, n + 1)
                        for j in range(4):
                            d, g = divmod(j, 2)
                            dve.wait_ge(exp_ready, n * 4 + j + 1)
                            TT(SEG[:, j], SEG[:, j], CBM[:, d, g, :].unsqueeze(1).to_broadcast((P, 4, P)),
                               ALU.mult).then_inc(w_masked, 1)
                        dve.wait_ge(yo_full, n + 1)
                        step.then(TT(by_head(CURF[:]), by_head(CURF[:]), heads(CDEC, 0), ALU.mult))
                        dve.wait_ge(sf_full, n + 1)
                        step.then(TT(CURF[:], CURF[:], bank(1), ALU.add))
                        TT(by_head(Y2[:]), by_head(bank(7)), heads(EACS, 8), ALU.mult)
                        step.then(TT(by_head(Y1[:]), by_head(bank(6)), heads(EACS, 0), ALU.mult))
                        step.then(TT(Y1[:], Y1[:], Y2[:], ALU.add))
                        dve.wait_ge(xs_ready, n + 1)
                        step.then(TT(by_head(Y2[:]), by_head(XS[:]), per_head(par_("d_skip")), ALU.mult))
                        step.then(TT(Y1[:], Y1[:], Y2[:], ALU.add))
                        dve.wait_ge(yd_full, n + 1)
                        step.then(TT(Y1[:], Y1[:], bank(5), ALU.add))
                        TT(YT[:, bass.ds(c, 1), 0:INNER].rearrange("p a n -> p (a n)"), Y1[:],
                           ZG[:, par, 0:2, :].rearrange("p a b -> p (a b)"), ALU.mult).then_inc(yz_ready, 1)
                        dve.wait_ge(mx_full, n + 1)
                        step.then(TT(GT[:].rearrange("p (g e) -> p g e", g=GG),
                                     PS[:, 2, 0:GW].rearrange("p (g e) -> p g e", g=GG), per_head(par_("b_s")), ALU.add))
                        step.then(TT(YT[:, bass.ds(c, 1), INNER:INNER + GW].rearrange("p a n -> p (a n)"), GT[:],
                                     ZG[:, par, 2, :], ALU.mult))
                        dve.sem_inc(zg_used, 1)
                        dve.sem_inc(chunk_done, 1)
                        step.end()
                dve.wait_ge(yss_ready, 1 + (l + 1) * NT)
                step = Steps(dve, yr_step, 1)
                step.begin(l)
                step.then(TS(YSS[:], YSS[:], 1.0 / 256, EPS, ALU.mult, ALU.add))
                step.end()
                nc.vector.reciprocal(YSS[:], YSS[:]).then_inc(yinv_ready, 1)
                step = Steps(dve, q_step, 4)
                step.begin(l)
                for m in range(2):
                    dve.wait_ge(qsq_ready, l * 2 + m + 1)
                    step.then(nc.vector.reduce_sum(QSS[:, m], QSQ[:].rearrange("p t (h e) -> p (t h) e", e=AD), AX.X))
                    step.then(TS(QSS[:, m], QSS[:, m], 1.0 / AD, EPS, ALU.mult, ALU.add))
                    nc.vector.reciprocal(QSS[:, m], QSS[:, m]).then_inc(qinv_ready, 1)
                step.end()
                for m in range(2):
                    dve.wait_ge(qr_ready, l * 2 + m + 1)
                    q = QK[:, m].rearrange("p t (h e) -> p (t h) e", e=AD)
                    TT(q, q, QSS[:, m].unsqueeze(2).to_broadcast((P, NT * AH_, AD)), ALU.mult).then_inc(qn_ready, 1)
                dve.wait_ge(qt_ready, (l + 1) * 4)
                step = Steps(dve, att_step, 1)
                settle(dve)
                with dve.Fori(0, NT // 2) as i2:
                    for par in range(2):
                        i = i2 * 2 + par
                        n = l * NT + i
                        step.begin(n)
                        nc.vector.tensor_copy(QS[:, par], QTT[:, :, bass.ds(i * P, P)]).then_inc(qs_ready, 1)

                        def logits(h):
                            dve.wait_ge(s_full, n * 4 + h + 1)
                            if h % 2 == 0:
                                dve.wait_ge(toe_full[h // 2], 16 * (n + 1))
                            if h >= 2:
                                dve.wait_ge(pr_ready, n * 4 + h - 1)
                            settle(dve)
                            nc.vector.tensor_tensor_reduce(
                                out=LG[:, h % 2, :], in0=bank(2 * (h % 2), 2), in1=TOE[:, h // 2, h % 2, :],
                                scale=1.0, scalar=3e38, op0=ALU.add, op1=ALU.min,
                                accum_out=MN[:, h:h + 1]).then_inc(lg_ready, 1)
                            if h % 2:
                                dve.wait_ge(lg_ready, n * 4 + h + 1)
                                dve.sem_inc(toe_used, 1)

                        def evac(h):
                            dve.wait_ge(pt_full, n * 4 + h + 1)
                            if h >= 2:
                                dve.wait_ge(av_done, n * 4 + h - 1)
                            nc.vector.tensor_copy(PT[:, h % 2, 4:8, :].rearrange("p a b -> p (a b)"), bank(5)
                                                  ).then_inc(ptd_ready, 1)

                        logits(0)
                        logits(1)
                        evac(0)
                        logits(2)
                        evac(1)
                        logits(3)
                        evac(2)
                        evac(3)
                        dve.wait_ge(att_done, 1 + n)
                        step.then(nc.vector.reciprocal(RC[:], RSUM[:]))
                        step.end()
                        dve.wait_ge(av_done, n * 4 + 4)
                        TT(YT[:, bass.ds(i, 1), INNER + GW:DM].rearrange("p a (h e) -> p (a h) e", h=AH_),
                           PS[:, 6, 0:AW].rearrange("p (h e) -> p h e", h=AH_), per_head(RC[:]), ALU.mult
                           ).then_inc(att_done, 1)
                dve.wait_ge(yr_ready, l + 1)
                settle(dve)
                with dve.Fori(0, NT // 2) as i2:
                    for par in range(2):
                        c = i2 * 2 + par
                        n = l * NT + c
                        dve.wait_ge(yt_full, 1 + n)
                        for g in range(GROUPS):
                            cols = slice(g * 256, (g + 1) * 256)
                            ins = STT(YN[:, par, cols], YT[:, bass.ds(c, 1), cols].rearrange("p a n -> p (a n)"),
                                      YR[:, bass.ds(c, 1), g:g + 1].rearrange("p a n -> p (a n)"),
                                      par_("out_gain", g * 256, (g + 1) * 256), ALU.mult, ALU.mult)
                        ins.then_inc(yn_ready, 1)
                        dve.wait_ge(yh_ready, 1 + n + 1)
                        cols = bass.ds(c * P, P)
                        TT(HL[:, :, cols], bank(2 * par, 2).rearrange("p (k n) -> p k n", k=KT),
                           HH[:, :, cols].bitcast(F32), ALU.subtract).then_inc(yl_ready, 1)

                def add(f, n0, nb):
                    dt, th = divmod(f, 2)
                    dve.wait_ge(b_full, n0 + f + 1)
                    x = X[:, dt, th * HALF:(th + 1) * HALF]
                    TT(x, bank(4 + f % 4), x, ALU.add).then_inc(b_free, 1)

                dve.wait_ge(x_back, 16 * (l + 1))
                for f in range(16):
                    add(f, b0, 4)
                dve.wait_ge(b_free, 4 + b0 + 16)
                norm(2 * l + 1, par_("ffn_gain"))
                for x in range(2):
                    nc.vector.memset(FPAD[:, x, 0:1], 0.0)
                    last = nc.vector.memset(FPAD[:, x, SEQ + 1:SEQ + 2], 0.0)
                last.then_inc(pad_zero, 1)
                dve.wait_ge(pad_zero, 5 * l + 5)
                step = Steps(dve, f_step, 6)

                def conv(g, x):
                    part, ct = divmod(x, 2)
                    n = l * NG + g
                    t = (CVG, CVV)[part][:, ct, :]
                    at = PAR["ffn_conv"][0] + (part * FT + ct) * 4
                    dve.wait_ge(f_tap, n * 4 + x + 1)
                    step.then(STT(t, FPAD[:, x % 2, 0:SEQ], PARM[:, bass.ds(g * 8 + at, 1)], t, ALU.mult, ALU.add))
                    ins = STT(t, FPAD[:, x % 2, 2:2 + SEQ], PARM[:, bass.ds(g * 8 + at + 2, 1)], t,
                              ALU.mult, ALU.add)
                    if part:
                        step.then(ins)
                        dve.wait_ge(f_silu, n * 2 + ct + 1)
                        ins = TT(t, t, CVG[:, ct, :], ALU.mult)
                    ins.then_inc(f_conv, 1)

                def low(g, ct):
                    n = l * NG + g
                    dve.wait_ge(f_hi, n * 2 + ct + 1)
                    TT(ALO[:, ct, :], CVV[:, ct, :], AHI[:, ct, :].bitcast(F32), ALU.subtract
                       ).then_inc(act_ready, 1)

                def group(g, adds):
                    step.begin(l * NG + g)
                    n0 = b0 + 4 * OUT_U + (g - 1) * 16
                    conv(g, 0)
                    for f in range(4 if adds else 0):
                        add(f, n0, 0)
                    conv(g, 1)
                    for f in range(4, 16 if adds else 4):
                        add(f, n0, 0)
                    conv(g, 2)
                    conv(g, 3)
                    low(g, 0)
                    low(g, 1)
                    step.end()

                group(0, False)
                settle(dve)
                with dve.Fori(1, NG) as g:
                    group(g, True)
                for f in range(16):
                    add(f, b0 + 4 * OUT_U + (NG - 1) * 16, 0)


def rel_constants():
    d = np.arange(2 * SEQ) - SEQ
    nb, exact = NBUCK // 2, NBUCK // 4
    n = np.abs(d)
    large = exact + (np.log(np.maximum(n, 1).astype(np.float32) / np.float32(exact))
                     / np.float32(np.log(1024 / exact)) * np.float32(nb - exact)).astype(np.int32)
    bucket = np.where(d > 0, nb, 0) + np.where(n < exact, n, np.minimum(large, nb - 1))
    onehot = (np.arange(NBUCK)[:, None] == bucket[None, :]).astype(np.float32)
    count = sum(((d % dil == 0) & (n <= win // 2)).astype(np.int32)
                for win, dil in ((128, 1), (512, 4), (2048, 16)))
    ln = np.where(count > 0, -np.log(np.maximum(count, 1)), 1e30).astype(np.float32)
    return onehot, np.ascontiguousarray(np.broadcast_to(ln, (AH_, 2 * SEQ)))


def chip_constants():
    i = np.arange(P)
    return np.concatenate([np.eye(P), i[:, None] <= i[None, :], i[:, None] >= i[None, :], np.ones((P, P))],
                          axis=1).astype(np.float32)


def weight_stream(w_in, w_out, w_up, w_down):
    def cols(w, a):
        return w[:, a:a + UC].reshape(2, 4, P, UC).transpose(0, 2, 1, 3).reshape(2, P, 1024)

    def rows(w, a):
        return w[a:a + UC].reshape(2, P, DM)

    units = []
    for l in range(DEPTH):
        dt0 = XBC_T * P + INNER
        after = dt0 + 16
        units += [cols(w_in[l], a) for a in range(0, dt0, UC)]
        units += [cols(w_in[l], after + a) for a in range(0, 5 * UC, UC)]
        units += [cols(w_out[l], a) for a in range(0, DM, UC)]
        for g in range(NG):
            units += [cols(w_up[l], g * UC)]
            if g:
                units += [rows(w_down[l], (g - 1) * UC)]
            units += [cols(w_up[l], FFN + g * UC)]
        units += [rows(w_down[l], (NG - 1) * UC)]
    return np.stack(units)


def parameters(i):
    def feat(a):
        return a.reshape(-1, P).T

    def row(a):
        return np.broadcast_to(a.reshape(1, -1), (P, a.size))

    dt0 = XBC_T * P + INNER
    out = []
    for l in range(DEPTH):
        conv = i["ssd_conv_w"][l].reshape(CONV, XBC_T, P).transpose(2, 1, 0).reshape(P, -1)
        fcw = np.concatenate([i["ffn_conv_w"][l], i["ffn_conv_b"][l][None]], 0)
        parts = dict(
            mix_gain=feat(i["mix_norm_gain"][l]), ffn_gain=feat(i["ffn_norm_gain"][l]),
            conv_w=conv, conv_b=feat(i["ssd_conv_b"][l]), dt_bias=row(i["ssd_dt_bias"][l]),
            a_log=row(i["ssd_a_log"][l]), d_skip=row(i["ssd_d"][l]), out_gain=row(i["ssd_out_gain"][l]),
            v_gain=row(i["gmlp_v_gain"][l]), b_s=i["gmlp_b_s"][l].T,
            q_gain=np.concatenate([i["attn_q_gain"][l]] * 2)[:, None],
            k_gain=np.concatenate([i["attn_k_gain"][l]] * 2)[:, None],
            w_s=i["gmlp_w_s"][l].transpose(2, 0, 1).reshape(P, -1),
            w_dt=i["w_in"][l][:, dt0:dt0 + 16].reshape(KT, P, 16).transpose(1, 0, 2).reshape(P, -1),
            ffn_conv=fcw.reshape(4, 2 * FT, P).transpose(2, 1, 0).reshape(P, -1))
        out.append(np.concatenate([parts[n] for n, _ in _PARTS], axis=1))
    return np.stack(out)


def kernel(**inputs):
    from concourse import bacc
    from concourse.bass_utils import run_bass_kernel_spmd

    i = {k: np.asarray(v) for k, v in inputs.items()}
    onehot, lnrow = rel_constants()
    arrays = dict(
        xT=i["x"][0].T.reshape(KT, P, SEQ).transpose(1, 0, 2),
        wst=weight_stream(i["w_in"], i["w_out"], i["ffn_w_up"], i["ffn_w_down"]),
        par=parameters(i), consts=chip_constants(), onehot=onehot, lnrow=lnrow, table=i["rel_bias_table"])
    arrays = {k: np.ascontiguousarray(v) for k, v in arrays.items()}
    nc = bacc.Bacc("TRN2", target_bir_lowering=False, num_devices=1)
    aps = [nc.dram_tensor(k, v.shape, F32, kind="ExternalInput").ap() for k, v in arrays.items()]
    out = nc.dram_tensor("outT", (P, KT, SEQ), F32, kind="ExternalOutput").ap()
    trunk(nc, *aps, out)
    r = run_bass_kernel_spmd(nc, [arrays], core_ids=[0])
    y = np.asarray(r.results[0]["outT"])
    return np.ascontiguousarray(y.transpose(1, 0, 2).reshape(DM, SEQ).T)[None]
```

```python
import concourse.bass as bass
from concourse import mybir
from contextlib import ExitStack
import numpy as np

F32 = mybir.dt.float32
F32R = mybir.dt.float32r
ALU = mybir.AluOpType
ACT = mybir.ActivationFunctionType
AX = mybir.AxisListType

P = 128
DEPTH, SEQ, DM = 2, 1024, 1024
KT = DM // P
NT = SEQ // P
HALF = 512
HEADS, HD, GROUPS, STATE = 8, 64, 2, 128
INNER = HEADS * HD
XBC_T = (INNER + 2 * GROUPS * STATE) // P
CONV = 5
GG, GW = 4, 256
AH_, AD, AW = 4, 64, 256
FFN = 2816
FT = FFN // P
UC = 256
NG = FFN // UC
XBC_U = XBC_T * P // UC
TOK_U = 7
IN_U = XBC_U + TOK_U
OUT_U = DM // UC
UNITS = IN_U + OUT_U + 3 * NG
SLOTS = 3
AHEAD = IN_U + SLOTS
EPS = 1e-6
NBUCK = 32
A_FILLS = 2 * XBC_T + TOK_U * NT + 8 * NG
B_FILLS = 4 * OUT_U + 16 * NG
BF = 2 * KT
A_UP = 2 * XBC_T + TOK_U * NT

_PARTS = [("mix_gain", KT), ("ffn_gain", KT), ("conv_w", XBC_T * CONV), ("conv_b", XBC_T),
          ("dt_bias", 16), ("a_log", 16), ("d_skip", HEADS), ("out_gain", INNER), ("v_gain", GW),
          ("b_s", GG), ("q_gain", 1), ("k_gain", 1), ("w_s", GG * P), ("w_dt", KT * 16),
          ("ffn_conv", 2 * FT * 4)]
PAR = {}
_at = 0
for _n, _w in _PARTS:
    PAR[_n] = (_at, _w)
    _at += _w
NPAR = _at


class Steps:

    def __init__(self, eng, sem, per_pass):
        self.eng, self.sem, self.per = eng, sem, per_pass

    def begin(self, n):
        self.base, self.k = n * self.per, 0

    def then(self, ins):
        ins.then_inc(self.sem, 1)
        self.k += 1
        self.eng.wait_ge(self.sem, self.base + self.k)

    def end(self):
        assert self.k == self.per, f"{self.sem}: {self.k} steps, not {self.per}"


def trunk(nc, xT, wst, params, consts, onehot, lnrow, table, outT):
    xspill = nc.dram_tensor("xspill", (P, KT, SEQ), F32, kind="Internal").ap()
    xbc_d = nc.dram_tensor("xbc_d", (NT, P, XBC_T, P), F32, kind="Internal").ap()
    tok_d = nc.dram_tensor("tok_d", (TOK_U, P, NT, UC), F32, kind="Internal").ap()
    row_d = nc.dram_tensor("row_d", (AH_, 2 * SEQ), F32, kind="Internal").ap()
    toe_d = nc.dram_tensor("toe_d", (AH_, P * (2 * SEQ + 1)), F32, kind="Internal").ap()
    toe_rows = toe_d.rearrange("h (p n) -> p h n", p=P)[:, :, 0:2 * SEQ]
    toe_cols = toe_d[:, 0:P * 2 * SEQ].rearrange("h (p n) -> p h n", p=P)

    with ExitStack() as ctx:
        top = [-(-nc.sbuf_base // 32) * 32]

        def place(name, shape, at=None, dt=F32):
            size = 4 * int(np.prod(shape[1:]))
            if at is None:
                at = top[0]
                top[0] += -(-size // 32) * 32
            return nc.alloc_sbuf_tensor_at(name, shape, dt, offset=at)

        RAW = place("RAW", [P, 2, 1024])
        WH = place("WH", [P, SLOTS, 2048], dt=F32R)
        WL = place("WL", [P, SLOTS, 2048], dt=F32R)
        PARM = place("PARM", [P, NPAR])
        CST = place("CST", [P, 4 * P])
        WD = place("WD", [P, KT, 32], dt=F32R)
        U = place("U", [P, NT, 16])
        SPL = place("SPL", [P, NT, 16])
        DT = place("DT", [P, NT, 16])
        DTA = place("DTA", [P, NT, 16])
        ACS = place("ACS", [P, NT, 16])
        DEC = place("DEC", [P, NT, 16])
        EACS = place("EACS", [P, NT, 16])
        CDEC = place("CDEC", [P, NT, 16])
        WST = place("WST", [P, NT, 16])
        EA = place("EA", [P, 16])
        MS = place("MS", [P, NT])
        RS = place("RS", [P, NT])
        VSS = place("VSS", [P, NT])
        VR = place("VR", [P, NT])
        YSS = place("YSS", [P, NT, 2])
        YR = place("YR", [P, NT, 2])
        QSS = place("QSS", [P, 2, NT * AH_])
        NACS = place("NACS", [P, NT, 16])
        QGN = place("QGN", [P, 1])
        ident, tri_f, tri_b, ones = (CST[:, i * P:(i + 1) * P] for i in range(4))

        def par_(name, a=0, b=None):
            at, w = PAR[name]
            return PARM[:, at + a:at + (w if b is None else b)]

        h_at = top[0]
        top[0] += 2 * KT * SEQ * 4
        HH = place("HH", [P, KT, SEQ], h_at, F32R)
        HL = place("HL", [P, KT, SEQ], h_at + KT * SEQ * 4, F32R)
        x_at = top[0]
        top[0] += KT * SEQ * 4
        X = place("X", [P, KT, SEQ], x_at)
        YT = place("YT", [P, NT, DM], x_at)
        u_at = top[0]
        SQ = place("SQ", [P, 2, SEQ], u_at + 24608)
        HF = place("HF", [P, 2, SEQ], u_at + 32800)
        PAD = place("PAD", [P, 2, SEQ + 4], u_at)
        CV = place("CV", [P, 2, SEQ], u_at + 8224)
        SC = place("SC", [P, 2, SEQ], u_at + 16416)
        JUNK8 = place("JUNK8", [P, NT, UC], u_at)
        ST = place("ST", [P, 2, NT, UC], u_at + 24608)
        DTF = place("DTF", [32, SEQ], u_at + 32800)
        u_end = u_at + 24608 + 16384
        AHI = place("AHI", [P, 2, SEQ], u_at, F32R)
        ALO = place("ALO", [P, 2, SEQ], u_at + 8192, F32R)
        FPAD = place("FPAD", [P, 2, SEQ + 2], u_at + 16384)
        CVG = place("CVG", [P, 2, SEQ], u_at + 24608)
        CVV = place("CVV", [P, 2, SEQ], u_at + 32800)
        YN = place("YN", [P, 2, DM], u_at)
        ZG = place("ZG", [P, 2, 4, UC], u_at + 8192)
        XBS = place("XBS", [P, 2, XBC_T, P], u_at + 16384)
        QS = place("QS", [P, 2, 2, P], u_at + 24576)
        AST = place("AST", [P, 16], u_at + 26624)
        MN = place("MN", [P, AH_], u_at + 26688)
        RSUM = place("RSUM", [P, 2, AH_], u_at + 26720)
        RC = place("RC", [P, AH_], u_at + 26752)
        KN = place("KN", [P, NT, AW], u_at + 26784)
        JUNK = place("JUNK", [P, GROUPS, 256], u_at + 34976)
        IDR = place("IDR", [P, P], u_at + 37024, F32R)
        FAR = place("FAR", [P, 2, P], u_at + 37536, F32R)
        m_at = [h_at]

        def work(name, shape):
            t = place(name, shape, m_at[0])
            m_at[0] += 4 * int(np.prod(shape[1:]))
            assert m_at[0] <= v_at
            return t

        v_at = x_at - 2 * 4 * NT * AW
        V = place("V", [P, NT, AW], v_at)
        QN = place("QN", [P, NT, AW], v_at + 4 * NT * AW)

        BW = work("BW", [P, NT + 1, INNER])
        CURF = work("CURF", [P, INNER])
        XS = work("XS", [P, INNER])
        BC = work("BC", [P, 2, GROUPS, P])
        XD = work("XD", [P, 2, INNER])
        XW = work("XW", [P, INNER])
        seg_at = m_at[0]
        SEG = work("SEG", [P, 4, 4, P])
        XWA = place("XWA", [P, 2, INNER], seg_at)
        BSTA = place("BSTA", [P, 2, GROUPS * STATE], seg_at + 2 * 4 * INNER)
        Y1 = work("Y1", [P, INNER])
        Y2 = work("Y2", [P, INNER])
        VN = work("VN", [P, GW])
        GT = work("GT", [P, GW])
        m_at[0] = h_at
        KTT = work("KTT", [P, 2, SEQ])
        QTT = work("QTT", [P, 2, SEQ])
        TOE = work("TOE", [P, 2, 2, SEQ])
        LG = place("LG", [P, 2, SEQ], u_at)
        PR = place("PR", [P, 2, SEQ], u_at + 8192)
        PT = place("PT", [P, 2, NT, P], u_at + 16384)
        OH = place("OH", [NBUCK, 2 * SEQ], u_at)
        LNR = place("LNR", [AH_, 2 * SEQ], u_at + 8192)
        ROW = place("ROW", [AH_, 2 * SEQ], u_at + 16384)
        TAB = place("TAB", [NBUCK, AH_], u_at + 24576)
        assert u_end <= nc.sbuf_top, (u_end, nc.sbuf_top)

        PS = ctx.enter_context(nc.psum_tensor("PS", [P, 8, HALF], F32))

        def sem(name):
            return ctx.enter_context(nc.semaphore(name))

        raw_full = [sem("raw_full0"), sem("raw_full1")]
        hi_done, w_ready, w_used = sem("hi_done"), sem("w_ready"), sem("w_used")
        cst_in, x_in, par_in, oh_in = sem("cst_in"), sem("x_in"), sem("par_in"), sem("oh_in")
        row_ps, row_sb, row_out, toe_out = sem("row_ps"), sem("row_sb"), sem("row_out"), sem("toe_out")
        a_full, a_free, b_full, b_free = sem("a_full"), sem("a_free"), sem("b_full"), sem("b_free")
        sq_ready, sq_used, ss_ready = sem("sq_ready"), sem("sq_used"), sem("ss_ready")
        inv_ready, rs_ready, nb_ready = sem("inv_ready"), sem("rs_ready"), sem("nb_ready")
        hf_ready, hh_ready, h_ready = sem("hf_ready"), sem("hh_ready"), sem("h_ready")
        norm_step, settled = sem("norm_step"), sem("settled")
        x_spilled, x_back, y_out = sem("x_spilled"), sem("x_back"), sem("y_out")
        wdt_ready, pad_zero = sem("wdt_ready"), sem("pad_zero")
        tap_done, conv_done, silu_done = sem("tap_done"), sem("conv_done"), sem("silu_done")
        conv_step = sem("conv_step")
        xbc_out = [sem("xbc_out0"), sem("xbc_out1")]
        tok_out = [sem("tok_out0"), sem("tok_out1")]
        gv_done, vinv_ready, vr_ready, v_step = sem("gv_done"), sem("vinv_ready"), sem("vr_ready"), sem("v_step")
        dtf_full, dtf_ready = sem("dtf_full"), sem("dtf_ready")
        dt_full, u_ready, sp_ready, dta_ready = sem("dt_full"), sem("u_ready"), sem("sp_ready"), sem("dta_ready")
        acs_full, acs_ready, dec_ready, wst_ready = sem("acs_full"), sem("acs_ready"), sem("dec_ready"), sem("wst_ready")
        sp_step, dt_step = sem("sp_step"), sem("dt_step")
        xbs_full = [sem("xbs_full0"), sem("xbs_full1")]
        zg_full = [sem("zg_full0"), sem("zg_full1")]
        xbs_used, zg_used = sem("xbs_used"), sem("zg_used")
        ra_t_full, ra_bst, ra_xw, ra_s_full, ra_done, ra_step = (
            sem("ra_t_full"), sem("ra_bst"), sem("ra_xw"), sem("ra_s_full"), sem("ra_done"), sem("ra_step"))
        ast_ready, t_full, bst_ready, xs_ready = sem("ast_ready"), sem("t_full"), sem("bst_ready"), sem("xs_ready")
        ab_full, curf_ready, y12_done, gt_done = sem("ab_full"), sem("curf_ready"), sem("y12_done"), sem("gt_done")
        far_ready = sem("far_ready")
        exp_ready, w_masked, yo_full, sf_full = sem("exp_ready"), sem("w_masked"), sem("yo_full"), sem("sf_full")
        xd_ready, yd_full, yz_ready, yss_ready = sem("xd_ready"), sem("yd_full"), sem("yz_ready"), sem("yss_ready")
        vn_ready, mx_full, chunk_done, chunk_step = sem("vn_ready"), sem("mx_full"), sem("chunk_done"), sem("chunk_step")
        yinv_ready, yr_ready, yr_step = sem("yinv_ready"), sem("yr_ready"), sem("yr_step")
        qk_in, v_in, qsq_ready, qinv_ready = sem("qk_in"), sem("v_in"), sem("qsq_ready"), sem("qinv_ready")
        qr_ready, qn_ready, qt_full, qt_ready, q_step = (
            sem("qr_ready"), sem("qn_ready"), sem("qt_full"), sem("qt_ready"), sem("q_step"))
        toe_full = [sem("toe_full0"), sem("toe_full1")]
        toe_used = sem("toe_used")
        qs_ready, s_full, lg_ready, pr_ready = sem("qs_ready"), sem("s_full"), sem("lg_ready"), sem("pr_ready")
        pt_full, pta_ready, ptd_ready, av_done = sem("pt_full"), sem("pta_ready"), sem("ptd_ready"), sem("av_done")
        att_done, att_step = sem("att_done"), sem("att_step")
        yn_ready, yc_ready, yt_full, yh_ready, yl_ready = (
            sem("yn_ready"), sem("yc_ready"), sem("yt_full"), sem("yh_ready"), sem("yl_ready"))
        f_tap, f_conv, f_silu, f_hi, act_ready, f_step, down_done = (
            sem("f_tap"), sem("f_conv"), sem("f_silu"), sem("f_hi"), sem("act_ready"), sem("f_step"), sem("down_done"))

        block = ctx.enter_context(nc.Block())

        def settle(eng):
            eng.sem_inc(settled, 1)

        def bank(b, n=1):
            return PS[:, b, :] if n == 1 else PS[:, b:b + n, :].rearrange("p a b -> p (a b)")

        def per_head(t, w=HD):
            return t.unsqueeze(2).to_broadcast((P, t.shape[1], w))

        @block.sync
        def _(sp):
            def weights(l, first, last):
                settle(sp)
                with sp.Fori(first, last) as u:
                    for hf in range(2):
                        sp.wait_ge(w_ready, (l * UNITS + u) * 2 + hf + 1)
                        sp.dma_start(RAW[:, hf, :], wst[l * UNITS + u, hf]).then_inc(raw_full[hf], 16)

            sp.dma_start(CST[:], consts[:, :]).then_inc(cst_in, 16)
            sp.dma_start(X[:], xT[:, :, :]).then_inc(x_in, 16)
            with sp.Fori(0, DEPTH) as l:
                weights(l, 0, AHEAD)
                for par in range(2):
                    sp.wait_ge(xbc_out[par], (l + 1) * 16 * (XBC_T // 2))
                settle(sp)
                with sp.Fori(0, NT // 2) as i2:
                    for par in range(2):
                        sp.wait_ge(xbs_used, l * 2 * NT + i2 * 2 + par + 1)
                        sp.dma_start(XBS[:, par], xbc_d[i2 * -2 + (NT - 1 - par)]).then_inc(xbs_full[par], 16)
                sp.wait_ge(tok_out[0], (l + 1) * 16 * 4)
                settle(sp)
                sp.wait_ge(tok_out[1], (l + 1) * 16 * 3)
                settle(sp)
                sp.dma_start(QN[:], tok_d[4]).then_inc(qk_in, 16)
                sp.dma_start(KN[:], tok_d[5]).then_inc(qk_in, 16)
                sp.dma_start(V[:], tok_d[6]).then_inc(v_in, 16)
                settle(sp)
                with sp.Fori(0, NT // 2) as i2:
                    for par in range(2):
                        sp.wait_ge(xbs_used, l * 2 * NT + NT + i2 * 2 + par + 1)
                        sp.dma_start(XBS[:, par], xbc_d[2 * i2 + par]).then_inc(xbs_full[par], 16)
                        sp.wait_ge(zg_used, l * NT + i2 * 2 + par + 1)
                        sp.dma_start(ZG[:, par], tok_d[0:4, :, 2 * i2 + par, :].rearrange("u p n -> p u n")
                                     ).then_inc(zg_full[par], 16)
                sp.wait_ge(yz_ready, 1 + (l + 1) * NT)
                settle(sp)
                sp.wait_ge(toe_out, 16 * AH_)
                settle(sp)
                with sp.Fori(0, NT) as i:
                    for hp in range(2):
                        sp.wait_ge(toe_used, (l * NT + i) * 2 + hp + 1)
                        settle(sp)
                        sp.dma_start(TOE[:, hp], toe_cols[:, 2 * hp:2 * hp + 2, bass.ds(SEQ - P * i, SEQ)]
                                     ).then_inc(toe_full[hp], 16)
                sp.wait_ge(yn_ready, (l + 1) * NT)
                sp.wait_ge(yc_ready, (l + 1) * NT)
                sp.dma_start(X[:], xspill[:, :, :]).then_inc(x_back, 16)
                weights(l, AHEAD, UNITS)
            sp.wait_ge(b_free, BF + 4 + DEPTH * B_FILLS)
            sp.dma_start(outT[:, :, :], X[:]).then_inc(y_out, 16)
            sp.wait_ge(y_out, 16)

        @block.gpsimd
        def _(pool):
            pool.sem_inc(w_ready, 2)
            with pool.Fori(0, DEPTH * UNITS // SLOTS) as r:
                for s in range(SLOTS):
                    for hf in range(2):
                        n = (r * SLOTS + s) * 2 + hf
                        pool.wait_ge(raw_full[hf], 16 * (r * SLOTS + s + 1))
                        if hf == 0:
                            pool.wait_ge(w_used, r * SLOTS + s + 1)
                        hi = WH[:, s, hf * 1024:(hf + 1) * 1024]
                        settle(pool)
                        nc.gpsimd.tensor_copy(hi, RAW[:, hf, :]).then_inc(hi_done, 1)
                        pool.wait_ge(hi_done, n + 1)
                        nc.gpsimd.tensor_tensor(WL[:, s, hf * 1024:(hf + 1) * 1024], RAW[:, hf, :],
                                                hi.bitcast(F32), ALU.subtract).then_inc(w_ready, 1)

        @block.tensor
        def _(pe):
            def mm3(out, ws, xs, first, last, skip=False):
                (wh, wl), (xh, xl) = ws, xs
                kw = dict(skip_group_check=True) if skip else {}
                nc.tensor.matmul(out, wh, xh, start=first, stop=False, **kw)
                nc.tensor.matmul(out, wh, xl, start=False, stop=False, **kw)
                return nc.tensor.matmul(out, wl, xh, start=False, stop=last, **kw)

            def wtile(s, a):
                return WH[:, s, a:a + P], WL[:, s, a:a + P]

            def unit_ready(l, u):
                pe.wait_ge(w_ready, 2 + (l * UNITS + u) * 2 + 2)

            def norm_sum(n, k):
                pe.wait_ge(sq_ready, n * KT + k + 1)
                for t in range(NT):
                    last = nc.tensor.matmul(PS[:, 0, t:t + 1], SQ[:, k % 2, t * P:(t + 1) * P], ones[:, 0:1],
                                            start=(k == 0 and t == 0), stop=(k == KT - 1),
                                            skip_group_check=True)
                last.then_inc(sq_used, 1)

            def norm_spread(n):
                pe.wait_ge(rs_ready, n + 1)
                for t in range(NT):
                    last = nc.tensor.matmul(PS[:, 6 + t // 4, (t % 4) * P:(t % 4 + 1) * P],
                                            RS[:, t:t + 1].to_broadcast((P, P)), ident, start=True, stop=True)
                last.then_inc(nb_ready, 1)

            def columns_unit(l, u, s, n0, banks, full, free):
                unit_ready(l, u)
                for f in range(4):
                    ct, th = divmod(f, 2)
                    pe.wait_ge(free, n0 + f + 1 + (BF if free is b_free else 0))
                    for k in range(KT):
                        tok = slice(th * HALF, (th + 1) * HALF)
                        last = mm3(bank(banks + f), wtile(s, k * UC + ct * P), (HH[:, k, tok], HL[:, k, tok]),
                                   k == 0, k == KT - 1)
                    last.then_inc(full, 1)
                pe.wait_ge(full, n0 + 4)
                pe.sem_inc(w_used, 1)

            def first_unit(l, u, s, n0, n):
                unit_ready(l, u)
                pe.wait_ge(a_free, n0 + 4)
                for k in range(KT):
                    pe.wait_ge(h_ready, n * KT + k + 1)
                    for f in range(4):
                        ct, th = divmod(f, 2)
                        tok = slice(th * HALF, (th + 1) * HALF)
                        last = mm3(bank(f), wtile(s, k * UC + ct * P), (HH[:, k, tok], HL[:, k, tok]),
                                   k == 0, k == KT - 1)
                        if k == KT - 1:
                            last.then_inc(a_full, 1)
                pe.wait_ge(a_full, n0 + 4)
                pe.sem_inc(w_used, 1)

            pe.wait_ge(cst_in, 16)
            pe.sem_inc(w_used, SLOTS)
            for s in (chunk_done, yss_ready, ra_done, pta_ready, ptd_ready, att_done, yl_ready, yh_ready,
                      yt_full, act_ready, down_done, f_conv, av_done, exp_ready, curf_ready, y12_done,
                      w_masked, ab_full, yd_full, yz_ready):
                pe.sem_inc(s, 1)
            pe.sem_inc(att_done, 1)
            pe.sem_inc(exp_ready, 1)
            pe.wait_ge(oh_in, 48)
            for q in range(4):
                last = nc.tensor.matmul(PS[0:AH_, q, :], TAB[:, :], OH[:, q * HALF:(q + 1) * HALF],
                                        start=True, stop=True)
            last.then_inc(row_ps, 1)
            pe.wait_ge(row_sb, 1)
            with pe.Fori(0, DEPTH) as l:
                a0, b0 = l * A_FILLS, l * B_FILLS
                for k in range(KT):
                    norm_sum(2 * l, k)
                norm_spread(2 * l)
                first_unit(l, 0, 0, a0, 2 * l)
                for u in range(1, XBC_U):
                    columns_unit(l, u, u % SLOTS, a0 + 4 * u, 0, a_full, a_free)
                pe.wait_ge(wdt_ready, l + 1)
                for th in range(2):
                    tok = slice(th * HALF, (th + 1) * HALF)
                    for k in range(KT):
                        nc.tensor.matmul(PS[0:32, 4 + th, :], WD[:, k, :], HH[:, k, tok],
                                         start=(k == 0), stop=False, skip_group_check=True)
                        last = nc.tensor.matmul(PS[0:16, 4 + th, :], WD[:, k, 0:16], HL[:, k, tok],
                                                start=False, stop=(k == KT - 1), skip_group_check=True)
                last.then_inc(dtf_full, 1)
                pe.wait_ge(dtf_ready, l + 1)
                settle(pe)
                for t in range(NT):
                    last = nc.tensor.transpose(PS[:, 6, t * 32:(t + 1) * 32], DTF[:, t * P:(t + 1) * P],
                                               ident[0:32, 0:32])
                last.then_inc(dt_full, 1)
                def tokens_unit(i):
                    unit_ready(l, XBC_U + i)
                    s = (i + XBC_U % SLOTS) % SLOTS
                    wh, wl = WH[:, bass.ds(s, 1), :], WL[:, bass.ds(s, 1), :]
                    for t in range(NT):
                        pe.wait_ge(a_free, a0 + 2 * XBC_T + i * NT + t + 1)
                        for k in range(KT):
                            tok = slice(t * P, (t + 1) * P)
                            cols = slice(k * UC, (k + 1) * UC)
                            xh, xl = HH[:, k, tok], HL[:, k, tok]
                            o = PS[:, t % 4, 0:UC]
                            nc.tensor.matmul(o, xh, wh[:, :, cols], start=(k == 0), stop=False)
                            nc.tensor.matmul(o, xh, wl[:, :, cols], start=False, stop=False)
                            last = nc.tensor.matmul(o, xl, wh[:, :, cols], start=False, stop=(k == KT - 1))
                        last.then_inc(a_full, 1)
                    pe.wait_ge(a_full, a0 + 2 * XBC_T + i * NT + NT)
                    pe.sem_inc(w_used, 1)

                settle(pe)
                with pe.Fori(0, TOK_U // 2) as i:
                    tokens_unit(i)
                pe.wait_ge(dta_ready, l + 1)
                for d, tri in enumerate((tri_f, tri_b)):
                    nc.tensor.matmul(PS[:, 5, d * 64:(d + 1) * 64], tri, DTA[:, :, d * 8:(d + 1) * 8],
                                     start=(d == 0), stop=True, skip_group_check=True)
                nc.tensor.matmul(PS[:, 5, 128:256], ones, DTA[:], start=False, stop=True,
                                 skip_group_check=True).then_inc(acs_full, 1)
                settle(pe)
                with pe.Fori(TOK_U // 2, TOK_U) as i:
                    tokens_unit(i)
                pe.wait_ge(a_free, 4 + a0 + A_UP)

                def ra_turn(i, par, first=False):
                    n = l * NT + i
                    if not first:
                        pe.wait_ge(ra_done, 1 + n - 1)
                    for j in range(6):
                        last = nc.tensor.transpose(PS[:, 3 * par + j // 4, (j % 4) * P:(j % 4 + 1) * P],
                                                   XBS[:, par, j, :], ident)
                    last.then_inc(ra_t_full, 1)

                def ra_state(i, par):
                    n = l * NT + i
                    pe.wait_ge(ra_bst, n + 1)
                    pe.wait_ge(ra_xw, n + 1)
                    for g in range(GROUPS):
                        last = nc.tensor.matmul(PS[:, 2 + 3 * par, g * 256:(g + 1) * 256],
                                                BSTA[:, par, g * P:(g + 1) * P],
                                                XWA[:, par, g * 256:(g + 1) * 256], start=True, stop=True)
                    last.then_inc(ra_s_full, 1)

                pe.wait_ge(xbs_full[0], 16 * (l * NT + 1))
                ra_turn(0, 0, first=True)
                pe.wait_ge(ra_t_full, l * NT + 1)
                pe.sem_inc(xbs_used, 1)
                pe.wait_ge(xbs_full[1], 16 * (l * NT + 1))
                ra_turn(1, 1, first=True)
                ra_state(0, 0)
                pe.wait_ge(ra_t_full, l * NT + 2)
                pe.sem_inc(xbs_used, 1)
                settle(pe)
                with pe.Fori(1, NT // 2) as i2:
                    for par in range(2):
                        pe.wait_ge(xbs_full[par], 16 * (l * NT + i2 + 1))
                        ra_turn(i2 * 2 + par, par)
                        ra_state(i2 * 2 + (par - 1), 1 - par)
                        pe.wait_ge(ra_t_full, l * NT + i2 * 2 + par + 1)
                        pe.sem_inc(xbs_used, 1)
                ra_state(NT - 1, 1)
                pe.wait_ge(ra_done, 1 + (l + 1) * NT)
                pe.wait_ge(far_ready, l + 1)

                def chunk_turn(i2, par):
                    for j in range(6):
                        nc.tensor.transpose(PS[:, j // 4, (j % 4) * P:(j % 4 + 1) * P], XBS[:, par, j, :], ident)
                    for g in range(GROUPS):
                        last = nc.tensor.matmul(PS[:, 1, (2 + g) * P:(3 + g) * P], XBS[:, par, 4 + g, :],
                                                XBS[:, par, 6 + g, :], start=True, stop=True)
                    last.then_inc(t_full, 1)

                def chunk(i2, par, end):
                    c = i2 * 2 + par
                    n = l * NT + c

                    def sums(j):
                        d, g = divmod(j, 2)
                        pe.wait_ge(exp_ready, n * 4 + j + 1)
                        nc.tensor.matmul(bank(2 + j % 2), IDR[:, :],
                                         FAR[:, d, :].unsqueeze(1).to_broadcast((P, 4, P)),
                                         start=True, stop=False, skip_group_check=True)
                        for h in range(4):
                            e = d * 8 + g * 4 + h
                            last = nc.tensor.matmul(PS[:, 2 + j % 2, h * P:(h + 1) * P],
                                                    AST[:, e:e + 1].to_broadcast((P, P)),
                                                    tri_f if d == 0 else tri_b, start=False, stop=True,
                                                    skip_group_check=True)
                        last.then_inc(ab_full, 1)

                    pe.wait_ge(ast_ready, n + 1)
                    sums(0)
                    sums(1)
                    pe.wait_ge(curf_ready, 1 + n)
                    pe.wait_ge(y12_done, 1 + n)
                    for d in range(2):
                        for g in range(GROUPS):
                            cols = slice(g * 256, (g + 1) * 256)
                            st = CURF[:, cols] if d == 0 else BW[:, bass.ds(c + 1, 1), cols]
                            last = nc.tensor.matmul(PS[:, 5 + d, cols], XBS[:, par, 6 + g, :], st,
                                                    start=True, stop=True)
                    last.then_inc(yo_full, 1)
                    pe.wait_ge(vn_ready, n + 1)
                    for g in range(GG):
                        last = nc.tensor.matmul(PS[:, 7, g * HD:(g + 1) * HD], par_("w_s", g * P, (g + 1) * P),
                                                VN[:, g * HD:(g + 1) * HD], start=True, stop=True)
                    last.then_inc(mx_full, 1)
                    sums(2)
                    sums(3)
                    pe.wait_ge(yo_full, n + 1)
                    pe.sem_inc(xbs_used, 1)
                    pe.wait_ge(bst_ready, n + 1)
                    pe.wait_ge(xd_ready, n + 1)
                    pe.wait_ge(gt_done, n + 1)
                    for g in range(GROUPS):
                        last = nc.tensor.matmul(PS[:, 7, g * 256:(g + 1) * 256], BC[:, 0, g, :],
                                                XW[:, g * 256:(g + 1) * 256], start=True, stop=True)
                    last.then_inc(sf_full, 1)
                    if not end:
                        pe.wait_ge(xbs_full[1 - par], 16 * (l * NT + NT // 2 + i2 + par + 1))
                        pe.wait_ge(xs_ready, n + 1)
                        chunk_turn(i2, 1 - par)
                    pe.wait_ge(w_masked, 1 + n * 4 + 4)
                    pe.wait_ge(chunk_done, 1 + n)
                    for g in range(GROUPS):
                        for h in range(4):
                            e = g * 4 + h
                            for d in range(2):
                                last = nc.tensor.matmul(PS[:, 4, e * HD:(e + 1) * HD],
                                                        SEG[:, d * 2 + g, h, :], XD[:, d, e * HD:(e + 1) * HD],
                                                        start=(d == 0), stop=(d == 1))
                    last.then_inc(yd_full, 1)

                pe.wait_ge(xbs_full[0], 16 * (l * NT + NT // 2 + 1))
                chunk_turn(0, 0)
                settle(pe)
                with pe.Fori(0, NT // 2 - 1) as i2:
                    chunk(i2, 0, False)
                    chunk(i2, 1, False)
                chunk(NT // 2 - 1, 0, False)
                chunk(NT // 2 - 1, 1, True)
                pe.wait_ge(yz_ready, 1 + (l + 1) * NT)
                pe.wait_ge(qk_in, 32 * (l + 1))
                for m in range(2):
                    for hp in range(2):
                        f = (l * 2 + m) * 2 + hp
                        if m * 2 + hp >= 2:
                            pe.wait_ge(qt_ready, f - 1)
                        for t in range(NT):
                            last = nc.tensor.transpose(
                                PS[:, 2 * hp + t // 4, (t % 4) * P:(t % 4 + 1) * P],
                                (QN, KN)[m][:, t, hp * P:(hp + 1) * P], ident)
                        last.then_inc(qt_full, 1)
                pe.wait_ge(qt_ready, (l + 1) * 4)
                pe.wait_ge(v_in, 16 * (l + 1))

                def scores(base, j):
                    if j % AH_ == 0:
                        pe.wait_ge(qs_ready, l * NT + base + j // AH_ + 1)
                    s_base, h, par = (l * NT + base) * AH_, j % AH_, j // AH_ % 2
                    if j >= 2:
                        pe.wait_ge(lg_ready, s_base + j - 1)
                    rows = slice(AD * (h % 2), AD * (h % 2) + AD)
                    for th in range(2):
                        last = nc.tensor.matmul(bank(2 * (h % 2) + th), QS[rows, par, h // 2, :],
                                                KTT[rows, h // 2, th * HALF:(th + 1) * HALF],
                                                start=True, stop=True)
                    last.then_inc(s_full, 1)

                def turn(base, j):
                    s_base, h = (l * NT + base) * AH_, j % AH_
                    pe.wait_ge(pr_ready, s_base + j + 1)
                    pe.wait_ge(pta_ready, 1 + s_base + j)
                    pe.wait_ge(ptd_ready, 1 + s_base + j)
                    for t in range(NT):
                        last = nc.tensor.transpose(PS[:, 4 + t // 4, (t % 4) * P:(t % 4 + 1) * P],
                                                   PR[:, h % 2, t * P:(t + 1) * P], ident)
                    last.then_inc(pt_full, 1)

                def values(base, j):
                    s_base, h, par = (l * NT + base) * AH_, j % AH_, j // AH_ % 2
                    if h == 0:
                        pe.wait_ge(att_done, 1 + l * NT + base + par)
                    pe.wait_ge(pta_ready, 1 + s_base + j + 1)
                    pe.wait_ge(ptd_ready, 1 + s_base + j + 1)
                    for t in range(NT):
                        last = nc.tensor.matmul(PS[:, 6 + par, h * AD:(h + 1) * AD], PT[:, h % 2, t, :],
                                                V[:, t, h * AD:(h + 1) * AD],
                                                start=(t == 0), stop=(t == NT - 1))
                    last.then_inc(av_done, 1)

                def two_tiles(base, end):
                    for j in range(2 * AH_):
                        if not end or j + 2 < 2 * AH_:
                            scores(base, j + 2)
                        if not end or j + 1 < 2 * AH_:
                            turn(base, j + 1)
                        values(base, j)

                scores(0, 0)
                scores(0, 1)
                turn(0, 0)
                settle(pe)
                with pe.Fori(0, NT // 2 - 1) as i2:
                    two_tiles(i2 * 2, False)
                two_tiles(NT - 2, True)
                pe.wait_ge(att_done, 2 + (l + 1) * NT)
                settle(pe)
                with pe.Fori(0, NT // 2) as i2:
                    for par in range(2):
                        n = l * NT + i2 * 2 + par
                        pe.wait_ge(yn_ready, n + 1)
                        pe.wait_ge(yc_ready, n + 1)
                        pe.wait_ge(yl_ready, 1 + n)
                        for k in range(KT):
                            last = nc.tensor.transpose(PS[:, 2 * par + k // 4, (k % 4) * P:(k % 4 + 1) * P],
                                                       YN[:, par, k * P:(k + 1) * P], ident)
                        last.then_inc(yt_full, 1)
                pe.wait_ge(yl_ready, 1 + (l + 1) * NT)
                for u in range(OUT_U):
                    columns_unit(l, IN_U + u, (IN_U + u) % SLOTS, b0 + 4 * u, 4, b_full, b_free)
                    for k in range(2 * u - 2, 2 * u) if u else ():
                        norm_sum(2 * l + 1, k)
                for k in range(KT - 2, KT):
                    norm_sum(2 * l + 1, k)
                norm_spread(2 * l + 1)
                s0 = (IN_U + OUT_U) % SLOTS

                def up(g, unit, s, part):
                    columns_unit(l, unit, s, a0 + A_UP + g * 8 + part * 4, 0, a_full, a_free)

                def down(g, unit, s):
                    unit_ready(l, unit)
                    pe.wait_ge(act_ready, 1 + (l * NG + g) * 2 + 2)
                    n0 = b0 + 4 * OUT_U + g * 16
                    for f in range(16):
                        dt, th = divmod(f, 2)
                        tok = slice(th * HALF, (th + 1) * HALF)
                        pe.wait_ge(b_free, BF + n0 + f + 1)
                        for k in range(2):
                            last = mm3(bank(4 + f % 4), wtile(s, k * 1024 + dt * P),
                                       (AHI[:, k, tok], ALO[:, k, tok]), k == 0, k == 1)
                        last.then_inc(b_full, 1)
                    pe.wait_ge(b_full, n0 + 16)
                    pe.sem_inc(w_used, 1)
                    pe.sem_inc(down_done, 1)

                f0 = IN_U + OUT_U
                first_unit(l, f0, s0, a0 + A_UP, 2 * l + 1)
                up(0, f0 + 1, (s0 + 1) % SLOTS, 1)
                settle(pe)
                with pe.Fori(1, NG) as g:
                    up(g, f0 + g * 3 - 1, (s0 + 2) % SLOTS, 0)
                    down(g - 1, f0 + g * 3, s0)
                    up(g, f0 + g * 3 + 1, (s0 + 1) % SLOTS, 1)
                down(NG - 1, f0 + NG * 3 - 1, (s0 + 2) % SLOTS)

        @block.scalar
        def _(act):
            A = nc.scalar.activation

            def norm(n, x_value):
                for k in range(KT):
                    act.wait_ge(b_free, x_value + 2 * k + 2)
                    if k >= 2:
                        act.wait_ge(sq_used, n * KT + k - 1)
                    A(SQ[:, k % 2, :], X[:, k, :], ACT.Square).then_inc(sq_ready, 1)
                act.wait_ge(inv_ready, n + 1)
                A(RS[:], MS[:], ACT.Sqrt).then_inc(rs_ready, 1)
                for k in range(KT):
                    act.wait_ge(hf_ready, n * KT + k + 1)
                    A(HH[:, k, :], HF[:, k % 2, :], ACT.Copy).then_inc(hh_ready, 1)

            act.dma_start(OH[:], onehot[:, :]).then_inc(oh_in, 16)
            act.dma_start(TAB[:], table[:, :]).then_inc(oh_in, 16)
            act.dma_start(LNR[:], lnrow[:, :]).then_inc(oh_in, 16)
            act.sem_inc(a_free, 4)
            act.wait_ge(row_sb, 1)
            act.dma_start(row_d[:, :], ROW[:]).then_inc(row_out, 16)
            act.wait_ge(row_out, 16)
            for h in range(AH_):
                act.dma_start(toe_rows[:, h, :], row_d[h:h + 1, :].to_broadcast((P, 2 * SEQ))).then_inc(toe_out, 16)
            act.wait_ge(x_in, 16)
            with act.Fori(0, DEPTH) as l:
                a0, b0 = l * A_FILLS, l * B_FILLS
                act.wait_ge(act_ready, 1 + l * NG * 2)
                act.dma_start(PARM[:], params[l]).then_inc(par_in, 16)
                norm(2 * l, 4 + b0)
                act.dma_start(xspill[:, :, :], X[:]).then_inc(x_spilled, 16)

                def silu_out(ti):
                    act.wait_ge(conv_done, l * XBC_T + ti + 1)
                    if ti >= 2:
                        act.wait_ge(xbc_out[ti % 2], 16 * (l * (XBC_T // 2) + ti // 2))
                    A(SC[:, ti % 2, :], CV[:, ti % 2, :], ACT.Silu).then_inc(silu_done, 1)
                    act.wait_ge(silu_done, l * XBC_T + ti + 1)
                    act.dma_start(xbc_d[:, :, ti, :].rearrange("c p n -> p c n"),
                                  SC[:, ti % 2, :].rearrange("p (c n) -> p c n", c=NT)).then_inc(xbc_out[ti % 2], 16)

                act.wait_ge(par_in, 16 * (l + 1))
                for ti in range(XBC_T):
                    if ti >= 2:
                        act.wait_ge(conv_done, l * XBC_T + ti - 1)
                    for th in range(2):
                        act.wait_ge(a_full, a0 + 2 * ti + th + 1)
                        A(PAD[:, ti % 2, 2 + th * HALF:2 + (th + 1) * HALF], bank((2 * ti + th) % 4),
                          ACT.Copy).then_inc(a_free, 1)
                    act.wait_ge(a_free, 4 + a0 + 2 * ti + 2)
                    A(CV[:, ti % 2, :], PAD[:, ti % 2, 2:2 + SEQ], ACT.Identity,
                      scale=par_("conv_w", ti * CONV + 2, ti * CONV + 3),
                      bias=par_("conv_b", ti, ti + 1)).then_inc(tap_done, 1)
                    if ti >= 1:
                        silu_out(ti - 1)
                silu_out(XBC_T - 1)
                act.wait_ge(dtf_full, l + 1)
                A(DTF[:], PS[0:32, 4:6, :].rearrange("p a b -> p (a b)"), ACT.Copy).then_inc(dtf_ready, 1)
                step = Steps(act, sp_step, 3)
                step.begin(l)

                def tok_store(i):
                    act.dma_start(tok_d[i], ST[:, i % 2]).then_inc(tok_out[i % 2], 16)

                for i, func in enumerate((ACT.Silu, ACT.Silu, ACT.Gelu_apprx_tanh, ACT.Gelu_apprx_tanh,
                                          ACT.Copy, ACT.Copy, ACT.Copy)):
                    if i >= 2:
                        act.wait_ge(tok_out[i % 2], 16 * (l * (4 - i % 2) + i // 2))
                    if i == 1:
                        act.wait_ge(dt_full, l + 1)
                    for t in range(NT):
                        n = a0 + 2 * XBC_T + i * NT + t
                        act.wait_ge(a_full, n + 1)
                        A(ST[:, i % 2, t, :], PS[:, t % 4, 0:UC], func).then_inc(a_free, 1)
                        if i >= 5 and t == 3:
                            act.wait_ge(qinv_ready, l * 2 + i - 4)
                            A(QSS[:, i - 5], QSS[:, i - 5], ACT.Sqrt).then_inc(qr_ready, 1)
                    act.wait_ge(a_free, 4 + a0 + 2 * XBC_T + i * NT + NT)
                    if i == 3:
                        for t in range(NT):
                            last = A(JUNK8[:, t, :], ST[:, 1, t, :], ACT.Square,
                                     accum_out=VSS[:, t:t + 1])
                        last.then_inc(gv_done, 1)
                    if i == 4:
                        act.wait_ge(gv_done, l + 1)
                        act.wait_ge(vinv_ready, l + 1)
                        A(VR[:], VSS[:], ACT.Sqrt).then_inc(vr_ready, 1)
                    if i in (4, 5):
                        if i == 5:
                            act.wait_ge(qinv_ready, l * 2 + 1)
                        A(JUNK8[:], ST[:, i % 2], ACT.Square).then_inc(qsq_ready, 1)
                    if i not in (4, 5):
                        tok_store(i)
                    if i >= 5:
                        act.wait_ge(qn_ready, l * 2 + i - 4)
                        tok_store(i - 1)
                    if i == 0:
                        act.wait_ge(u_ready, l + 1)
                        A(EA[:], par_("a_log"), ACT.Exp)
                        step.then(A(SPL[:], U[:], ACT.Abs))
                        step.then(A(SPL[:], SPL[:], ACT.Exp, scale=-1.0))
                        A(SPL[:], SPL[:], ACT.Ln, bias=1.0).then_inc(sp_ready, 1)
                    if i == 3:
                        act.wait_ge(acs_ready, l + 1)
                        A(EACS[:], ACS[:], ACT.Exp)
                        A(CDEC[:], CDEC[:], ACT.Exp)
                        step.then(A(DEC[:], DEC[:], ACT.Exp))
                        act.sem_inc(dec_ready, 1)
                step.end()
                settle(act)
                with act.Fori(0, NT // 2) as i2:
                    for par in range(2):
                        n = l * NT + i2 * 2 + par
                        act.wait_ge(ra_t_full, n + 1)
                        A(BSTA[:, par, :], PS[:, 1 + 3 * par, 0:GROUPS * STATE], ACT.Copy).then_inc(ra_bst, 1)
                act.wait_ge(tok_out[0], (l + 1) * 16 * 4)
                act.wait_ge(tok_out[1], (l + 1) * 16 * 3)
                settle(act)
                with act.Fori(0, NT // 2) as i2:
                    for par in range(2):
                        c = i2 * 2 + par
                        n = l * NT + c
                        act.wait_ge(ab_full, 1 + n * 4)
                        settle(act)
                        A(AST[:], DTA[:, bass.ds(c, 1), :], ACT.Copy).then_inc(ast_ready, 1)
                        act.wait_ge(t_full, n + 1)
                        act.wait_ge(w_masked, 1 + n * 4)
                        A(BC[:].rearrange("p a g n -> p (a g n)"), bank(1), ACT.Copy).then_inc(bst_ready, 1)
                        for j in range(4):
                            d, g = divmod(j, 2)
                            act.wait_ge(ab_full, 1 + n * 4 + j + 1)
                            if j == 0:
                                act.wait_ge(yd_full, 1 + n)
                            settle(act)
                            for h in range(4):
                                e = d * 8 + g * 4 + h
                                last = A(SEG[:, j, h, :], PS[:, 2 + j % 2, h * P:(h + 1) * P], ACT.Exp,
                                         bias=NACS[:, bass.ds(c, 1), e:e + 1].rearrange("p a b -> p (a b)"))
                            last.then_inc(exp_ready, 1)
                            if j == 0:
                                act.wait_ge(xd_ready, n + 1)
                                act.wait_ge(yz_ready, 1 + n)
                                A(XS[:], bank(0), ACT.Copy).then_inc(xs_ready, 1)
                for m in range(2):
                    for hp in range(2):
                        act.wait_ge(qt_full, (l * 2 + m) * 2 + hp + 1)
                        A((QTT, KTT)[m][:, hp, :], bank(2 * hp, 2), ACT.Copy,
                          scale=QGN[:] if m == 0 else par_("k_gain")).then_inc(qt_ready, 1)

                def exps(base, j):
                    s_base, h, par = (l * NT + base) * AH_, j % AH_, j // AH_ % 2
                    act.wait_ge(lg_ready, s_base + j + 1)
                    if j >= 2:
                        act.wait_ge(pt_full, s_base + j - 1)
                    A(PR[:, h % 2, :], LG[:, h % 2, :], ACT.Exp, scale=-1.0, bias=MN[:, h:h + 1],
                      accum_out=RSUM[:, par, h:h + 1]).then_inc(pr_ready, 1)

                def evac(base, j):
                    s_base, h = (l * NT + base) * AH_, j % AH_
                    act.wait_ge(pt_full, s_base + j + 1)
                    if j:
                        act.wait_ge(av_done, 1 + s_base + j - 1)
                    A(PT[:, h % 2, 0:4, :], bank(4), ACT.Copy).then_inc(pta_ready, 1)

                def two_tiles(base, end):
                    for j in range(2 * AH_):
                        if not end or j + 1 < 2 * AH_:
                            evac(base, j + 1)
                        if not end or j + 2 < 2 * AH_:
                            exps(base, j + 2)

                exps(0, 0)
                exps(0, 1)
                evac(0, 0)
                act.wait_ge(yz_ready, 1 + (l + 1) * NT)
                for c in range(NT):
                    if c:
                        act.wait_ge(yss_ready, 1 + l * NT + c)
                    for g in range(GROUPS):
                        last = A(JUNK[:, g], YT[:, c, g * 256:(g + 1) * 256], ACT.Square,
                                 accum_out=YSS[:, c, g:g + 1])
                    last.then_inc(yss_ready, 1)
                settle(act)
                with act.Fori(0, NT // 2 - 1) as i2:
                    two_tiles(i2 * 2, False)
                two_tiles(NT - 2, True)
                act.wait_ge(yinv_ready, l + 1)
                A(YR[:], YSS[:], ACT.Sqrt).then_inc(yr_ready, 1)
                settle(act)
                with act.Fori(0, NT // 2) as i2:
                    for par in range(2):
                        n = l * NT + i2 * 2 + par
                        act.wait_ge(att_done, 2 + (l + 1) * NT)
                        act.wait_ge(yh_ready, 1 + n)
                        A(YN[:, par, INNER:DM], YT[:, bass.ds(i2 * 2 + par, 1), INNER:DM], ACT.Copy
                          ).then_inc(yc_ready, 1)
                        act.wait_ge(yt_full, 1 + n + 1)
                        cols = bass.ds((i2 * 2 + par) * P, P)
                        A(HH[:, :, cols], bank(2 * par, 2).rearrange("p (k n) -> p k n", k=KT), ACT.Copy
                          ).then_inc(yh_ready, 1)
                norm(2 * l + 1, 4 + b0 + BF)
                settle(act)
                with act.Fori(0, NG) as g:
                    n = l * NG + g
                    af = a0 + A_UP + g * 8

                    def take(x):
                        part, ct = divmod(x, 2)
                        act.wait_ge(f_conv, 1 + n * 4 + max(x - 1, 0))
                        for th in range(2):
                            f = 2 * x + th
                            act.wait_ge(a_full, af + f + 1)
                            A(FPAD[:, x % 2, 1 + th * HALF:1 + (th + 1) * HALF], bank(f % 4), ACT.Copy
                              ).then_inc(a_free, 1)
                        act.wait_ge(a_free, 4 + af + 2 * x + 2)
                        if part:
                            act.wait_ge(act_ready, 1 + n * 2)
                        at = PAR["ffn_conv"][0] + (part * FT + ct) * 4
                        A((CVG, CVV)[part][:, ct, :], FPAD[:, x % 2, 1:1 + SEQ], ACT.Identity,
                          scale=PARM[:, bass.ds(g * 8 + at + 1, 1)], bias=PARM[:, bass.ds(g * 8 + at + 3, 1)]
                          ).then_inc(f_tap, 1)

                    def silu(ct):
                        act.wait_ge(f_conv, 1 + n * 4 + ct + 1)
                        A(CVG[:, ct, :], CVG[:, ct, :], ACT.Silu).then_inc(f_silu, 1)

                    def high(ct):
                        act.wait_ge(f_conv, 1 + n * 4 + 3 + ct)
                        if ct == 0:
                            act.wait_ge(down_done, 1 + n)
                        A(AHI[:, ct, :], CVV[:, ct, :], ACT.Copy).then_inc(f_hi, 1)

                    take(0)
                    take(1)
                    silu(0)
                    take(2)
                    silu(1)
                    take(3)
                    high(0)
                    high(1)

        @block.vector
        def _(dve):
            TT, STT, TS = nc.vector.tensor_tensor, nc.vector.scalar_tensor_tensor, nc.vector.tensor_scalar

            def norm(n, gain):
                step = Steps(dve, norm_step, 1)
                step.begin(n)
                dve.wait_ge(sq_used, (n + 1) * KT)
                step.then(TS(MS[:], PS[:, 0, 0:NT], 1.0 / DM, EPS, ALU.mult, ALU.add))
                step.end()
                nc.vector.reciprocal(MS[:], MS[:]).then_inc(inv_ready, 1)
                dve.wait_ge(nb_ready, n + 1)
                for k in range(KT + 1):
                    if k < KT:
                        if k >= 2:
                            dve.wait_ge(h_ready, n * KT + k - 1)
                        STT(HF[:, k % 2, :], X[:, k, :], gain[:, k:k + 1], bank(6, 2), ALU.mult, ALU.mult
                            ).then_inc(hf_ready, 1)
                    if k >= 1:
                        dve.wait_ge(hh_ready, n * KT + k)
                        TT(HL[:, k - 1, :], HF[:, (k - 1) % 2, :], HH[:, k - 1, :].bitcast(F32), ALU.subtract
                           ).then_inc(h_ready, 1)
                dve.wait_ge(h_ready, (n + 1) * KT)

            dve.sem_inc(b_free, BF + 4)
            dve.sem_inc(xbs_used, 2)
            dve.sem_inc(zg_used, 2)
            dve.sem_inc(toe_used, 2)
            dve.wait_ge(row_ps, 1)
            dve.wait_ge(oh_in, 48)
            STT(ROW[:], PS[0:AH_, 0:4, :].rearrange("p a b -> p (a b)"), -1.0, LNR[:], ALU.mult, ALU.add
                ).then_inc(row_sb, 1)
            dve.wait_ge(row_out, 16)
            with dve.Fori(0, DEPTH) as l:
                a0, b0 = l * A_FILLS, l * B_FILLS
                dve.wait_ge(par_in, 16 * (l + 1))
                norm(2 * l, par_("mix_gain"))
                w_dt = par_("w_dt").rearrange("p (k e) -> p k e", k=KT)
                nc.vector.tensor_copy(WD[:, :, 0:16], w_dt).then_inc(pad_zero, 1)
                dve.wait_ge(pad_zero, 5 * l + 1)
                TT(WD[:, :, 16:32], w_dt, WD[:, :, 0:16].bitcast(F32), ALU.subtract).then_inc(wdt_ready, 1)
                TS(QGN[:], par_("q_gain"), -(AD ** -0.5), None, ALU.mult)
                for x in range(2):
                    nc.vector.memset(PAD[:, x, 0:2], 0.0)
                    last = nc.vector.memset(PAD[:, x, SEQ + 2:SEQ + 4], 0.0)
                last.then_inc(pad_zero, 1)
                dve.wait_ge(pad_zero, 5 * l + 2)
                step = Steps(dve, conv_step, 3 * XBC_T)
                step.begin(l)
                for ti in range(XBC_T):
                    dve.wait_ge(tap_done, l * XBC_T + ti + 1)
                    for n, j in enumerate((0, 1, 3, 4)):
                        ins = STT(CV[:, ti % 2, :], PAD[:, ti % 2, j:j + SEQ],
                                  par_("conv_w", ti * CONV + j, ti * CONV + j + 1), CV[:, ti % 2, :],
                                  ALU.mult, ALU.add)
                        if n < 3:
                            step.then(ins)
                    ins.then_inc(conv_done, 1)
                step.end()
                dve.wait_ge(dt_full, l + 1)
                step = Steps(dve, dt_step, 4)
                step.begin(l)
                raw = PS[:, 6, 0:NT * 32].rearrange("p (t e) -> p t e", t=NT)
                step.then(TT(U[:], raw[:, :, 0:16], par_("dt_bias").unsqueeze(1).to_broadcast((P, NT, 16)), ALU.add))
                TT(U[:], U[:], raw[:, :, 16:32], ALU.add).then_inc(u_ready, 1)
                dve.wait_ge(sp_ready, l + 1)
                step.then(STT(DT[:], U[:], 0.0, SPL[:], ALU.max, ALU.add))
                STT(DTA[:], DT[:], -1.0, EA[:].unsqueeze(1).to_broadcast((P, NT, 16)), ALU.mult, ALU.mult
                    ).then_inc(dta_ready, 1)
                dve.wait_ge(acs_full, l + 1)
                for d in range(2):
                    ins = nc.vector.tensor_copy(ACS[:, :, d * 8:(d + 1) * 8],
                                                PS[:, 5, d * 64:(d + 1) * 64].rearrange("p (t e) -> p t e", t=NT))
                step.then(ins)
                tot = PS[:, 5, 128:256].rearrange("p (t e) -> p t e", t=NT)
                nc.vector.tensor_copy(CDEC[:], tot)
                TS(NACS[:], ACS[:], -1.0, None, ALU.mult)
                TT(DEC[:], tot, ACS[:], ALU.subtract).then_inc(acs_ready, 1)
                dve.wait_ge(dec_ready, l + 1)
                step.then(TT(WST[:], DT[:], DEC[:], ALU.mult))
                step.end()
                step = Steps(dve, v_step, 1)
                step.begin(l)
                dve.wait_ge(gv_done, l + 1)
                step.then(TS(VSS[:], VSS[:], 1.0 / GW, EPS, ALU.mult, ALU.add))
                step.end()
                nc.vector.reciprocal(VSS[:], VSS[:]).then_inc(vinv_ready, 1)
                step = Steps(dve, q_step, 4)
                step.begin(l)
                for m in range(2):
                    dve.wait_ge(qsq_ready, l * 2 + m + 1)
                    step.then(nc.vector.reduce_sum(QSS[:, m], JUNK8[:].rearrange("p t (h e) -> p (t h) e", e=AD), AX.X))
                    step.then(TS(QSS[:, m], QSS[:, m], 1.0 / AD, EPS, ALU.mult, ALU.add))
                    nc.vector.reciprocal(QSS[:, m], QSS[:, m]).then_inc(qinv_ready, 1)
                    dve.wait_ge(qr_ready, l * 2 + m + 1)
                    q = ST[:, m].rearrange("p t (h e) -> p (t h) e", e=AD)
                    TT(q, q, QSS[:, m].unsqueeze(2).to_broadcast((P, NT * AH_, AD)), ALU.mult).then_inc(qn_ready, 1)
                step.end()
                dve.wait_ge(a_free, 4 + a0 + A_UP)
                nc.vector.memset(BW[:, NT, :], 0.0).then_inc(pad_zero, 1)
                nc.vector.memset(CURF[:], 0.0).then_inc(pad_zero, 1)
                dve.wait_ge(pad_zero, 5 * l + 4)
                dve.wait_ge(tok_out[0], (l + 1) * 16 * 4)
                dve.wait_ge(tok_out[1], (l + 1) * 16 * 3)
                nc.vector.tensor_copy(IDR[:], ident)
                for d, tri in enumerate((tri_f, tri_b)):
                    last = TS(FAR[:, d, :], tri, 1.0, 1e30, ALU.subtract, ALU.mult)
                last.then_inc(far_ready, 1)
                step = Steps(dve, ra_step, 1)
                settle(dve)
                with dve.Fori(0, NT // 2) as i2:
                    for par in range(2):
                        n = l * NT + i2 * 2 + par
                        c = i2 * -2 + (NT - 1 - par)
                        step.begin(n)

                        def by_decay(t):
                            return t[:, bass.ds(c, 1), 8:16].rearrange("p a h -> p (a h)").unsqueeze(
                                2).to_broadcast((P, HEADS, HD))

                        dve.wait_ge(ra_t_full, n + 1)
                        TT(XWA[:, par].rearrange("p (h e) -> p h e", h=HEADS),
                           bank(3 * par).rearrange("p (h e) -> p h e", h=HEADS), by_decay(WST), ALU.mult
                           ).then_inc(ra_xw, 1)
                        new = BW[:, bass.ds(c, 1), :].rearrange("p a n -> p (a n)")
                        old = BW[:, bass.ds(c + 1, 1), :].rearrange("p a n -> p (a n)")
                        dve.wait_ge(ra_done, 1 + n)
                        step.then(TT(new.rearrange("p (h e) -> p h e", h=HEADS),
                                     old.rearrange("p (h e) -> p h e", h=HEADS), by_decay(CDEC), ALU.mult))
                        step.end()
                        dve.wait_ge(ra_s_full, n + 1)
                        TT(new, new, bank(2 + 3 * par), ALU.add).then_inc(ra_done, 1)
                dve.wait_ge(vr_ready, l + 1)
                dve.wait_ge(x_spilled, 16 * (l + 1))
                step = Steps(dve, chunk_step, 4)
                settle(dve)
                with dve.Fori(0, NT // 2) as i2:
                    for par in range(2):
                        c = i2 * 2 + par
                        n = l * NT + c
                        step.begin(n)

                        def heads(t, lo):
                            return t[:, bass.ds(c, 1), lo:lo + 8].rearrange("p a h -> p (a h)").unsqueeze(
                                2).to_broadcast((P, HEADS, HD))

                        def by_head(t):
                            return t.rearrange("p (h e) -> p h e", h=HEADS)

                        dve.wait_ge(zg_full[par], 16 * (l * (NT // 2) + i2 + 1))
                        STT(VN[:], ZG[:, par, 3, :], VR[:, bass.ds(c, 1)], par_("v_gain"), ALU.mult, ALU.mult
                            ).then_inc(vn_ready, 1)
                        dve.wait_ge(t_full, n + 1)
                        TT(by_head(XW[:]), by_head(bank(0)), heads(WST, 0), ALU.mult)
                        TT(by_head(XD[:, 0, :]), by_head(bank(0)), heads(DT, 0), ALU.mult)
                        TT(by_head(XD[:, 1, :]), by_head(bank(0)), heads(DT, 8), ALU.mult).then_inc(xd_ready, 1)
                        dve.wait_ge(mx_full, n + 1)
                        TT(GT[:].rearrange("p (g e) -> p g e", g=GG),
                           PS[:, 7, 0:GW].rearrange("p (g e) -> p g e", g=GG), per_head(par_("b_s")), ALU.add
                           ).then_inc(gt_done, 1)
                        dve.wait_ge(gt_done, n + 1)
                        TT(YT[:, bass.ds(c, 1), INNER:INNER + GW].rearrange("p a n -> p (a n)"), GT[:],
                           ZG[:, par, 2, :], ALU.mult)
                        dve.wait_ge(yo_full, n + 1)
                        step.then(TT(by_head(CURF[:]), by_head(CURF[:]), heads(CDEC, 0), ALU.mult))
                        TT(by_head(Y2[:]), by_head(bank(6)), heads(EACS, 8), ALU.mult)
                        TT(by_head(Y1[:]), by_head(bank(5)), heads(EACS, 0), ALU.mult).then_inc(y12_done, 1)
                        dve.wait_ge(bst_ready, n + 1)
                        for j in range(4):
                            d, g = divmod(j, 2)
                            dve.wait_ge(exp_ready, 2 + n * 4 + j + 1)
                            TT(SEG[:, j], SEG[:, j], BC[:, 1, g, :].unsqueeze(1).to_broadcast((P, 4, P)),
                               ALU.mult).then_inc(w_masked, 1)
                        dve.wait_ge(sf_full, n + 1)
                        TT(CURF[:], CURF[:], bank(7), ALU.add).then_inc(curf_ready, 1)
                        dve.wait_ge(y12_done, 1 + n + 1)
                        step.then(TT(Y1[:], Y1[:], Y2[:], ALU.add))
                        dve.wait_ge(xs_ready, n + 1)
                        step.then(TT(by_head(Y2[:]), by_head(XS[:]), per_head(par_("d_skip")), ALU.mult))
                        step.then(TT(Y1[:], Y1[:], Y2[:], ALU.add))
                        dve.wait_ge(yd_full, 1 + n + 1)
                        TT(Y1[:], Y1[:], bank(4), ALU.add).then_inc(chunk_done, 1)
                        dve.wait_ge(chunk_done, 1 + n + 1)
                        TT(YT[:, bass.ds(c, 1), 0:INNER].rearrange("p a n -> p (a n)"), Y1[:],
                           ZG[:, par, 0:2, :].rearrange("p a b -> p (a b)"), ALU.mult).then_inc(yz_ready, 1)
                        dve.wait_ge(yz_ready, 1 + n + 1)
                        dve.sem_inc(zg_used, 1)
                        step.end()
                dve.wait_ge(qt_ready, (l + 1) * 4)
                step = Steps(dve, att_step, 1)

                def queries(base, par):
                    nc.vector.tensor_copy(QS[:, par % 2], QTT[:, :, bass.ds(base * P + par * P, P)]
                                          ).then_inc(qs_ready, 1)

                def logits(base, j):
                    n, h = l * NT + base, j % AH_
                    dve.wait_ge(s_full, n * AH_ + j + 1)
                    if h % 2 == 0:
                        dve.wait_ge(toe_full[h // 2], 16 * (n + j // AH_ + 1))
                    if j >= 2:
                        dve.wait_ge(pr_ready, n * AH_ + j - 1)
                    settle(dve)
                    nc.vector.tensor_tensor_reduce(
                        out=LG[:, h % 2, :], in0=bank(2 * (h % 2), 2),
                        in1=TOE[:, h // 2, h % 2, :],
                        scale=1.0, scalar=3e38, op0=ALU.add, op1=ALU.min,
                        accum_out=MN[:, h:h + 1]).then_inc(lg_ready, 1)
                    if h % 2:
                        dve.wait_ge(lg_ready, n * AH_ + j + 1)
                        dve.sem_inc(toe_used, 1)

                def evac(base, j):
                    n, h = l * NT + base, j % AH_
                    dve.wait_ge(pt_full, n * AH_ + j + 1)
                    if j:
                        dve.wait_ge(av_done, 1 + n * AH_ + j - 1)
                    nc.vector.tensor_copy(PT[:, h % 2, 4:8, :].rearrange("p a b -> p (a b)"), bank(5)
                                          ).then_inc(ptd_ready, 1)

                def take(base, par):
                    n = l * NT + base + par
                    step.begin(n)
                    dve.wait_ge(av_done, 1 + n * AH_ + AH_)
                    dve.wait_ge(att_done, 2 + n)
                    step.then(nc.vector.reciprocal(RC[:], RSUM[:, par]))
                    step.end()
                    TT(YT[:, bass.ds(base + par, 1), INNER + GW:DM].rearrange("p a (h e) -> p (a h) e", h=AH_),
                       PS[:, 6 + par, 0:AW].rearrange("p (h e) -> p h e", h=AH_), per_head(RC[:]), ALU.mult
                       ).then_inc(att_done, 1)

                def two_tiles(base, end):
                    for j in range(2 * AH_):
                        if j % AH_ == 0 and not (end and j):
                            queries(base, j // AH_ + 1)
                        if not end or j + 2 < 2 * AH_:
                            logits(base, j + 2)
                        if not end or j + 1 < 2 * AH_:
                            evac(base, j + 1)
                        if j == AH_:
                            take(base, 0)
                    take(base, 1)

                queries(0, 0)
                logits(0, 0)
                logits(0, 1)
                evac(0, 0)
                dve.wait_ge(yss_ready, 1 + (l + 1) * NT)
                yss = Steps(dve, yr_step, 1)
                yss.begin(l)
                yss.then(TS(YSS[:], YSS[:], 1.0 / 256, EPS, ALU.mult, ALU.add))
                yss.end()
                nc.vector.reciprocal(YSS[:], YSS[:]).then_inc(yinv_ready, 1)
                settle(dve)
                with dve.Fori(0, NT // 2 - 1) as i2:
                    two_tiles(i2 * 2, False)
                two_tiles(NT - 2, True)
                dve.wait_ge(yr_ready, l + 1)
                settle(dve)
                with dve.Fori(0, NT // 2) as i2:
                    for par in range(2):
                        c = i2 * 2 + par
                        n = l * NT + c
                        dve.wait_ge(yt_full, 1 + n)
                        for g in range(GROUPS):
                            cols = slice(g * 256, (g + 1) * 256)
                            ins = STT(YN[:, par, cols], YT[:, bass.ds(c, 1), cols].rearrange("p a n -> p (a n)"),
                                      YR[:, bass.ds(c, 1), g:g + 1].rearrange("p a n -> p (a n)"),
                                      par_("out_gain", g * 256, (g + 1) * 256), ALU.mult, ALU.mult)
                        ins.then_inc(yn_ready, 1)
                        dve.wait_ge(yh_ready, 1 + n + 1)
                        cols = bass.ds(c * P, P)
                        TT(HL[:, :, cols], bank(2 * par, 2).rearrange("p (k n) -> p k n", k=KT),
                           HH[:, :, cols].bitcast(F32), ALU.subtract).then_inc(yl_ready, 1)

                def add(f, n0, nb):
                    dt, th = divmod(f, 2)
                    dve.wait_ge(b_full, n0 + f + 1)
                    x = X[:, dt, th * HALF:(th + 1) * HALF]
                    TT(x, bank(4 + f % 4), x, ALU.add).then_inc(b_free, 1)

                dve.wait_ge(x_back, 16 * (l + 1))
                for f in range(16):
                    add(f, b0, 4)
                dve.wait_ge(b_free, BF + 4 + b0 + 16)
                norm(2 * l + 1, par_("ffn_gain"))
                for x in range(2):
                    nc.vector.memset(FPAD[:, x, 0:1], 0.0)
                    last = nc.vector.memset(FPAD[:, x, SEQ + 1:SEQ + 2], 0.0)
                last.then_inc(pad_zero, 1)
                dve.wait_ge(pad_zero, 5 * l + 5)
                step = Steps(dve, f_step, 6)

                def conv(g, x):
                    part, ct = divmod(x, 2)
                    n = l * NG + g
                    t = (CVG, CVV)[part][:, ct, :]
                    at = PAR["ffn_conv"][0] + (part * FT + ct) * 4
                    dve.wait_ge(f_tap, n * 4 + x + 1)
                    step.then(STT(t, FPAD[:, x % 2, 0:SEQ], PARM[:, bass.ds(g * 8 + at, 1)], t, ALU.mult, ALU.add))
                    ins = STT(t, FPAD[:, x % 2, 2:2 + SEQ], PARM[:, bass.ds(g * 8 + at + 2, 1)], t,
                              ALU.mult, ALU.add)
                    if part:
                        step.then(ins)
                        dve.wait_ge(f_silu, n * 2 + ct + 1)
                        ins = TT(t, t, CVG[:, ct, :], ALU.mult)
                    ins.then_inc(f_conv, 1)

                def low(g, ct):
                    n = l * NG + g
                    dve.wait_ge(f_hi, n * 2 + ct + 1)
                    TT(ALO[:, ct, :], CVV[:, ct, :], AHI[:, ct, :].bitcast(F32), ALU.subtract
                       ).then_inc(act_ready, 1)

                def group(g, adds):
                    step.begin(l * NG + g)
                    n0 = b0 + 4 * OUT_U + (g - 1) * 16
                    conv(g, 0)
                    for f in range(4 if adds else 0):
                        add(f, n0, 0)
                    conv(g, 1)
                    for f in range(4, 16 if adds else 4):
                        add(f, n0, 0)
                    conv(g, 2)
                    conv(g, 3)
                    low(g, 0)
                    low(g, 1)
                    step.end()

                group(0, False)
                settle(dve)
                with dve.Fori(1, NG) as g:
                    group(g, True)
                for f in range(16):
                    add(f, b0 + 4 * OUT_U + (NG - 1) * 16, 0)


def rel_constants():
    d = np.arange(2 * SEQ) - SEQ
    nb, exact = NBUCK // 2, NBUCK // 4
    n = np.abs(d)
    large = exact + (np.log(np.maximum(n, 1).astype(np.float32) / np.float32(exact))
                     / np.float32(np.log(1024 / exact)) * np.float32(nb - exact)).astype(np.int32)
    bucket = np.where(d > 0, nb, 0) + np.where(n < exact, n, np.minimum(large, nb - 1))
    onehot = (np.arange(NBUCK)[:, None] == bucket[None, :]).astype(np.float32)
    count = sum(((d % dil == 0) & (n <= win // 2)).astype(np.int32)
                for win, dil in ((128, 1), (512, 4), (2048, 16)))
    ln = np.where(count > 0, -np.log(np.maximum(count, 1)), 1e30).astype(np.float32)
    return onehot, np.ascontiguousarray(np.broadcast_to(ln, (AH_, 2 * SEQ)))


def chip_constants():
    i = np.arange(P)
    return np.concatenate([np.eye(P), i[:, None] <= i[None, :], i[:, None] >= i[None, :], np.ones((P, P))],
                          axis=1).astype(np.float32)


def weight_stream(w_in, w_out, w_up, w_down):
    def cols(w, a):
        return w[:, a:a + UC].reshape(2, 4, P, UC).transpose(0, 2, 1, 3).reshape(2, P, 1024)

    def rows(w, a):
        return w[a:a + UC].reshape(2, P, DM)

    units = []
    for l in range(DEPTH):
        dt0 = XBC_T * P + INNER
        after = dt0 + 16
        units += [cols(w_in[l], a) for a in range(0, dt0, UC)]
        units += [cols(w_in[l], after + a) for a in range(0, 5 * UC, UC)]
        units += [cols(w_out[l], a) for a in range(0, DM, UC)]
        for g in range(NG):
            units += [cols(w_up[l], g * UC)]
            if g:
                units += [rows(w_down[l], (g - 1) * UC)]
            units += [cols(w_up[l], FFN + g * UC)]
        units += [rows(w_down[l], (NG - 1) * UC)]
    return np.stack(units)


def parameters(i):
    def feat(a):
        return a.reshape(-1, P).T

    def row(a):
        return np.broadcast_to(a.reshape(1, -1), (P, a.size))

    dt0 = XBC_T * P + INNER
    out = []
    for l in range(DEPTH):
        conv = i["ssd_conv_w"][l].reshape(CONV, XBC_T, P).transpose(2, 1, 0).reshape(P, -1)
        fcw = np.concatenate([i["ffn_conv_w"][l], i["ffn_conv_b"][l][None]], 0)
        parts = dict(
            mix_gain=feat(i["mix_norm_gain"][l]), ffn_gain=feat(i["ffn_norm_gain"][l]),
            conv_w=conv, conv_b=feat(i["ssd_conv_b"][l]), dt_bias=row(i["ssd_dt_bias"][l]),
            a_log=row(i["ssd_a_log"][l]), d_skip=row(i["ssd_d"][l]), out_gain=row(i["ssd_out_gain"][l]),
            v_gain=row(i["gmlp_v_gain"][l]), b_s=i["gmlp_b_s"][l].T,
            q_gain=np.concatenate([i["attn_q_gain"][l]] * 2)[:, None],
            k_gain=np.concatenate([i["attn_k_gain"][l]] * 2)[:, None],
            w_s=i["gmlp_w_s"][l].transpose(2, 0, 1).reshape(P, -1),
            w_dt=i["w_in"][l][:, dt0:dt0 + 16].reshape(KT, P, 16).transpose(1, 0, 2).reshape(P, -1),
            ffn_conv=fcw.reshape(4, 2 * FT, P).transpose(2, 1, 0).reshape(P, -1))
        out.append(np.concatenate([parts[n] for n, _ in _PARTS], axis=1))
    return np.stack(out)


def kernel(**inputs):
    from concourse import bacc
    from concourse.bass_utils import run_bass_kernel_spmd

    i = {k: np.asarray(v) for k, v in inputs.items()}
    onehot, lnrow = rel_constants()
    arrays = dict(
        xT=i["x"][0].T.reshape(KT, P, SEQ).transpose(1, 0, 2),
        wst=weight_stream(i["w_in"], i["w_out"], i["ffn_w_up"], i["ffn_w_down"]),
        par=parameters(i), consts=chip_constants(), onehot=onehot, lnrow=lnrow, table=i["rel_bias_table"])
    arrays = {k: np.ascontiguousarray(v) for k, v in arrays.items()}
    nc = bacc.Bacc("TRN2", target_bir_lowering=False, num_devices=1)
    aps = [nc.dram_tensor(k, v.shape, F32, kind="ExternalInput").ap() for k, v in arrays.items()]
    out = nc.dram_tensor("outT", (P, KT, SEQ), F32, kind="ExternalOutput").ap()
    trunk(nc, *aps, out)
    r = run_bass_kernel_spmd(nc, [arrays], core_ids=[0])
    y = np.asarray(r.results[0]["outT"])
    return np.ascontiguousarray(y.transpose(1, 0, 2).reshape(DM, SEQ).T)[None]
```

```python
import concourse.bass as bass
from concourse import mybir
from contextlib import ExitStack
import numpy as np

F32 = mybir.dt.float32
F32R = mybir.dt.float32r
ALU = mybir.AluOpType
ACT = mybir.ActivationFunctionType
AX = mybir.AxisListType

P = 128
DEPTH, SEQ, DM = 2, 1024, 1024
KT = DM // P
NT = SEQ // P
HALF = 512
HEADS, HD, GROUPS, STATE = 8, 64, 2, 128
INNER = HEADS * HD
XBC_T = (INNER + 2 * GROUPS * STATE) // P
CONV = 5
GG, GW = 4, 256
AH_, AD, AW = 4, 64, 256
FFN = 2816
FT = FFN // P
UC = 256
NG = FFN // UC
XBC_U = XBC_T * P // UC
TOK_U = 7
IN_U = XBC_U + TOK_U
OUT_U = DM // UC
UNITS = IN_U + OUT_U + 3 * NG
SLOTS = 3
AHEAD = IN_U + SLOTS
EPS = 1e-6
NBUCK = 32
A_FILLS = 2 * XBC_T + TOK_U * NT + 8 * NG
B_FILLS = 4 * OUT_U + 16 * NG
BF = 2 * KT
A_UP = 2 * XBC_T + TOK_U * NT

_PARTS = [("mix_gain", KT), ("ffn_gain", KT), ("conv_w", XBC_T * CONV), ("conv_b", XBC_T),
          ("dt_bias", 16), ("a_log", 16), ("d_skip", HEADS), ("out_gain", INNER), ("v_gain", GW),
          ("b_s", GG), ("q_gain", 1), ("k_gain", 1), ("w_s", GG * P), ("w_dt", KT * 16),
          ("ffn_conv", 2 * FT * 4)]
PAR = {}
_at = 0
for _n, _w in _PARTS:
    PAR[_n] = (_at, _w)
    _at += _w
NPAR = _at


class Steps:

    def __init__(self, eng, sem, per_pass):
        self.eng, self.sem, self.per = eng, sem, per_pass

    def begin(self, n):
        self.base, self.k = n * self.per, 0

    def then(self, ins):
        ins.then_inc(self.sem, 1)
        self.k += 1
        self.eng.wait_ge(self.sem, self.base + self.k)

    def end(self):
        assert self.k == self.per, f"{self.sem}: {self.k} steps, not {self.per}"


def trunk(nc, xT, wst, params, consts, onehot, lnrow, table, outT):
    xspill = nc.dram_tensor("xspill", (P, KT, SEQ), F32, kind="Internal").ap()
    xbc_d = nc.dram_tensor("xbc_d", (NT, P, XBC_T, P), F32, kind="Internal").ap()
    tok_d = nc.dram_tensor("tok_d", (TOK_U, P, NT, UC), F32, kind="Internal").ap()
    row_d = nc.dram_tensor("row_d", (AH_, 2 * SEQ), F32, kind="Internal").ap()
    toe_d = nc.dram_tensor("toe_d", (AH_, P * (2 * SEQ + 1)), F32, kind="Internal").ap()
    toe_rows = toe_d.rearrange("h (p n) -> p h n", p=P)[:, :, 0:2 * SEQ]
    toe_cols = toe_d[:, 0:P * 2 * SEQ].rearrange("h (p n) -> p h n", p=P)

    with ExitStack() as ctx:
        top = [-(-nc.sbuf_base // 32) * 32]

        def place(name, shape, at=None, dt=F32):
            size = 4 * int(np.prod(shape[1:]))
            if at is None:
                at = top[0]
                top[0] += -(-size // 32) * 32
            return nc.alloc_sbuf_tensor_at(name, shape, dt, offset=at)

        RAW = place("RAW", [P, 2, 1024])
        WH = place("WH", [P, SLOTS, 2048], dt=F32R)
        WL = place("WL", [P, SLOTS, 2048], dt=F32R)
        PARM = place("PARM", [P, NPAR])
        CST = place("CST", [P, 4 * P])
        WD = place("WD", [P, KT, 32], dt=F32R)
        U = place("U", [P, NT, 16])
        SPL = place("SPL", [P, NT, 16])
        LDT = place("LDT", [P, NT, 16])
        DT = place("DT", [P, NT, 16])
        DTA = place("DTA", [P, NT, 16])
        ACS = place("ACS", [P, NT, 16])
        DEC = place("DEC", [P, NT, 16])
        EACS = place("EACS", [P, NT, 16])
        CDEC = place("CDEC", [P, NT, 16])
        WST = place("WST", [P, NT, 16])
        EA = place("EA", [P, 16])
        VSS = place("VSS", [P, NT])
        VR = place("VR", [P, NT])
        YSS = place("YSS", [P, NT, 2])
        YR = place("YR", [P, NT, 2])
        QSS = place("QSS", [P, 2, NT * AH_])
        NACS = place("NACS", [P, NT, 16])
        QGN = place("QGN", [P, 1])
        ident, tri_f, tri_b, ones = (CST[:, i * P:(i + 1) * P] for i in range(4))

        def par_(name, a=0, b=None):
            at, w = PAR[name]
            return PARM[:, at + a:at + (w if b is None else b)]

        h_at = top[0]
        top[0] += 2 * KT * SEQ * 4
        HH = place("HH", [P, KT, SEQ], h_at, F32R)
        HL = place("HL", [P, KT, SEQ], h_at + KT * SEQ * 4, F32R)
        x_at = top[0]
        top[0] += KT * SEQ * 4
        X = place("X", [P, KT, SEQ], x_at)
        YT = place("YT", [P, NT, DM], x_at)
        u_at = top[0]
        ACC = place("ACC", [P, SEQ], u_at + 16384)
        INV = place("INV", [P, SEQ], u_at + 20480)
        SQ = place("SQ", [P, 2, SEQ], u_at + 24608)
        HF = place("HF", [P, 2, SEQ], u_at + 32800)
        PAD = place("PAD", [P, 2, SEQ + 4], u_at)
        CV = place("CV", [P, 2, SEQ], u_at + 8224)
        SC = place("SC", [P, 2, SEQ], u_at + 16416)
        JUNK8 = place("JUNK8", [P, NT, UC], u_at)
        ST = place("ST", [P, 2, NT, UC], u_at + 24608)
        DTF = place("DTF", [32, SEQ], u_at + 32800)
        u_end = u_at + 24608 + 16384
        AHI = place("AHI", [P, 2, SEQ], u_at, F32R)
        ALO = place("ALO", [P, 2, SEQ], u_at + 8192, F32R)
        FPAD = place("FPAD", [P, 2, SEQ + 2], u_at + 16384)
        CVG = place("CVG", [P, 2, SEQ], u_at + 24608)
        CVV = place("CVV", [P, 2, SEQ], u_at + 32800)
        YN = place("YN", [P, 2, DM], u_at)
        ZG = place("ZG", [P, 2, 4, UC], u_at + 8192)
        XBS = place("XBS", [P, 2, XBC_T, P], u_at + 16384)
        QSL = place("QSL", [P, 2, 2, P], u_at + 24576, F32R)
        QS = place("QS", [P, 2, AH_, P], u_at + 37024, F32R)
        assert u_at + 37024 + 2 * AH_ * P * 4 <= nc.sbuf_top
        AST = place("AST", [P, 16], u_at + 26624)
        MN = place("MN", [P, AH_], u_at + 26688)
        RSUM = place("RSUM", [P, 2, AH_], u_at + 26720)
        RC = place("RC", [P, AH_], u_at + 26752)
        KN = place("KN", [P, NT, AW], u_at + 26784)
        JUNK = place("JUNK", [P, GROUPS, 256], u_at + 34976)
        IDR = place("IDR", [P, P], u_at + 37024, F32R)
        FAR = place("FAR", [P, 2, P], u_at + 37536, F32R)
        m_at = [h_at]

        def work(name, shape):
            t = place(name, shape, m_at[0])
            m_at[0] += 4 * int(np.prod(shape[1:]))
            assert m_at[0] <= v_at
            return t

        v_at = x_at - 2 * 4 * NT * AW
        V = place("V", [P, NT, AW], v_at)
        QN = place("QN", [P, NT, AW], v_at + 4 * NT * AW)

        BW = work("BW", [P, NT + 1, INNER])
        CURF = work("CURF", [P, INNER])
        XS = work("XS", [P, 2, INNER])
        BC = work("BC", [P, 2, GROUPS, P])
        XW = work("XW", [P, INNER])
        seg_at = m_at[0]
        SEG = [work("SEG0", [P, 4, 4, P]), place("SEG1", [P, 4, 4, P], u_at)]
        XWA = place("XWA", [P, 2, INNER], seg_at)
        BSTA = place("BSTA", [P, 2, GROUPS * STATE], seg_at + 2 * 4 * INNER)
        Y1 = work("Y1", [P, INNER])
        Y2 = work("Y2", [P, INNER])
        VN = work("VN", [P, GW])
        GT = work("GT", [P, GW])
        m_at[0] = h_at
        KX = place("KX", [P, AH_, SEQ], m_at[0], F32R)
        QH = place("QH", [P, AH_, SEQ], m_at[0] + 4 * AH_ * SEQ, F32R)
        m_at[0] += 8 * AH_ * SEQ
        QL = place("QL", [P, 2, SEQ], u_at + 26784, F32R)
        KL = place("KL", [P, 2, SEQ], u_at, F32R)
        TOE = work("TOE", [P, 2, 2, SEQ])
        LG = place("LG", [P, 2, SEQ], u_at)
        PR = place("PR", [P, 2, SEQ], u_at + 8192)
        PT = place("PT", [P, 2, NT, P], u_at + 16384)
        OH = place("OH", [NBUCK, 2 * SEQ], h_at)
        LNR = place("LNR", [AH_, 2 * SEQ], h_at + 8192)
        ROW = place("ROW", [AH_, 2 * SEQ], u_at)
        TAB = place("TAB", [NBUCK, AH_], h_at + 24576)
        assert u_end <= nc.sbuf_top, (u_end, nc.sbuf_top)

        PS = ctx.enter_context(nc.psum_tensor("PS", [P, 8, HALF], F32))

        def sem(name):
            return ctx.enter_context(nc.semaphore(name))

        raw_full = [sem("raw_full0"), sem("raw_full1")]
        hi_done, w_ready, w_used = sem("hi_done"), sem("w_ready"), sem("w_used")
        cst_in, par_in, oh_in = sem("cst_in"), sem("par_in"), sem("oh_in")
        x_in = [sem(f"x_in{i}") for i in range(4)]
        row_ps, row_sb, row_out, toe_out = sem("row_ps"), sem("row_sb"), sem("row_out"), sem("toe_out")
        a_full, a_free, b_full, b_free = sem("a_full"), sem("a_free"), sem("b_full"), sem("b_free")
        sq_ready, sq_used, ss_ready = sem("sq_ready"), sem("sq_used"), sem("ss_ready")
        inv_ready, rs_ready, nb_ready = sem("inv_ready"), sem("rs_ready"), sem("nb_ready")
        hf_ready, hh_ready, h_ready = sem("hf_ready"), sem("hh_ready"), sem("h_ready")
        norm_step, settled = sem("norm_step"), sem("settled")
        x_spilled, x_back, y_out = sem("x_spilled"), sem("x_back"), sem("y_out")
        wdt_ready, pad_zero = sem("wdt_ready"), sem("pad_zero")
        tap_done, conv_done, silu_done = sem("tap_done"), sem("conv_done"), sem("silu_done")
        conv_step = sem("conv_step")
        xbc_out = [sem("xbc_out0"), sem("xbc_out1")]
        tok_out = [sem("tok_out0"), sem("tok_out1")]
        gv_done, vinv_ready, vr_ready, v_step = sem("gv_done"), sem("vinv_ready"), sem("vr_ready"), sem("v_step")
        dtf_full, dtf_ready = sem("dtf_full"), sem("dtf_ready")
        dt_full, u_ready, sp_ready, dta_ready = sem("dt_full"), sem("u_ready"), sem("sp_ready"), sem("dta_ready")
        acs_full, acs_ready, dec_ready, wst_ready = sem("acs_full"), sem("acs_ready"), sem("dec_ready"), sem("wst_ready")
        sp_step, dt_step = sem("sp_step"), sem("dt_step")
        xbs_full = [sem("xbs_full0"), sem("xbs_full1")]
        zg_full = [sem("zg_full0"), sem("zg_full1")]
        xbs_used, zg_used = sem("xbs_used"), sem("zg_used")
        ra_t_full, ra_bst, ra_xw, ra_s_full, ra_done, ra_step = (
            sem("ra_t_full"), sem("ra_bst"), sem("ra_xw"), sem("ra_s_full"), sem("ra_done"), sem("ra_step"))
        ast_ready, t_full, bst_ready, xs_ready = sem("ast_ready"), sem("t_full"), sem("bst_ready"), sem("xs_ready")
        ab_full, curf_ready, y12_done, gt_done = sem("ab_full"), sem("curf_ready"), sem("y12_done"), sem("gt_done")
        far_ready, ldt_ready = sem("far_ready"), sem("ldt_ready")
        exp_ready, w_masked, yo_full, sf_full = sem("exp_ready"), sem("w_masked"), sem("yo_full"), sem("sf_full")
        xw_ready, yd_full, yz_ready, yss_ready = sem("xw_ready"), sem("yd_full"), sem("yz_ready"), sem("yss_ready")
        vn_ready, mx_full, chunk_done, chunk_step = sem("vn_ready"), sem("mx_full"), sem("chunk_done"), sem("chunk_step")
        yinv_ready, yr_ready, yr_step = sem("yinv_ready"), sem("yr_ready"), sem("yr_step")
        qk_in, v_in, qsq_ready, qinv_ready = sem("qk_in"), sem("v_in"), sem("qsq_ready"), sem("qinv_ready")
        qr_ready, qn_ready, qt_full, qt_ready, q_step = (
            sem("qr_ready"), sem("qn_ready"), sem("qt_full"), sem("qt_ready"), sem("q_step"))
        toe_full = [sem("toe_full0"), sem("toe_full1")]
        toe_used = sem("toe_used")
        qh_ready, kx_in, qx_in = sem("qh_ready"), sem("kx_in"), sem("qx_in")
        qs_ready, s_full, lg_ready, pr_ready = sem("qs_ready"), sem("s_full"), sem("lg_ready"), sem("pr_ready")
        pt_full, pta_ready, ptd_ready, av_done = sem("pt_full"), sem("pta_ready"), sem("ptd_ready"), sem("av_done")
        att_done, att_step = sem("att_done"), sem("att_step")
        yn_ready, yc_ready, yt_full, yh_ready, yl_ready = (
            sem("yn_ready"), sem("yc_ready"), sem("yt_full"), sem("yh_ready"), sem("yl_ready"))
        f_tap, f_conv, f_silu, f_hi, act_ready, f_step, down_done = (
            sem("f_tap"), sem("f_conv"), sem("f_silu"), sem("f_hi"), sem("act_ready"), sem("f_step"), sem("down_done"))

        block = ctx.enter_context(nc.Block())

        def settle(eng):
            eng.sem_inc(settled, 1)

        def bank(b, n=1):
            return PS[:, b, :] if n == 1 else PS[:, b:b + n, :].rearrange("p a b -> p (a b)")

        def own(h):
            return slice(AD * (h % 2), AD * (h % 2) + AD)

        def per_head(t, w=HD):
            return t.unsqueeze(2).to_broadcast((P, t.shape[1], w))

        @block.sync
        def _(sp):
            def weights(l, first, last):
                settle(sp)
                with sp.Fori(first, last) as u:
                    for hf in range(2):
                        sp.wait_ge(w_ready, (l * UNITS + u) * 2 + hf + 1)
                        sp.dma_start(RAW[:, hf, :], wst[l * UNITS + u, hf]).then_inc(raw_full[hf], 16)

            sp.dma_start(CST[:], consts[:, :]).then_inc(cst_in, 16)
            for i in range(4):
                k = slice(i * KT // 4, (i + 1) * KT // 4)
                sp.dma_start(X[:, k], xT[:, k, :]).then_inc(x_in[i], 16)
            with sp.Fori(0, DEPTH) as l:
                weights(l, 0, AHEAD)
                for par in range(2):
                    sp.wait_ge(xbc_out[par], (l + 1) * 16 * (XBC_T // 2))
                settle(sp)
                with sp.Fori(0, NT // 2) as i2:
                    for par in range(2):
                        sp.wait_ge(xbs_used, l * 2 * NT + i2 * 2 + par + 1)
                        sp.dma_start(XBS[:, par], xbc_d[i2 * -2 + (NT - 1 - par)]).then_inc(xbs_full[par], 16)
                sp.wait_ge(tok_out[0], (l + 1) * 16 * 4)
                settle(sp)
                sp.wait_ge(tok_out[1], (l + 1) * 16 * 3)
                settle(sp)
                with sp.Fori(0, NT // 2) as i2:
                    for par in range(2):
                        sp.wait_ge(xbs_used, l * 2 * NT + NT + i2 * 2 + par + 1)
                        sp.dma_start(XBS[:, par], xbc_d[2 * i2 + par]).then_inc(xbs_full[par], 16)
                        sp.wait_ge(zg_used, l * NT + i2 * 2 + par + 1)
                        sp.dma_start(ZG[:, par], tok_d[0:4, :, 2 * i2 + par, :].rearrange("u p n -> p u n")
                                     ).then_inc(zg_full[par], 16)
                sp.dma_start(QN[:], tok_d[4]).then_inc(qk_in, 16)
                sp.dma_start(KN[:], tok_d[5]).then_inc(qk_in, 16)
                sp.dma_start(V[:], tok_d[6]).then_inc(v_in, 16)
                sp.wait_ge(yz_ready, 2 + (l + 1) * NT)
                settle(sp)
                sp.wait_ge(toe_out, 16 * AH_)
                settle(sp)
                with sp.Fori(0, NT) as i:
                    for hp in range(2):
                        sp.wait_ge(toe_used, (l * NT + i) * 2 + hp + 1)
                        settle(sp)
                        sp.dma_start(TOE[:, hp], toe_cols[:, 2 * hp:2 * hp + 2, bass.ds(SEQ - P * i, SEQ)]
                                     ).then_inc(toe_full[hp], 16)
                sp.wait_ge(yn_ready, (l + 1) * NT)
                sp.wait_ge(yc_ready, (l + 1) * NT)
                sp.dma_start(X[:], xspill[:, :, :]).then_inc(x_back, 16)
                weights(l, AHEAD, UNITS)
            sp.wait_ge(b_free, BF + 4 + DEPTH * B_FILLS)
            sp.dma_start(outT[:, :, :], X[:]).then_inc(y_out, 16)
            sp.wait_ge(y_out, 16)

        @block.gpsimd
        def _(pool):
            pool.sem_inc(w_ready, 2)
            pool.wait_ge(row_sb, 1)
            pool.dma_start(row_d[:, :], ROW[:]).then_inc(row_out, 16)
            pool.wait_ge(row_out, 16)
            for h in range(AH_):
                pool.dma_start(toe_rows[:, h, :], row_d[h:h + 1, :].to_broadcast((P, 2 * SEQ))).then_inc(toe_out, 16)
            with pool.Fori(0, DEPTH * UNITS // SLOTS) as r:
                for s in range(SLOTS):
                    for hf in range(2):
                        n = (r * SLOTS + s) * 2 + hf
                        pool.wait_ge(raw_full[hf], 16 * (r * SLOTS + s + 1))
                        if hf == 0:
                            pool.wait_ge(w_used, r * SLOTS + s + 1)
                        hi = WH[:, s, hf * 1024:(hf + 1) * 1024]
                        settle(pool)
                        nc.gpsimd.tensor_copy(hi, RAW[:, hf, :]).then_inc(hi_done, 1)
                        pool.wait_ge(hi_done, n + 1)
                        nc.gpsimd.tensor_tensor(WL[:, s, hf * 1024:(hf + 1) * 1024], RAW[:, hf, :],
                                                hi.bitcast(F32), ALU.subtract).then_inc(w_ready, 1)

        @block.tensor
        def _(pe):
            def mm3(out, ws, xs, first, last, skip=False):
                (wh, wl), (xh, xl) = ws, xs
                kw = dict(skip_group_check=True) if skip else {}
                nc.tensor.matmul(out, wh, xh, start=first, stop=False, **kw)
                nc.tensor.matmul(out, wh, xl, start=False, stop=False, **kw)
                return nc.tensor.matmul(out, wl, xh, start=False, stop=last, **kw)

            def wtile(s, a):
                return WH[:, s, a:a + P], WL[:, s, a:a + P]

            def unit_ready(l, u):
                pe.wait_ge(w_ready, 2 + (l * UNITS + u) * 2 + 2)

            def norm_spread(n):
                pe.wait_ge(sq_used, (n + 1) * KT)
                for th in range(2):
                    nc.tensor.matmul(bank(6 + th), ones, ACC[:, th * HALF:(th + 1) * HALF],
                                     start=True, stop=True).then_inc(nb_ready, 1)

            def columns_unit(l, u, s, n0, banks, full, free):
                unit_ready(l, u)
                for f in range(4):
                    ct, th = divmod(f, 2)
                    pe.wait_ge(free, n0 + f + 1 + (BF if free is b_free else 0))
                    for k in range(KT):
                        tok = slice(th * HALF, (th + 1) * HALF)
                        last = mm3(bank(banks + f), wtile(s, k * UC + ct * P), (HH[:, k, tok], HL[:, k, tok]),
                                   k == 0, k == KT - 1)
                    last.then_inc(full, 1)
                pe.wait_ge(full, n0 + 4)
                pe.sem_inc(w_used, 1)

            def first_unit(l, u, s, n0, n):
                unit_ready(l, u)
                pe.wait_ge(a_free, n0 + 4)
                for k in range(KT):
                    pe.wait_ge(h_ready, n * KT + k + 1)
                    for f in range(4):
                        ct, th = divmod(f, 2)
                        tok = slice(th * HALF, (th + 1) * HALF)
                        last = mm3(bank(f), wtile(s, k * UC + ct * P), (HH[:, k, tok], HL[:, k, tok]),
                                   k == 0, k == KT - 1)
                        if k == KT - 1:
                            last.then_inc(a_full, 1)
                pe.wait_ge(a_full, n0 + 4)
                pe.sem_inc(w_used, 1)

            pe.wait_ge(cst_in, 16)
            pe.sem_inc(w_used, SLOTS)
            for s in (chunk_done, yss_ready, ra_done, pta_ready, ptd_ready, att_done, yl_ready, yh_ready,
                      yt_full, act_ready, down_done, f_conv, av_done, exp_ready, curf_ready, y12_done,
                      w_masked, ab_full, yd_full, yz_ready):
                pe.sem_inc(s, 1)
            pe.sem_inc(att_done, 1)
            pe.sem_inc(exp_ready, 1)
            for s in (yz_ready, yd_full, w_masked):
                pe.sem_inc(s, 1)
            for s in (yt_full, yl_ready):
                pe.sem_inc(s, 1)
            pe.wait_ge(oh_in, 48)
            for q in range(4):
                last = nc.tensor.matmul(PS[0:AH_, q, :], TAB[:, :], OH[:, q * HALF:(q + 1) * HALF],
                                        start=True, stop=True)
            last.then_inc(row_ps, 1)
            pe.wait_ge(row_sb, 1)
            with pe.Fori(0, DEPTH) as l:
                a0, b0 = l * A_FILLS, l * B_FILLS
                norm_spread(2 * l)
                first_unit(l, 0, 0, a0, 2 * l)
                for u in range(1, XBC_U):
                    columns_unit(l, u, u % SLOTS, a0 + 4 * u, 0, a_full, a_free)
                pe.wait_ge(wdt_ready, l + 1)
                for th in range(2):
                    tok = slice(th * HALF, (th + 1) * HALF)
                    for k in range(KT):
                        nc.tensor.matmul(PS[0:32, 4 + th, :], WD[:, k, :], HH[:, k, tok],
                                         start=(k == 0), stop=False, skip_group_check=True)
                        last = nc.tensor.matmul(PS[0:16, 4 + th, :], WD[:, k, 0:16], HL[:, k, tok],
                                                start=False, stop=(k == KT - 1), skip_group_check=True)
                last.then_inc(dtf_full, 1)
                pe.wait_ge(dtf_ready, l + 1)
                settle(pe)
                for t in range(NT):
                    last = nc.tensor.transpose(PS[:, 6, t * 32:(t + 1) * 32], DTF[:, t * P:(t + 1) * P],
                                               ident[0:32, 0:32])
                last.then_inc(dt_full, 1)
                def tokens_unit(i):
                    unit_ready(l, XBC_U + i)
                    s = (i + XBC_U % SLOTS) % SLOTS
                    wh, wl = WH[:, bass.ds(s, 1), :], WL[:, bass.ds(s, 1), :]
                    for t in range(NT):
                        pe.wait_ge(a_free, a0 + 2 * XBC_T + i * NT + t + 1)
                        for k in range(KT):
                            tok = slice(t * P, (t + 1) * P)
                            cols = slice(k * UC, (k + 1) * UC)
                            xh, xl = HH[:, k, tok], HL[:, k, tok]
                            o = PS[:, t % 4, 0:UC]
                            nc.tensor.matmul(o, xh, wh[:, :, cols], start=(k == 0), stop=False)
                            nc.tensor.matmul(o, xh, wl[:, :, cols], start=False, stop=False)
                            last = nc.tensor.matmul(o, xl, wh[:, :, cols], start=False, stop=(k == KT - 1))
                        last.then_inc(a_full, 1)
                    pe.wait_ge(a_full, a0 + 2 * XBC_T + i * NT + NT)
                    pe.sem_inc(w_used, 1)

                settle(pe)
                with pe.Fori(0, TOK_U // 2) as i:
                    tokens_unit(i)
                pe.wait_ge(dta_ready, l + 1)
                for d, tri in enumerate((tri_f, tri_b)):
                    nc.tensor.matmul(PS[:, 5, d * 64:(d + 1) * 64], tri, DTA[:, :, d * 8:(d + 1) * 8],
                                     start=(d == 0), stop=True, skip_group_check=True)
                nc.tensor.matmul(PS[:, 5, 128:256], ones, DTA[:], start=False, stop=True,
                                 skip_group_check=True).then_inc(acs_full, 1)
                settle(pe)
                with pe.Fori(TOK_U // 2, TOK_U) as i:
                    tokens_unit(i)
                pe.wait_ge(a_free, 4 + a0 + A_UP)

                def ra_turn(i, par):
                    for j in range(6):
                        last = nc.tensor.transpose(PS[:, 3 * par + j // 4, (j % 4) * P:(j % 4 + 1) * P],
                                                   XBS[:, par, j, :], ident)
                    last.then_inc(ra_t_full, 1)

                def ra_state(i, par, first=False):
                    n = l * NT + i
                    pe.wait_ge(ra_bst, n + 1)
                    pe.wait_ge(ra_xw, n + 1)
                    if not first:
                        pe.wait_ge(ra_done, n)
                    for g in range(GROUPS):
                        last = nc.tensor.matmul(PS[:, 2 + 3 * par, g * 256:(g + 1) * 256],
                                                BSTA[:, par, g * P:(g + 1) * P],
                                                XWA[:, par, g * 256:(g + 1) * 256], start=True, stop=True)
                    last.then_inc(ra_s_full, 1)

                pe.wait_ge(xbs_full[0], 16 * (l * NT + 1))
                ra_turn(0, 0)
                pe.wait_ge(ra_t_full, l * NT + 1)
                pe.sem_inc(xbs_used, 1)
                pe.wait_ge(xbs_full[1], 16 * (l * NT + 1))
                ra_turn(1, 1)
                ra_state(0, 0, first=True)
                pe.wait_ge(ra_t_full, l * NT + 2)
                pe.sem_inc(xbs_used, 1)
                settle(pe)
                with pe.Fori(1, NT // 2) as i2:
                    for par in range(2):
                        pe.wait_ge(xbs_full[par], 16 * (l * NT + i2 + 1))
                        ra_turn(i2 * 2 + par, par)
                        pe.wait_ge(ra_t_full, l * NT + i2 * 2 + par + 1)
                        pe.sem_inc(xbs_used, 1)
                        ra_state(i2 * 2 + (par - 1), 1 - par)
                ra_state(NT - 1, 1)
                pe.wait_ge(ra_done, 1 + (l + 1) * NT)
                pe.wait_ge(far_ready, l + 1)

                def chunk_turn(i2, par):
                    for j in range(6):
                        nc.tensor.transpose(PS[:, j // 4, (j % 4) * P:(j % 4 + 1) * P], XBS[:, par, j, :], ident)
                    for g in range(GROUPS):
                        last = nc.tensor.matmul(PS[:, 1, (2 + g) * P:(3 + g) * P], XBS[:, par, 4 + g, :],
                                                XBS[:, par, 6 + g, :], start=True, stop=True)
                    last.then_inc(t_full, 1)

                def sums(n, j):
                        g, d = divmod(j, 2)
                        if j == 0:
                            pe.wait_ge(ast_ready, n + 1)
                        pe.wait_ge(exp_ready, n * 4 + j + 1)
                        nc.tensor.matmul(bank(2 + j % 2), IDR[:, :],
                                         FAR[:, d, :].unsqueeze(1).to_broadcast((P, 4, P)),
                                         start=True, stop=False, skip_group_check=True)
                        for h in range(4):
                            e = d * 8 + g * 4 + h
                            last = nc.tensor.matmul(PS[:, 2 + j % 2, h * P:(h + 1) * P],
                                                    AST[:, e:e + 1].to_broadcast((P, P)),
                                                    tri_f if d == 0 else tri_b, start=False, stop=True,
                                                    skip_group_check=True)
                        last.then_inc(ab_full, 1)

                def chunk(i2, par, end):
                    c = i2 * 2 + par
                    n = l * NT + c
                    pe.wait_ge(curf_ready, 1 + n)
                    pe.wait_ge(y12_done, 1 + n)
                    for d in range(2):
                        for g in range(GROUPS):
                            cols = slice(g * 256, (g + 1) * 256)
                            st = CURF[:, cols] if d == 0 else BW[:, bass.ds(c + 1, 1), cols]
                            last = nc.tensor.matmul(PS[:, 5 + d, cols], XBS[:, par, 6 + g, :], st,
                                                    start=True, stop=True)
                    last.then_inc(yo_full, 1)
                    sums(n, 2)
                    sums(n, 3)
                    pe.wait_ge(vn_ready, n + 1)
                    for g in range(GG):
                        last = nc.tensor.matmul(PS[:, 7, g * HD:(g + 1) * HD], par_("w_s", g * P, (g + 1) * P),
                                                VN[:, g * HD:(g + 1) * HD], start=True, stop=True)
                    last.then_inc(mx_full, 1)
                    pe.wait_ge(yo_full, n + 1)
                    pe.sem_inc(xbs_used, 1)
                    pe.wait_ge(bst_ready, n + 1)
                    pe.wait_ge(xw_ready, n + 1)
                    pe.wait_ge(gt_done, n + 1)
                    for g in range(GROUPS):
                        last = nc.tensor.matmul(PS[:, 7, g * 256:(g + 1) * 256], BC[:, 0, g, :],
                                                XW[:, g * 256:(g + 1) * 256], start=True, stop=True)
                    last.then_inc(sf_full, 1)
                    if not end:
                        pe.wait_ge(xbs_full[1 - par], 16 * (l * NT + NT // 2 + i2 + par + 1))
                        pe.wait_ge(bst_ready, n + 1)
                        chunk_turn(i2, 1 - par)
                        sums(n + 1, 0)
                        sums(n + 1, 1)
                    pe.wait_ge(xs_ready, n + 1)
                    pe.wait_ge(chunk_done, 1 + n)
                    for g in range(GROUPS):
                        pe.wait_ge(w_masked, 2 + n * 2 + g + 1)
                        for h in range(4):
                            e = g * 4 + h
                            last = nc.tensor.matmul(PS[:, 4, e * HD:(e + 1) * HD], SEG[par][:, 2 * g, h, :],
                                                    XS[:, par, e * HD:(e + 1) * HD], start=True, stop=True)
                    last.then_inc(yd_full, 1)

                pe.wait_ge(xbs_full[0], 16 * (l * NT + NT // 2 + 1))
                chunk_turn(0, 0)
                sums(l * NT, 0)
                sums(l * NT, 1)
                settle(pe)
                with pe.Fori(0, NT // 2 - 1) as i2:
                    chunk(i2, 0, False)
                    chunk(i2, 1, False)
                chunk(NT // 2 - 1, 0, False)
                chunk(NT // 2 - 1, 1, True)
                pe.wait_ge(yz_ready, 2 + (l + 1) * NT)
                pe.wait_ge(qk_in, 32 * (l + 1))
                for f in range(4):
                    for t in range(NT):
                        last = nc.tensor.transpose(
                            PS[:, 2 * f + t // 4, (t % 4) * P:(t % 4 + 1) * P],
                            (KN, QN)[f // 2][:, t, f % 2 * P:(f % 2 + 1) * P], ident)
                    last.then_inc(qt_full, 1)
                pe.wait_ge(qt_ready, (l + 1) * 2 * AH_)
                pe.wait_ge(kx_in, 32 * (l + 1))
                pe.wait_ge(qx_in, 32 * (l + 1))
                pe.wait_ge(v_in, 16 * (l + 1))

                def scores(base, j):
                    if j % AH_ == 0:
                        pe.wait_ge(qs_ready, l * NT + base + j // AH_ + 1)
                    s_base, h, par = (l * NT + base) * AH_, j % AH_, j // AH_ % 2
                    if j >= 2:
                        pe.wait_ge(lg_ready, s_base + j - 1)
                    rows = own(h)
                    for th in range(2):
                        keys = slice(th * HALF, (th + 1) * HALF)
                        nc.tensor.matmul(bank(2 * (h % 2) + th), QS[:, par, h, :], KX[:, h, keys],
                                         start=True, stop=False)
                        last = nc.tensor.matmul(bank(2 * (h % 2) + th), QSL[rows, par, h // 2, :],
                                                KX[rows, h, keys], start=False, stop=True)
                    last.then_inc(s_full, 1)

                def turn(base, j):
                    s_base, h = (l * NT + base) * AH_, j % AH_
                    pe.wait_ge(pr_ready, s_base + j + 1)
                    pe.wait_ge(pta_ready, 1 + s_base + j)
                    pe.wait_ge(ptd_ready, 1 + s_base + j)
                    for t in range(NT):
                        last = nc.tensor.transpose(PS[:, 4 + t // 4, (t % 4) * P:(t % 4 + 1) * P],
                                                   PR[:, h % 2, t * P:(t + 1) * P], ident)
                    last.then_inc(pt_full, 1)

                def values(base, j):
                    s_base, h, par = (l * NT + base) * AH_, j % AH_, j // AH_ % 2
                    if h == 0:
                        pe.wait_ge(att_done, 1 + l * NT + base + par)
                    pe.wait_ge(pta_ready, 1 + s_base + j + 1)
                    pe.wait_ge(ptd_ready, 1 + s_base + j + 1)
                    for t in range(NT):
                        last = nc.tensor.matmul(PS[:, 6 + par, h * AD:(h + 1) * AD], PT[:, h % 2, t, :],
                                                V[:, t, h * AD:(h + 1) * AD],
                                                start=(t == 0), stop=(t == NT - 1))
                    last.then_inc(av_done, 1)

                def two_tiles(base, end):
                    for j in range(2 * AH_):
                        if not end or j + 2 < 2 * AH_:
                            scores(base, j + 2)
                        if not end or j + 1 < 2 * AH_:
                            turn(base, j + 1)
                        values(base, j)

                scores(0, 0)
                scores(0, 1)
                turn(0, 0)
                settle(pe)
                with pe.Fori(0, NT // 2 - 1) as i2:
                    two_tiles(i2 * 2, False)
                two_tiles(NT - 2, True)
                pe.wait_ge(att_done, 2 + (l + 1) * NT)
                settle(pe)
                with pe.Fori(0, NT // 2) as i2:
                    for par in range(2):
                        n = l * NT + i2 * 2 + par
                        pe.wait_ge(yn_ready, n + 1)
                        pe.wait_ge(yc_ready, n + 1)
                        pe.wait_ge(yl_ready, 1 + n)
                        for k in range(KT):
                            last = nc.tensor.transpose(PS[:, 2 * par + k // 4, (k % 4) * P:(k % 4 + 1) * P],
                                                       YN[:, par, k * P:(k + 1) * P], ident)
                        last.then_inc(yt_full, 1)
                pe.wait_ge(yl_ready, 2 + (l + 1) * NT)
                for u in range(OUT_U):
                    columns_unit(l, IN_U + u, (IN_U + u) % SLOTS, b0 + 4 * u, 4, b_full, b_free)
                norm_spread(2 * l + 1)
                s0 = (IN_U + OUT_U) % SLOTS

                def up(g, unit, s, part):
                    columns_unit(l, unit, s, a0 + A_UP + g * 8 + part * 4, 0, a_full, a_free)

                def down(g, unit, s):
                    unit_ready(l, unit)
                    pe.wait_ge(act_ready, 1 + (l * NG + g) * 2 + 2)
                    n0 = b0 + 4 * OUT_U + g * 16
                    for f in range(16):
                        dt, th = divmod(f, 2)
                        tok = slice(th * HALF, (th + 1) * HALF)
                        pe.wait_ge(b_free, BF + n0 + f + 1)
                        for k in range(2):
                            last = mm3(bank(4 + f % 4), wtile(s, k * 1024 + dt * P),
                                       (AHI[:, k, tok], ALO[:, k, tok]), k == 0, k == 1)
                        last.then_inc(b_full, 1)
                    pe.wait_ge(b_full, n0 + 16)
                    pe.sem_inc(w_used, 1)
                    pe.sem_inc(down_done, 1)

                f0 = IN_U + OUT_U
                first_unit(l, f0, s0, a0 + A_UP, 2 * l + 1)
                up(0, f0 + 1, (s0 + 1) % SLOTS, 1)
                settle(pe)
                with pe.Fori(1, NG) as g:
                    up(g, f0 + g * 3 - 1, (s0 + 2) % SLOTS, 0)
                    down(g - 1, f0 + g * 3, s0)
                    up(g, f0 + g * 3 + 1, (s0 + 1) % SLOTS, 1)
                down(NG - 1, f0 + NG * 3 - 1, (s0 + 2) % SLOTS)

        @block.scalar
        def _(act):
            A = nc.scalar.activation

            def norm(n, x_value):
                for k in range(KT):
                    act.wait_ge(b_free, x_value + 2 * k + 2)
                    if k >= 2:
                        act.wait_ge(sq_used, n * KT + k - 1)
                    A(SQ[:, k % 2, :], X[:, k, :], ACT.Square).then_inc(sq_ready, 1)
                for th in range(2):
                    act.wait_ge(inv_ready, 2 * n + th + 1)
                    tok = slice(th * HALF, (th + 1) * HALF)
                    A(INV[:, tok], INV[:, tok], ACT.Sqrt).then_inc(rs_ready, 1)
                for k in range(KT):
                    act.wait_ge(hf_ready, n * KT + k + 1)
                    A(HH[:, k, :], HF[:, k % 2, :], ACT.Copy).then_inc(hh_ready, 1)

            act.dma_start(OH[:], onehot[:, :]).then_inc(oh_in, 16)
            act.dma_start(TAB[:], table[:, :]).then_inc(oh_in, 16)
            act.dma_start(LNR[:], lnrow[:, :]).then_inc(oh_in, 16)
            act.sem_inc(a_free, 4)
            with act.Fori(0, DEPTH) as l:
                a0, b0 = l * A_FILLS, l * B_FILLS
                act.wait_ge(act_ready, 1 + l * NG * 2)
                act.dma_start(PARM[:], params[l]).then_inc(par_in, 16)
                norm(2 * l, 4 + b0)
                act.dma_start(xspill[:, :, :], X[:]).then_inc(x_spilled, 16)

                def silu_out(ti):
                    act.wait_ge(conv_done, l * XBC_T + ti + 1)
                    if ti >= 2:
                        act.wait_ge(xbc_out[ti % 2], 16 * (l * (XBC_T // 2) + ti // 2))
                    A(SC[:, ti % 2, :], CV[:, ti % 2, :], ACT.Silu).then_inc(silu_done, 1)
                    act.wait_ge(silu_done, l * XBC_T + ti + 1)
                    act.dma_start(xbc_d[:, :, ti, :].rearrange("c p n -> p c n"),
                                  SC[:, ti % 2, :].rearrange("p (c n) -> p c n", c=NT)).then_inc(xbc_out[ti % 2], 16)

                act.wait_ge(par_in, 16 * (l + 1))
                act.wait_ge(row_out, 16)
                for ti in range(XBC_T):
                    if ti >= 2:
                        act.wait_ge(conv_done, l * XBC_T + ti - 1)
                    for th in range(2):
                        act.wait_ge(a_full, a0 + 2 * ti + th + 1)
                        A(PAD[:, ti % 2, 2 + th * HALF:2 + (th + 1) * HALF], bank((2 * ti + th) % 4),
                          ACT.Copy).then_inc(a_free, 1)
                    act.wait_ge(a_free, 4 + a0 + 2 * ti + 2)
                    A(CV[:, ti % 2, :], PAD[:, ti % 2, 2:2 + SEQ], ACT.Identity,
                      scale=par_("conv_w", ti * CONV + 2, ti * CONV + 3),
                      bias=par_("conv_b", ti, ti + 1)).then_inc(tap_done, 1)
                    if ti >= 1:
                        silu_out(ti - 1)
                silu_out(XBC_T - 1)
                act.wait_ge(dtf_full, l + 1)
                A(DTF[:], PS[0:32, 4:6, :].rearrange("p a b -> p (a b)"), ACT.Copy).then_inc(dtf_ready, 1)
                step = Steps(act, sp_step, 3)
                step.begin(l)

                def tok_store(i):
                    act.dma_start(tok_d[i], ST[:, i % 2]).then_inc(tok_out[i % 2], 16)

                for i, func in enumerate((ACT.Silu, ACT.Silu, ACT.Gelu_apprx_tanh, ACT.Gelu_apprx_tanh,
                                          ACT.Copy, ACT.Copy, ACT.Copy)):
                    if i >= 2:
                        act.wait_ge(tok_out[i % 2], 16 * (l * (4 - i % 2) + i // 2))
                    if i == 1:
                        act.wait_ge(dt_full, l + 1)
                    for t in range(NT):
                        n = a0 + 2 * XBC_T + i * NT + t
                        act.wait_ge(a_full, n + 1)
                        A(ST[:, i % 2, t, :], PS[:, t % 4, 0:UC], func).then_inc(a_free, 1)
                        if i >= 5 and t == 3:
                            act.wait_ge(qinv_ready, l * 2 + i - 4)
                            A(QSS[:, i - 5], QSS[:, i - 5], ACT.Sqrt).then_inc(qr_ready, 1)
                    act.wait_ge(a_free, 4 + a0 + 2 * XBC_T + i * NT + NT)
                    if i == 3:
                        for t in range(NT):
                            last = A(JUNK8[:, t, :], ST[:, 1, t, :], ACT.Square,
                                     accum_out=VSS[:, t:t + 1])
                        last.then_inc(gv_done, 1)
                    if i == 4:
                        act.wait_ge(gv_done, l + 1)
                        act.wait_ge(vinv_ready, l + 1)
                        A(VR[:], VSS[:], ACT.Sqrt).then_inc(vr_ready, 1)
                    if i in (4, 5):
                        if i == 5:
                            act.wait_ge(qinv_ready, l * 2 + 1)
                        A(JUNK8[:], ST[:, i % 2], ACT.Square).then_inc(qsq_ready, 1)
                    if i not in (4, 5):
                        tok_store(i)
                    if i >= 5:
                        act.wait_ge(qn_ready, l * 2 + i - 4)
                        tok_store(i - 1)
                    if i == 0:
                        act.wait_ge(u_ready, l + 1)
                        A(EA[:], par_("a_log"), ACT.Exp)
                        step.then(A(SPL[:], U[:], ACT.Abs))
                        step.then(A(SPL[:], SPL[:], ACT.Exp, scale=-1.0))
                        A(SPL[:], SPL[:], ACT.Ln, bias=1.0).then_inc(sp_ready, 1)
                    if i == 3:
                        act.wait_ge(acs_ready, l + 1)
                        A(LDT[:], U[:], ACT.Ln)
                        A(EACS[:], ACS[:], ACT.Exp)
                        A(CDEC[:], CDEC[:], ACT.Exp)
                        step.then(A(DEC[:], DEC[:], ACT.Exp))
                        act.sem_inc(dec_ready, 1)
                step.end()
                settle(act)
                with act.Fori(0, NT // 2) as i2:
                    for par in range(2):
                        n = l * NT + i2 * 2 + par
                        act.wait_ge(ra_t_full, n + 1)
                        A(BSTA[:, par, :], PS[:, 1 + 3 * par, 0:GROUPS * STATE], ACT.Copy).then_inc(ra_bst, 1)
                act.wait_ge(tok_out[0], (l + 1) * 16 * 4)
                act.wait_ge(tok_out[1], (l + 1) * 16 * 3)
                settle(act)
                act.wait_ge(ldt_ready, l + 1)
                settle(act)
                with act.Fori(0, NT // 2) as i2:
                    for par in range(2):
                        c = i2 * 2 + par
                        n = l * NT + c
                        act.wait_ge(ab_full, 1 + n * 4)
                        settle(act)
                        A(AST[:], DTA[:, bass.ds(c, 1), :], ACT.Copy).then_inc(ast_ready, 1)
                        act.wait_ge(t_full, n + 1)
                        act.wait_ge(yz_ready, n + 1)
                        A(XS[:, par], bank(0), ACT.Copy).then_inc(xs_ready, 1)
                        act.wait_ge(w_masked, 2 + n * 2)
                        A(BC[:].rearrange("p a g n -> p (a g n)"), bank(1), ACT.Copy).then_inc(bst_ready, 1)
                        for j in range(4):
                            g, d = divmod(j, 2)
                            act.wait_ge(ab_full, 1 + n * 4 + j + 1)
                            if j == 0:
                                act.wait_ge(yd_full, n + 1)
                            settle(act)
                            for h in range(4):
                                e = d * 8 + g * 4 + h
                                last = A(SEG[par][:, j, h, :], PS[:, 2 + j % 2, h * P:(h + 1) * P], ACT.Exp,
                                         bias=NACS[:, bass.ds(c, 1), e:e + 1].rearrange("p a b -> p (a b)"))
                            last.then_inc(exp_ready, 1)
                for f in range(2 * AH_):
                    h = f % AH_
                    act.wait_ge(qt_full, l * 4 + f // 2 + 1)
                    A((KX, QH)[f // AH_][own(h), h, :], bank(2 * (f // 2), 2)[own(h)], ACT.Copy,
                      scale=QGN[own(h)] if f >= AH_ else par_("k_gain")[own(h)]).then_inc(qh_ready, 1)
                    if f == AH_ + 1:
                        act.wait_ge(qt_ready, l * 2 * AH_ + AH_)
                        act.dma_start(KX[AD:P, 0:AH_:2, :].bitcast(F32), KL[0:AD].bitcast(F32)).then_inc(kx_in, 16)
                        act.dma_start(KX[0:AD, 1:AH_:2, :].bitcast(F32), KL[AD:P].bitcast(F32)).then_inc(kx_in, 16)
                act.wait_ge(qh_ready, (l + 1) * 2 * AH_)
                act.dma_start(QH[AD:P, 0:AH_:2, :].bitcast(F32), QH[0:AD, 0:AH_:2, :].bitcast(F32)).then_inc(qx_in, 16)
                act.dma_start(QH[0:AD, 1:AH_:2, :].bitcast(F32), QH[AD:P, 1:AH_:2, :].bitcast(F32)).then_inc(qx_in, 16)

                def exps(base, j):
                    s_base, h, par = (l * NT + base) * AH_, j % AH_, j // AH_ % 2
                    act.wait_ge(lg_ready, s_base + j + 1)
                    if j >= 2:
                        act.wait_ge(pt_full, s_base + j - 1)
                    A(PR[:, h % 2, :], LG[:, h % 2, :], ACT.Exp, scale=-1.0, bias=MN[:, h:h + 1],
                      accum_out=RSUM[:, par, h:h + 1]).then_inc(pr_ready, 1)

                def evac(base, j):
                    s_base, h = (l * NT + base) * AH_, j % AH_
                    act.wait_ge(pt_full, s_base + j + 1)
                    if j:
                        act.wait_ge(av_done, 1 + s_base + j - 1)
                    A(PT[:, h % 2, 0:4, :], bank(4), ACT.Copy).then_inc(pta_ready, 1)

                def two_tiles(base, end):
                    for j in range(2 * AH_):
                        if not end or j + 1 < 2 * AH_:
                            evac(base, j + 1)
                        if not end or j + 2 < 2 * AH_:
                            exps(base, j + 2)

                exps(0, 0)
                exps(0, 1)
                evac(0, 0)
                act.wait_ge(yz_ready, 2 + (l + 1) * NT)
                for c in range(NT):
                    if c:
                        act.wait_ge(yss_ready, 1 + l * NT + c)
                    for g in range(GROUPS):
                        last = A(JUNK[:, g], YT[:, c, g * 256:(g + 1) * 256], ACT.Square,
                                 accum_out=YSS[:, c, g:g + 1])
                    last.then_inc(yss_ready, 1)
                settle(act)
                with act.Fori(0, NT // 2 - 1) as i2:
                    two_tiles(i2 * 2, False)
                two_tiles(NT - 2, True)
                act.wait_ge(yinv_ready, l + 1)
                A(YR[:], YSS[:], ACT.Sqrt).then_inc(yr_ready, 1)
                act.wait_ge(att_done, 2 + (l + 1) * NT)

                def stage(i2, par):
                    c = i2 * 2 + par
                    act.wait_ge(yt_full, 1 + l * NT + c)
                    A(YN[:, par % 2, INNER:DM], YT[:, bass.ds(c, 1), INNER:DM], ACT.Copy).then_inc(yc_ready, 1)

                def high_part(i2, par):
                    c = i2 * 2 + par
                    act.wait_ge(yt_full, 2 + l * NT + c + 1)
                    A(HH[:, :, bass.ds(c * P, P)], bank(2 * par, 2).rearrange("p (k n) -> p k n", k=KT), ACT.Copy
                      ).then_inc(yh_ready, 1)

                stage(0, 0)
                settle(act)
                with act.Fori(0, NT // 2 - 1) as i2:
                    for par in range(2):
                        stage(i2, par + 1)
                        high_part(i2, par)
                stage(NT // 2 - 1, 1)
                high_part(NT // 2 - 1, 0)
                high_part(NT // 2 - 1, 1)
                norm(2 * l + 1, 4 + b0 + BF)
                settle(act)
                with act.Fori(0, NG) as g:
                    n = l * NG + g
                    af = a0 + A_UP + g * 8

                    def take(x):
                        part, ct = divmod(x, 2)
                        act.wait_ge(f_conv, 1 + n * 4 + max(x - 1, 0))
                        for th in range(2):
                            f = 2 * x + th
                            act.wait_ge(a_full, af + f + 1)
                            A(FPAD[:, x % 2, 1 + th * HALF:1 + (th + 1) * HALF], bank(f % 4), ACT.Copy
                              ).then_inc(a_free, 1)
                        act.wait_ge(a_free, 4 + af + 2 * x + 2)
                        if part:
                            act.wait_ge(act_ready, 1 + n * 2)
                        at = PAR["ffn_conv"][0] + (part * FT + ct) * 4
                        A((CVG, CVV)[part][:, ct, :], FPAD[:, x % 2, 1:1 + SEQ], ACT.Identity,
                          scale=PARM[:, bass.ds(g * 8 + at + 1, 1)], bias=PARM[:, bass.ds(g * 8 + at + 3, 1)]
                          ).then_inc(f_tap, 1)

                    def silu(ct):
                        act.wait_ge(f_conv, 1 + n * 4 + ct + 1)
                        A(CVG[:, ct, :], CVG[:, ct, :], ACT.Silu).then_inc(f_silu, 1)

                    def high(ct):
                        act.wait_ge(f_conv, 1 + n * 4 + 3 + ct)
                        if ct == 0:
                            act.wait_ge(down_done, 1 + n)
                        A(AHI[:, ct, :], CVV[:, ct, :], ACT.Copy).then_inc(f_hi, 1)

                    take(0)
                    take(1)
                    silu(0)
                    take(2)
                    silu(1)
                    take(3)
                    high(0)
                    high(1)

        @block.vector
        def _(dve):
            TT, STT, TS = nc.vector.tensor_tensor, nc.vector.scalar_tensor_tensor, nc.vector.tensor_scalar

            def norm(n, gain):
                step = Steps(dve, norm_step, 2)
                step.begin(n)
                for th in range(2):
                    dve.wait_ge(nb_ready, 2 * n + th + 1)
                    tok = slice(th * HALF, (th + 1) * HALF)
                    step.then(TS(INV[:, tok], bank(6 + th), 1.0 / DM, EPS, ALU.mult, ALU.add))
                    nc.vector.reciprocal(INV[:, tok], INV[:, tok]).then_inc(inv_ready, 1)
                step.end()
                dve.wait_ge(rs_ready, 2 * n + 2)
                for k in range(KT + 1):
                    if k < KT:
                        if k >= 2:
                            dve.wait_ge(h_ready, n * KT + k - 1)
                        STT(HF[:, k % 2, :], X[:, k, :], gain[:, k:k + 1], INV[:], ALU.mult, ALU.mult
                            ).then_inc(hf_ready, 1)
                    if k >= 1:
                        dve.wait_ge(hh_ready, n * KT + k)
                        TT(HL[:, k - 1, :], HF[:, (k - 1) % 2, :], HH[:, k - 1, :].bitcast(F32), ALU.subtract
                           ).then_inc(h_ready, 1)
                dve.wait_ge(h_ready, (n + 1) * KT)

            def square_sum(n, k):
                dve.wait_ge(sq_ready, n * KT + k + 1)
                if k == 1:
                    TT(ACC[:], SQ[:, 0, :], SQ[:, 1, :], ALU.add).then_inc(sq_used, 2)
                else:
                    dve.wait_ge(sq_used, n * KT + k)
                    TT(ACC[:], ACC[:], SQ[:, k % 2, :], ALU.add).then_inc(sq_used, 1)

            dve.sem_inc(b_free, 4)
            dve.sem_inc(xbs_used, 2)
            dve.sem_inc(zg_used, 2)
            dve.sem_inc(toe_used, 2)
            for i in range(4):
                dve.wait_ge(x_in[i], 16)
                dve.sem_inc(b_free, BF // 4)
            dve.wait_ge(row_ps, 1)
            dve.wait_ge(oh_in, 48)
            STT(ROW[:], PS[0:AH_, 0:4, :].rearrange("p a b -> p (a b)"), -1.0, LNR[:], ALU.mult, ALU.add
                ).then_inc(row_sb, 1)
            with dve.Fori(0, DEPTH) as l:
                a0, b0 = l * A_FILLS, l * B_FILLS
                for k in range(1, KT):
                    square_sum(2 * l, k)
                dve.wait_ge(par_in, 16 * (l + 1))
                norm(2 * l, par_("mix_gain"))
                w_dt = par_("w_dt").rearrange("p (k e) -> p k e", k=KT)
                nc.vector.tensor_copy(WD[:, :, 0:16], w_dt).then_inc(pad_zero, 1)
                dve.wait_ge(pad_zero, 5 * l + 1)
                TT(WD[:, :, 16:32], w_dt, WD[:, :, 0:16].bitcast(F32), ALU.subtract).then_inc(wdt_ready, 1)
                TS(QGN[:], par_("q_gain"), -(AD ** -0.5), None, ALU.mult)
                dve.wait_ge(row_out, 16)
                for x in range(2):
                    nc.vector.memset(PAD[:, x, 0:2], 0.0)
                    last = nc.vector.memset(PAD[:, x, SEQ + 2:SEQ + 4], 0.0)
                last.then_inc(pad_zero, 1)
                dve.wait_ge(pad_zero, 5 * l + 2)
                step = Steps(dve, conv_step, 3 * XBC_T)
                step.begin(l)
                for ti in range(XBC_T):
                    dve.wait_ge(tap_done, l * XBC_T + ti + 1)
                    for n, j in enumerate((0, 1, 3, 4)):
                        ins = STT(CV[:, ti % 2, :], PAD[:, ti % 2, j:j + SEQ],
                                  par_("conv_w", ti * CONV + j, ti * CONV + j + 1), CV[:, ti % 2, :],
                                  ALU.mult, ALU.add)
                        if n < 3:
                            step.then(ins)
                    ins.then_inc(conv_done, 1)
                step.end()
                dve.wait_ge(dt_full, l + 1)
                step = Steps(dve, dt_step, 4)
                step.begin(l)
                raw = PS[:, 6, 0:NT * 32].rearrange("p (t e) -> p t e", t=NT)
                step.then(TT(U[:], raw[:, :, 0:16], par_("dt_bias").unsqueeze(1).to_broadcast((P, NT, 16)), ALU.add))
                TT(U[:], U[:], raw[:, :, 16:32], ALU.add).then_inc(u_ready, 1)
                dve.wait_ge(sp_ready, l + 1)
                step.then(STT(DT[:], U[:], 0.0, SPL[:], ALU.max, ALU.add))
                STT(DTA[:], DT[:], -1.0, EA[:].unsqueeze(1).to_broadcast((P, NT, 16)), ALU.mult, ALU.mult
                    ).then_inc(dta_ready, 1)
                dve.wait_ge(acs_full, l + 1)
                for d in range(2):
                    ins = nc.vector.tensor_copy(ACS[:, :, d * 8:(d + 1) * 8],
                                                PS[:, 5, d * 64:(d + 1) * 64].rearrange("p (t e) -> p t e", t=NT))
                step.then(ins)
                tot = PS[:, 5, 128:256].rearrange("p (t e) -> p t e", t=NT)
                nc.vector.tensor_copy(CDEC[:], tot)
                nc.vector.tensor_scalar_max(U[:], DT[:], 1.2e-38)
                TT(DEC[:], tot, ACS[:], ALU.subtract).then_inc(acs_ready, 1)
                dve.wait_ge(dec_ready, l + 1)
                step.then(TT(WST[:], DT[:], DEC[:], ALU.mult))
                step.end()
                TT(NACS[:], LDT[:], ACS[:], ALU.subtract).then_inc(ldt_ready, 1)
                step = Steps(dve, v_step, 1)
                step.begin(l)
                dve.wait_ge(gv_done, l + 1)
                step.then(TS(VSS[:], VSS[:], 1.0 / GW, EPS, ALU.mult, ALU.add))
                step.end()
                nc.vector.reciprocal(VSS[:], VSS[:]).then_inc(vinv_ready, 1)
                step = Steps(dve, q_step, 4)
                step.begin(l)
                for m in range(2):
                    dve.wait_ge(qsq_ready, l * 2 + m + 1)
                    step.then(nc.vector.reduce_sum(QSS[:, m], JUNK8[:].rearrange("p t (h e) -> p (t h) e", e=AD), AX.X))
                    step.then(TS(QSS[:, m], QSS[:, m], 1.0 / AD, EPS, ALU.mult, ALU.add))
                    nc.vector.reciprocal(QSS[:, m], QSS[:, m]).then_inc(qinv_ready, 1)
                    dve.wait_ge(qr_ready, l * 2 + m + 1)
                    q = ST[:, m].rearrange("p t (h e) -> p (t h) e", e=AD)
                    TT(q, q, QSS[:, m].unsqueeze(2).to_broadcast((P, NT * AH_, AD)), ALU.mult).then_inc(qn_ready, 1)
                step.end()
                dve.wait_ge(a_free, 4 + a0 + A_UP)
                nc.vector.memset(BW[:, NT, :], 0.0).then_inc(pad_zero, 1)
                nc.vector.memset(CURF[:], 0.0).then_inc(pad_zero, 1)
                dve.wait_ge(pad_zero, 5 * l + 4)
                dve.wait_ge(tok_out[0], (l + 1) * 16 * 4)
                dve.wait_ge(tok_out[1], (l + 1) * 16 * 3)
                nc.vector.tensor_copy(IDR[:], ident)
                for d, tri in enumerate((tri_f, tri_b)):
                    last = TS(FAR[:, d, :], tri, 1.0, 1e30, ALU.subtract, ALU.mult)
                last.then_inc(far_ready, 1)
                step = Steps(dve, ra_step, 1)
                settle(dve)
                with dve.Fori(0, NT // 2) as i2:
                    for par in range(2):
                        n = l * NT + i2 * 2 + par
                        c = i2 * -2 + (NT - 1 - par)
                        step.begin(n)

                        def by_decay(t):
                            return t[:, bass.ds(c, 1), 8:16].rearrange("p a h -> p (a h)").unsqueeze(
                                2).to_broadcast((P, HEADS, HD))

                        dve.wait_ge(ra_t_full, n + 1)
                        TT(XWA[:, par].rearrange("p (h e) -> p h e", h=HEADS),
                           bank(3 * par).rearrange("p (h e) -> p h e", h=HEADS), by_decay(WST), ALU.mult
                           ).then_inc(ra_xw, 1)
                        new = BW[:, bass.ds(c, 1), :].rearrange("p a n -> p (a n)")
                        old = BW[:, bass.ds(c + 1, 1), :].rearrange("p a n -> p (a n)")
                        dve.wait_ge(ra_done, 1 + n)
                        step.then(TT(new.rearrange("p (h e) -> p h e", h=HEADS),
                                     old.rearrange("p (h e) -> p h e", h=HEADS), by_decay(CDEC), ALU.mult))
                        step.end()
                        dve.wait_ge(ra_s_full, n + 1)
                        TT(new, new, bank(2 + 3 * par), ALU.add).then_inc(ra_done, 1)
                dve.wait_ge(vr_ready, l + 1)
                dve.wait_ge(x_spilled, 16 * (l + 1))
                step = Steps(dve, chunk_step, 6)
                settle(dve)
                with dve.Fori(0, NT // 2) as i2:
                    for par in range(2):
                        c = i2 * 2 + par
                        n = l * NT + c
                        step.begin(n)

                        def heads(t, lo):
                            return t[:, bass.ds(c, 1), lo:lo + 8].rearrange("p a h -> p (a h)").unsqueeze(
                                2).to_broadcast((P, HEADS, HD))

                        def by_head(t):
                            return t.rearrange("p (h e) -> p h e", h=HEADS)

                        dve.wait_ge(zg_full[par], 16 * (l * (NT // 2) + i2 + 1))
                        STT(VN[:], ZG[:, par, 3, :], VR[:, bass.ds(c, 1)], par_("v_gain"), ALU.mult, ALU.mult
                            ).then_inc(vn_ready, 1)
                        dve.wait_ge(xs_ready, n + 1)
                        TT(by_head(XW[:]), by_head(XS[:, par]), heads(WST, 0), ALU.mult).then_inc(xw_ready, 1)
                        dve.wait_ge(yo_full, n + 1)
                        step.then(TT(by_head(CURF[:]), by_head(CURF[:]), heads(CDEC, 0), ALU.mult))
                        TT(by_head(Y2[:]), by_head(bank(6)), heads(EACS, 8), ALU.mult)
                        TT(by_head(Y1[:]), by_head(bank(5)), heads(EACS, 0), ALU.mult).then_inc(y12_done, 1)
                        dve.wait_ge(mx_full, n + 1)
                        TT(GT[:].rearrange("p (g e) -> p g e", g=GG),
                           PS[:, 7, 0:GW].rearrange("p (g e) -> p g e", g=GG), per_head(par_("b_s")), ALU.add
                           ).then_inc(gt_done, 1)
                        dve.wait_ge(gt_done, n + 1)
                        TT(YT[:, bass.ds(c, 1), INNER:INNER + GW].rearrange("p a n -> p (a n)"), GT[:],
                           ZG[:, par, 2, :], ALU.mult)
                        dve.wait_ge(bst_ready, n + 1)
                        for g in range(GROUPS):
                            dve.wait_ge(exp_ready, 2 + n * 4 + 2 * g + 2)
                            step.then(TT(SEG[par][:, 2 * g], SEG[par][:, 2 * g], SEG[par][:, 2 * g + 1], ALU.add))
                            TT(SEG[par][:, 2 * g], SEG[par][:, 2 * g], BC[:, 1, g, :].unsqueeze(1).to_broadcast((P, 4, P)),
                               ALU.mult).then_inc(w_masked, 1)
                        dve.wait_ge(sf_full, n + 1)
                        TT(CURF[:], CURF[:], bank(7), ALU.add).then_inc(curf_ready, 1)
                        dve.wait_ge(y12_done, 1 + n + 1)
                        step.then(TT(Y1[:], Y1[:], Y2[:], ALU.add))
                        step.then(TT(by_head(Y2[:]), by_head(XS[:, par]), per_head(par_("d_skip")), ALU.mult))
                        step.then(TT(Y1[:], Y1[:], Y2[:], ALU.add))
                        dve.wait_ge(yd_full, 2 + n + 1)
                        TT(Y1[:], Y1[:], bank(4), ALU.add).then_inc(chunk_done, 1)
                        dve.wait_ge(chunk_done, 1 + n + 1)
                        TT(YT[:, bass.ds(c, 1), 0:INNER].rearrange("p a n -> p (a n)"), Y1[:],
                           ZG[:, par, 0:2, :].rearrange("p a b -> p (a b)"), ALU.mult).then_inc(yz_ready, 1)
                        dve.wait_ge(yz_ready, 2 + n + 1)
                        dve.sem_inc(zg_used, 1)
                        step.end()
                for f in range(2 * AH_):
                    h = f % AH_
                    dve.wait_ge(qh_ready, l * 2 * AH_ + f + 1)
                    lo, hi, gain = ((KL, KX, par_("k_gain")), (QL, QH, QGN))[f // AH_]
                    STT(lo[own(h), h // 2, :], bank(2 * (f // 2), 2)[own(h)], gain[own(h)],
                        hi[own(h), h, :].bitcast(F32), ALU.mult, ALU.subtract).then_inc(qt_ready, 1)
                dve.wait_ge(qt_ready, (l + 1) * 2 * AH_)
                dve.wait_ge(qx_in, 32 * (l + 1))
                dve.wait_ge(kx_in, 32 * (l + 1))
                step = Steps(dve, att_step, 1)

                def queries(base, par):
                    cols = bass.ds(base * P + par * P, P)
                    nc.vector.tensor_copy(QS[:, par % 2], QH[:, :, cols])
                    nc.vector.tensor_copy(QSL[:, par % 2], QL[:, :, cols]).then_inc(qs_ready, 1)

                def logits(base, j):
                    n, h = l * NT + base, j % AH_
                    dve.wait_ge(s_full, n * AH_ + j + 1)
                    if h % 2 == 0:
                        dve.wait_ge(toe_full[h // 2], 16 * (n + j // AH_ + 1))
                    if j >= 2:
                        dve.wait_ge(pr_ready, n * AH_ + j - 1)
                    settle(dve)
                    nc.vector.tensor_tensor_reduce(
                        out=LG[:, h % 2, :], in0=bank(2 * (h % 2), 2),
                        in1=TOE[:, h // 2, h % 2, :],
                        scale=1.0, scalar=3e38, op0=ALU.add, op1=ALU.min,
                        accum_out=MN[:, h:h + 1]).then_inc(lg_ready, 1)
                    if h % 2:
                        dve.wait_ge(lg_ready, n * AH_ + j + 1)
                        dve.sem_inc(toe_used, 1)

                def evac(base, j):
                    n, h = l * NT + base, j % AH_
                    dve.wait_ge(pt_full, n * AH_ + j + 1)
                    if j:
                        dve.wait_ge(av_done, 1 + n * AH_ + j - 1)
                    nc.vector.tensor_copy(PT[:, h % 2, 4:8, :].rearrange("p a b -> p (a b)"), bank(5)
                                          ).then_inc(ptd_ready, 1)

                def take(base, par):
                    n = l * NT + base + par
                    step.begin(n)
                    dve.wait_ge(av_done, 1 + n * AH_ + AH_)
                    dve.wait_ge(att_done, 2 + n)
                    step.then(nc.vector.reciprocal(RC[:], RSUM[:, par]))
                    step.end()
                    TT(YT[:, bass.ds(base + par, 1), INNER + GW:DM].rearrange("p a (h e) -> p (a h) e", h=AH_),
                       PS[:, 6 + par, 0:AW].rearrange("p (h e) -> p h e", h=AH_), per_head(RC[:]), ALU.mult
                       ).then_inc(att_done, 1)

                def two_tiles(base, end):
                    for j in range(2 * AH_):
                        if j % AH_ == 0 and not (end and j):
                            queries(base, j // AH_ + 1)
                        if not end or j + 2 < 2 * AH_:
                            logits(base, j + 2)
                        if not end or j + 1 < 2 * AH_:
                            evac(base, j + 1)
                        if j == AH_:
                            take(base, 0)
                    take(base, 1)

                queries(0, 0)
                logits(0, 0)
                logits(0, 1)
                evac(0, 0)
                dve.wait_ge(yss_ready, 1 + (l + 1) * NT)
                yss = Steps(dve, yr_step, 1)
                yss.begin(l)
                yss.then(TS(YSS[:], YSS[:], 1.0 / 256, EPS, ALU.mult, ALU.add))
                yss.end()
                nc.vector.reciprocal(YSS[:], YSS[:]).then_inc(yinv_ready, 1)
                settle(dve)
                with dve.Fori(0, NT // 2 - 1) as i2:
                    two_tiles(i2 * 2, False)
                two_tiles(NT - 2, True)
                dve.wait_ge(yr_ready, l + 1)

                def normalise(i2, par):
                    c = i2 * 2 + par
                    dve.wait_ge(yt_full, 1 + l * NT + c)
                    for g in range(GROUPS):
                        cols = slice(g * 256, (g + 1) * 256)
                        ins = STT(YN[:, par % 2, cols], YT[:, bass.ds(c, 1), cols].rearrange("p a n -> p (a n)"),
                                  YR[:, bass.ds(c, 1), g:g + 1].rearrange("p a n -> p (a n)"),
                                  par_("out_gain", g * 256, (g + 1) * 256), ALU.mult, ALU.mult)
                    ins.then_inc(yn_ready, 1)

                def low_part(i2, par):
                    c = i2 * 2 + par
                    dve.wait_ge(yh_ready, 1 + l * NT + c + 1)
                    cols = bass.ds(c * P, P)
                    TT(HL[:, :, cols], bank(2 * par, 2).rearrange("p (k n) -> p k n", k=KT),
                       HH[:, :, cols].bitcast(F32), ALU.subtract).then_inc(yl_ready, 1)

                normalise(0, 0)
                settle(dve)
                with dve.Fori(0, NT // 2 - 1) as i2:
                    for par in range(2):
                        normalise(i2, par + 1)
                        low_part(i2, par)
                normalise(NT // 2 - 1, 1)
                low_part(NT // 2 - 1, 0)
                low_part(NT // 2 - 1, 1)

                def add(f, n0, nb):
                    dt, th = divmod(f, 2)
                    dve.wait_ge(b_full, n0 + f + 1)
                    x = X[:, dt, th * HALF:(th + 1) * HALF]
                    TT(x, bank(4 + f % 4), x, ALU.add).then_inc(b_free, 1)

                dve.wait_ge(x_back, 16 * (l + 1))
                for k in range(KT):
                    add(2 * k, b0, 4)
                    add(2 * k + 1, b0, 4)
                    if k >= 2:
                        square_sum(2 * l + 1, k - 1)
                square_sum(2 * l + 1, KT - 1)
                dve.wait_ge(b_free, BF + 4 + b0 + 16)
                norm(2 * l + 1, par_("ffn_gain"))
                for x in range(2):
                    nc.vector.memset(FPAD[:, x, 0:1], 0.0)
                    last = nc.vector.memset(FPAD[:, x, SEQ + 1:SEQ + 2], 0.0)
                last.then_inc(pad_zero, 1)
                dve.wait_ge(pad_zero, 5 * l + 5)
                step = Steps(dve, f_step, 6)

                def conv(g, x):
                    part, ct = divmod(x, 2)
                    n = l * NG + g
                    t = (CVG, CVV)[part][:, ct, :]
                    at = PAR["ffn_conv"][0] + (part * FT + ct) * 4
                    dve.wait_ge(f_tap, n * 4 + x + 1)
                    step.then(STT(t, FPAD[:, x % 2, 0:SEQ], PARM[:, bass.ds(g * 8 + at, 1)], t, ALU.mult, ALU.add))
                    ins = STT(t, FPAD[:, x % 2, 2:2 + SEQ], PARM[:, bass.ds(g * 8 + at + 2, 1)], t,
                              ALU.mult, ALU.add)
                    if part:
                        step.then(ins)
                        dve.wait_ge(f_silu, n * 2 + ct + 1)
                        ins = TT(t, t, CVG[:, ct, :], ALU.mult)
                    ins.then_inc(f_conv, 1)

                def low(g, ct):
                    n = l * NG + g
                    dve.wait_ge(f_hi, n * 2 + ct + 1)
                    TT(ALO[:, ct, :], CVV[:, ct, :], AHI[:, ct, :].bitcast(F32), ALU.subtract
                       ).then_inc(act_ready, 1)

                def group(g, adds):
                    step.begin(l * NG + g)
                    n0 = b0 + 4 * OUT_U + (g - 1) * 16
                    conv(g, 0)
                    for f in range(4 if adds else 0):
                        add(f, n0, 0)
                    conv(g, 1)
                    for f in range(4, 16 if adds else 4):
                        add(f, n0, 0)
                    conv(g, 2)
                    conv(g, 3)
                    low(g, 0)
                    low(g, 1)
                    step.end()

                group(0, False)
                settle(dve)
                with dve.Fori(1, NG) as g:
                    group(g, True)
                for f in range(16):
                    add(f, b0 + 4 * OUT_U + (NG - 1) * 16, 0)


def rel_constants():
    d = np.arange(2 * SEQ) - SEQ
    nb, exact = NBUCK // 2, NBUCK // 4
    n = np.abs(d)
    large = exact + (np.log(np.maximum(n, 1).astype(np.float32) / np.float32(exact))
                     / np.float32(np.log(1024 / exact)) * np.float32(nb - exact)).astype(np.int32)
    bucket = np.where(d > 0, nb, 0) + np.where(n < exact, n, np.minimum(large, nb - 1))
    onehot = (np.arange(NBUCK)[:, None] == bucket[None, :]).astype(np.float32)
    count = sum(((d % dil == 0) & (n <= win // 2)).astype(np.int32)
                for win, dil in ((128, 1), (512, 4), (2048, 16)))
    ln = np.where(count > 0, -np.log(np.maximum(count, 1)), 1e30).astype(np.float32)
    return onehot, np.ascontiguousarray(np.broadcast_to(ln, (AH_, 2 * SEQ)))


def chip_constants():
    i = np.arange(P)
    return np.concatenate([np.eye(P), i[:, None] <= i[None, :], i[:, None] >= i[None, :], np.ones((P, P))],
                          axis=1).astype(np.float32)


def weight_stream(w_in, w_out, w_up, w_down):
    def cols(w, a):
        return w[:, a:a + UC].reshape(2, 4, P, UC).transpose(0, 2, 1, 3).reshape(2, P, 1024)

    def rows(w, a):
        return w[a:a + UC].reshape(2, P, DM)

    units = []
    for l in range(DEPTH):
        dt0 = XBC_T * P + INNER
        after = dt0 + 16
        units += [cols(w_in[l], a) for a in range(0, dt0, UC)]
        units += [cols(w_in[l], after + a) for a in range(0, 5 * UC, UC)]
        units += [cols(w_out[l], a) for a in range(0, DM, UC)]
        for g in range(NG):
            units += [cols(w_up[l], g * UC)]
            if g:
                units += [rows(w_down[l], (g - 1) * UC)]
            units += [cols(w_up[l], FFN + g * UC)]
        units += [rows(w_down[l], (NG - 1) * UC)]
    return np.stack(units)


def parameters(i):
    def feat(a):
        return a.reshape(-1, P).T

    def row(a):
        return np.broadcast_to(a.reshape(1, -1), (P, a.size))

    dt0 = XBC_T * P + INNER
    out = []
    for l in range(DEPTH):
        conv = i["ssd_conv_w"][l].reshape(CONV, XBC_T, P).transpose(2, 1, 0).reshape(P, -1)
        fcw = np.concatenate([i["ffn_conv_w"][l], i["ffn_conv_b"][l][None]], 0)
        parts = dict(
            mix_gain=feat(i["mix_norm_gain"][l]), ffn_gain=feat(i["ffn_norm_gain"][l]),
            conv_w=conv, conv_b=feat(i["ssd_conv_b"][l]), dt_bias=row(i["ssd_dt_bias"][l]),
            a_log=row(i["ssd_a_log"][l]), d_skip=row(i["ssd_d"][l]), out_gain=row(i["ssd_out_gain"][l]),
            v_gain=row(i["gmlp_v_gain"][l]), b_s=i["gmlp_b_s"][l].T,
            q_gain=np.concatenate([i["attn_q_gain"][l]] * 2)[:, None],
            k_gain=np.concatenate([i["attn_k_gain"][l]] * 2)[:, None],
            w_s=i["gmlp_w_s"][l].transpose(2, 0, 1).reshape(P, -1),
            w_dt=i["w_in"][l][:, dt0:dt0 + 16].reshape(KT, P, 16).transpose(1, 0, 2).reshape(P, -1),
            ffn_conv=fcw.reshape(4, 2 * FT, P).transpose(2, 1, 0).reshape(P, -1))
        out.append(np.concatenate([parts[n] for n, _ in _PARTS], axis=1))
    return np.stack(out)


def kernel(**inputs):
    from concourse import bacc
    from concourse.bass_utils import run_bass_kernel_spmd

    i = {k: np.asarray(v) for k, v in inputs.items()}
    onehot, lnrow = rel_constants()
    arrays = dict(
        xT=i["x"][0].T.reshape(KT, P, SEQ).transpose(1, 0, 2),
        wst=weight_stream(i["w_in"], i["w_out"], i["ffn_w_up"], i["ffn_w_down"]),
        par=parameters(i), consts=chip_constants(), onehot=onehot, lnrow=lnrow, table=i["rel_bias_table"])
    arrays = {k: np.ascontiguousarray(v) for k, v in arrays.items()}
    nc = bacc.Bacc("TRN2", target_bir_lowering=False, num_devices=1)
    aps = [nc.dram_tensor(k, v.shape, F32, kind="ExternalInput").ap() for k, v in arrays.items()]
    out = nc.dram_tensor("outT", (P, KT, SEQ), F32, kind="ExternalOutput").ap()
    trunk(nc, *aps, out)
    r = run_bass_kernel_spmd(nc, [arrays], core_ids=[0])
    y = np.asarray(r.results[0]["outT"])
    return np.ascontiguousarray(y.transpose(1, 0, 2).reshape(DM, SEQ).T)[None]
```
